# Optimizing a Trainium2 kernel written in Bass

```python
import jax, jax.numpy as jnp
from jax import lax
import numpy as np

D_MODEL = 1024
BATCH = 1
SEQ = 512
DEPTH = 1

MEM_LEN = 256
HG_HEADS = 4
HG_DK = 128
HG_DV = 128
HG_WIDTH = HG_HEADS * HG_DV
HG_CHUNK = 64
SG_GROUPS = 4
SG_DIM = 128
SG_WIDTH = SG_GROUPS * SG_DIM
SG_CHUNK = 128
MIX_WIDTH = HG_WIDTH + SG_WIDTH
IN_WIDTH = 4 * HG_WIDTH + 2 * SG_WIDTH
X_HEADS = 4
X_HEAD_DIM = D_MODEL // X_HEADS
D_FF = 2816
ALPHA = (2.0 * DEPTH) ** 0.25
BETA = (8.0 * DEPTH) ** -0.25
LN_EPS = 1e-5


def _layer_norm(x, g, b):
    xf = x.astype(jnp.float32)
    mu = jnp.mean(xf, axis=-1, keepdims=True)
    var = jnp.mean(jnp.square(xf - mu), axis=-1, keepdims=True)
    return ((xf - mu) * lax.rsqrt(var + LN_EPS) * g + b).astype(x.dtype)

def _rms_norm(x, g):
    xf = x.astype(jnp.float32)
    return xf * lax.rsqrt(jnp.mean(jnp.square(xf), axis=-1, keepdims=True) + LN_EPS) * g

def _swiglu(x, w_gate, w_up, w_down):
    return (jax.nn.silu(x @ w_gate) * (x @ w_up)) @ w_down

def _hgrn2(q, fz, iv, lb):
    B, T, H, DK = q.shape
    DV = iv.shape[-1]
    n_chunks = T // HG_CHUNK
    q = q.astype(jnp.float32)
    fz = fz.astype(jnp.float32)
    iv = iv.astype(jnp.float32)
    log_f = jnp.log(lb + (1.0 - lb) * jax.nn.sigmoid(fz))
    k = (1.0 - lb) * jax.nn.sigmoid(-fz)

    def chunks(a):
        return a.reshape(B, n_chunks, HG_CHUNK, H, a.shape[-1]).transpose(1, 0, 3, 2, 4)

    causal = jnp.tril(jnp.ones((HG_CHUNK, HG_CHUNK), dtype=bool))[:, :, None]

    def step(S, inp):
        qc, kc, vc, lfc = inp
        b = jnp.cumsum(lfc, axis=2)
        diff = b[:, :, :, None, :] - b[:, :, None, :, :]
        decay = jnp.where(causal, jnp.exp(jnp.where(causal, diff, 0.0)), 0.0)
        scores = jnp.einsum('bhtd,bhsd,bhtsd->bhts', qc, kc, decay)
        o = (jnp.einsum('bhts,bhsv->bhtv', scores, vc)
             + jnp.einsum('bhtd,bhdv->bhtv', qc * jnp.exp(b), S))
        b_end = b[:, :, -1:, :]
        S = (jnp.exp(b_end[:, :, 0, :])[..., None] * S
             + jnp.einsum('bhsd,bhsv->bhdv', kc * jnp.exp(b_end - b), vc))
        return S, o

    S0 = jnp.zeros((B, H, DK, DV), jnp.float32)
    _, o = lax.scan(step, S0, (chunks(q), chunks(k), chunks(iv), chunks(log_f)))
    return o.transpose(1, 0, 3, 2, 4).reshape(B, T, H, DV)

def _spatial_gating(uv, w_s, b_s, ln_g, ln_b):
    B, T, _ = uv.shape
    u, v = jnp.split(uv, 2, axis=-1)
    v = _layer_norm(v.reshape(B, T, SG_GROUPS, SG_DIM), ln_g, ln_b)
    v = v.reshape(B, T // SG_CHUNK, SG_CHUNK, SG_GROUPS, SG_DIM)
    causal = jnp.tril(jnp.ones((SG_CHUNK, SG_CHUNK), dtype=bool))
    w = jnp.where(causal, w_s, 0.0)
    s = jnp.einsum('gts,bnsgc->bntgc', w, v) + b_s.T[None, None, :, :, None]
    return u * s.reshape(B, T, SG_WIDTH)

def _token_mixers(h, w_in, lb, hg_norm_g, sg_ln_g, sg_ln_b, sg_w_s, sg_b_s, w_out):
    B, T, _ = h.shape
    proj = h @ w_in
    q, fz, iv, g, uv = jnp.split(
        proj, [HG_WIDTH, 2 * HG_WIDTH, 3 * HG_WIDTH, 4 * HG_WIDTH], axis=-1)
    heads = lambda a: a.reshape(B, T, HG_HEADS, -1)
    o = _hgrn2(heads(q), heads(fz), heads(iv), lb)
    o = _rms_norm(o, hg_norm_g) * jax.nn.silu(heads(g).astype(jnp.float32))
    o_a = o.reshape(B, T, HG_WIDTH).astype(h.dtype)
    o_b = _spatial_gating(jax.nn.gelu(uv), sg_w_s, sg_b_s, sg_ln_g, sg_ln_b)
    return jnp.concatenate([o_a, o_b], axis=-1) @ w_out

def _memory_cross_attention(h, mem, mem_g, mem_b, wq, wk, wv, wo):
    B, T, _ = h.shape
    M = mem.shape[1]
    m = _layer_norm(mem, mem_g, mem_b)
    q = (h @ wq).reshape(B, T, X_HEADS, X_HEAD_DIM)
    k = (m @ wk).reshape(B, M, X_HEADS, X_HEAD_DIM)
    v = (m @ wv).reshape(B, M, X_HEADS, X_HEAD_DIM)
    s = jnp.einsum('bthd,bmhd->bhtm', q.astype(jnp.float32), k.astype(jnp.float32)) * (X_HEAD_DIM ** -0.5)
    p = jax.nn.softmax(s, axis=-1).astype(h.dtype)
    o = jnp.einsum('bhtm,bmhd->bthd', p, v).reshape(B, T, D_MODEL)
    return o @ wo

def first_inputs(seed: int = 0) -> dict:
    key = jax.random.key(seed)
    ks = iter(jax.random.split(key, 48))
    L = DEPTH

    def nrm(shape, scale):
        return jax.random.normal(next(ks), shape, jnp.float32) * scale

    def gain(shape):
        return 1.0 + nrm(shape, 0.05)

    def bias(shape):
        return nrm(shape, 0.01)

    d_in = D_MODEL ** -0.5
    f_in = D_FF ** -0.5
    return {
        "x": nrm((BATCH, SEQ, D_MODEL), 1.0),
        "mem": nrm((BATCH, MEM_LEN, D_MODEL), 1.0),
        "ffn1_w_gate": nrm((L, D_MODEL, D_FF), d_in),
        "ffn1_w_up": nrm((L, D_MODEL, D_FF), d_in),
        "ffn1_w_down": nrm((L, D_FF, D_MODEL), f_in * BETA),
        "ln1_g": gain((L, D_MODEL)),
        "ln1_b": bias((L, D_MODEL)),
        "w_in": nrm((L, D_MODEL, IN_WIDTH), d_in),
        "hg_lb_logits": nrm((DEPTH + 1, HG_HEADS, HG_DK), 0.5),
        "hg_norm_g": gain((L, HG_DV)),
        "sg_ln_g": gain((L, SG_GROUPS, SG_DIM)),
        "sg_ln_b": bias((L, SG_GROUPS, SG_DIM)),
        "sg_w_s": nrm((L, SG_GROUPS, SG_CHUNK, SG_CHUNK), SG_CHUNK ** -0.5),
        "sg_b_s": gain((L, SG_GROUPS, SG_CHUNK)),
        "w_out": nrm((L, MIX_WIDTH, D_MODEL), (MIX_WIDTH ** -0.5) * BETA),
        "ln2_g": gain((L, D_MODEL)),
        "ln2_b": bias((L, D_MODEL)),
        "mem_ln_g": gain((L, D_MODEL)),
        "mem_ln_b": bias((L, D_MODEL)),
        "xa_w_q": nrm((L, D_MODEL, D_MODEL), d_in),
        "xa_w_k": nrm((L, D_MODEL, D_MODEL), d_in),
        "xa_w_v": nrm((L, D_MODEL, D_MODEL), d_in * BETA),
        "xa_w_o": nrm((L, D_MODEL, D_MODEL), d_in * BETA),
        "ln3_g": gain((L, D_MODEL)),
        "ln3_b": bias((L, D_MODEL)),
        "ffn2_w_gate": nrm((L, D_MODEL, D_FF), d_in),
        "ffn2_w_up": nrm((L, D_MODEL, D_FF), d_in),
        "ffn2_w_down": nrm((L, D_FF, D_MODEL), f_in * BETA),
        "ln4_g": gain((L, D_MODEL)),
        "ln4_b": bias((L, D_MODEL)),
    }

def first_block(x, mem, ffn1_w_gate, ffn1_w_up, ffn1_w_down, ln1_g, ln1_b,
              w_in, hg_lb_logits, hg_norm_g, sg_ln_g, sg_ln_b, sg_w_s, sg_b_s,
              w_out, ln2_g, ln2_b, mem_ln_g, mem_ln_b, xa_w_q, xa_w_k, xa_w_v,
              xa_w_o, ln3_g, ln3_b, ffn2_w_gate, ffn2_w_up, ffn2_w_down,
              ln4_g, ln4_b):
    lower_bounds = jnp.cumsum(jax.nn.softmax(hg_lb_logits.astype(jnp.float32), axis=0), axis=0)
    h = x
    for l in range(DEPTH):
        h = _layer_norm(ALPHA * h + 0.5 * _swiglu(h, ffn1_w_gate[l], ffn1_w_up[l], ffn1_w_down[l]),
                        ln1_g[l], ln1_b[l])
        mix = _token_mixers(h, w_in[l], lower_bounds[l], hg_norm_g[l], sg_ln_g[l], sg_ln_b[l],
                            sg_w_s[l], sg_b_s[l], w_out[l])
        h = _layer_norm(ALPHA * h + mix, ln2_g[l], ln2_b[l])
        xa = _memory_cross_attention(h, mem, mem_ln_g[l], mem_ln_b[l], xa_w_q[l], xa_w_k[l],
                                     xa_w_v[l], xa_w_o[l])
        h = _layer_norm(ALPHA * h + xa, ln3_g[l], ln3_b[l])
        h = _layer_norm(ALPHA * h + 0.5 * _swiglu(h, ffn2_w_gate[l], ffn2_w_up[l], ffn2_w_down[l]),
                        ln4_g[l], ln4_b[l])
    return h


GRID_W = 64
CTX_LEN = 256
D_BRANCH = D_MODEL // 2
NA_HEAD_DIM = 64
NA_HEADS = D_BRANCH // NA_HEAD_DIM
WIN_ROWS = 8
WIN_COLS = 16
Q_COLS = 16
BAND_COLS = min(Q_COLS + WIN_COLS, GRID_W)
SHORT_CONV_W = 3
CONF_CONV_W = 31
N_BRANCH = 3
EPS = 1e-6
NEG_INF = -1e30

A_Q = 0 * D_BRANCH
A_K = 1 * D_BRANCH
A_V = 2 * D_BRANCH
A_Z = 3 * D_BRANCH
B_B = 4 * D_BRANCH
B_C = 5 * D_BRANCH
B_V = 6 * D_BRANCH
B_Z = 7 * D_BRANCH
C_GLU = 8 * D_BRANCH
C_Z = 10 * D_BRANCH
GATES = 11 * D_BRANCH
D_IN = GATES + N_BRANCH * D_MODEL


def rms_norm(x, g):
    x32 = x.astype(jnp.float32)
    y = x32 * lax.rsqrt(jnp.mean(x32 * x32, axis=-1, keepdims=True) + EPS)
    return (y * g.astype(jnp.float32)).astype(x.dtype)

def layer_norm(x, g, b):
    x32 = x.astype(jnp.float32)
    mu = jnp.mean(x32, axis=-1, keepdims=True)
    var = jnp.mean(jnp.square(x32 - mu), axis=-1, keepdims=True)
    y = (x32 - mu) * lax.rsqrt(var + EPS) * g.astype(jnp.float32) + b.astype(jnp.float32)
    return y.astype(x.dtype)

def dw_conv(x, w):
    k = w.shape[0]
    return lax.conv_general_dilated(
        x, w[:, None, :].astype(x.dtype), window_strides=(1,),
        padding=[((k - 1) // 2, k // 2)],
        dimension_numbers=('NWC', 'WIO', 'NWC'),
        feature_group_count=x.shape[-1])

def modulate(x, cond, norm_g, w_ada, b_ada):
    shift, scale, gate = jnp.split(jax.nn.silu(cond) @ w_ada + b_ada, 3, axis=-1)
    if cond.ndim == 2:
        shift, scale, gate = shift[:, None], scale[:, None], gate[:, None]
    return rms_norm(x, norm_g) * (1 + scale) + shift, gate

def heads(t):
    return t.reshape(t.shape[:-1] + (NA_HEADS, NA_HEAD_DIM))

def na_query(z, qn_g):
    return rms_norm(heads(z[..., A_Q:A_K]), qn_g) * NA_HEAD_DIM ** -0.5

def na_kv(zkv, kn_g):
    return rms_norm(heads(zkv[..., :D_BRANCH]), kn_g), heads(zkv[..., D_BRANCH:])

def neighbourhood_attention(q, k, v, kc, vc, rpb):
    bsz, seq, n_h, hd = q.shape
    rows = seq // GRID_W
    win_r = min(WIN_ROWS, rows)
    n_cb = GRID_W // Q_COLS
    qg = q.reshape(bsz, rows, n_cb, Q_COLS, n_h, hd)
    kg = k.reshape(bsz, rows, GRID_W, n_h, hd)
    vg = v.reshape(bsz, rows, GRID_W, n_h, hd)
    qcol = jnp.arange(GRID_W).reshape(n_cb, Q_COLS)
    col_start = jnp.clip(qcol - WIN_COLS // 2, 0, GRID_W - WIN_COLS)
    band_start = jnp.clip(jnp.arange(n_cb) * Q_COLS - WIN_COLS // 2, 0, GRID_W - BAND_COLS)
    band_cols = band_start[:, None] + jnp.arange(BAND_COLS)
    rel = band_cols[:, None, :] - col_start[:, :, None]
    col_valid = (rel >= 0) & (rel < WIN_COLS)
    dcol = jnp.clip(band_cols[:, None, :] - qcol[:, :, None], -(WIN_COLS - 1), WIN_COLS - 1) + WIN_COLS - 1
    n_loc = win_r * BAND_COLS

    def row_block(r):
        rs = jnp.clip(r - win_r // 2, 0, rows - win_r)
        q_r = lax.dynamic_index_in_dim(qg, r, axis=1, keepdims=False)
        k_r = lax.dynamic_slice_in_dim(kg, rs, win_r, axis=1)
        v_r = lax.dynamic_slice_in_dim(vg, rs, win_r, axis=1)
        kb = k_r[:, :, band_cols]
        vb = v_r[:, :, band_cols]
        s_loc = jnp.einsum('bcqhd,brcmhd->bhcqrm', q_r, kb).astype(jnp.float32)
        drow = rs + jnp.arange(win_r) - r + WIN_ROWS - 1
        bias = jnp.transpose(rpb[:, drow][:, :, dcol], (0, 2, 3, 1, 4))
        s_loc = jnp.where(col_valid[:, :, None, :], s_loc + bias.astype(jnp.float32), NEG_INF)
        s_ctx = jnp.einsum('bcqhd,blhd->bhcql', q_r, kc).astype(jnp.float32)
        s = jnp.concatenate([s_loc.reshape(bsz, n_h, n_cb, Q_COLS, n_loc), s_ctx], axis=-1)
        p = jax.nn.softmax(s, axis=-1).astype(v.dtype)
        p_loc = p[..., :n_loc].reshape(bsz, n_h, n_cb, Q_COLS, win_r, BAND_COLS)
        p_ctx = p[..., n_loc:]
        return (jnp.einsum('bhcqrm,brcmhd->bcqhd', p_loc, vb)
                + jnp.einsum('bhcql,blhd->bcqhd', p_ctx, vc))

    out = lax.map(row_block, jnp.arange(rows))
    return jnp.moveaxis(out, 0, 1).reshape(bsz, seq, n_h * hd)

def context_attention(qc, kc, vc):
    s = jnp.einsum('blhd,bmhd->bhlm', qc, kc).astype(jnp.float32)
    p = jax.nn.softmax(s, axis=-1).astype(vc.dtype)
    o = jnp.einsum('bhlm,bmhd->blhd', p, vc)
    return o.reshape(o.shape[:2] + (NA_HEADS * NA_HEAD_DIM,))

def short_conv_branch(z, w_conv):
    bg, cg, val, gz = z[..., B_B:B_C], z[..., B_C:B_V], z[..., B_V:B_Z], z[..., B_Z:C_GLU]
    return bg * dw_conv(cg * val, w_conv) * jax.nn.silu(gz)

def conformer_branch(z, w_conv, b_conv, ln_g, ln_b):
    a, g = z[..., C_GLU:C_GLU + D_BRANCH], z[..., C_GLU + D_BRANCH:C_Z]
    u = dw_conv(a * jax.nn.sigmoid(g), w_conv) + b_conv
    u = jax.nn.silu(layer_norm(u, ln_g, ln_b))
    return u * jax.nn.silu(z[..., C_Z:GATES])

def merge_branches(z, ya, yb, yc, w_out_a, w_out_b, w_out_c, w_o):
    ga, gb, gc = jnp.split(jax.nn.sigmoid(z[..., GATES:]), N_BRANCH, axis=-1)
    m = ga * (ya @ w_out_a) + gb * (yb @ w_out_b) + gc * (yc @ w_out_c)
    return m @ w_o

def hybrid_layer(x, xc, c, c_ctx, lp, update_ctx):
    h, gate = modulate(x, c, lp['norm_g'], lp['w_ada'], lp['b_ada'])
    hc, gate_c = modulate(xc, c_ctx, lp['norm_g'], lp['w_ada'], lp['b_ada'])
    z = h @ lp['w_in']
    if update_ctx:
        zc = hc @ lp['w_in']
        kc, vc = na_kv(zc[..., A_K:A_Z], lp['k_norm_g'])
    else:
        kc, vc = na_kv(hc @ lp['w_in'][:, A_K:A_Z], lp['k_norm_g'])

    q = na_query(z, lp['q_norm_g'])
    k, v = na_kv(z[..., A_K:A_Z], lp['k_norm_g'])
    ya = neighbourhood_attention(q, k, v, kc, vc, lp['rpb']) * jax.nn.silu(z[..., A_Z:B_B])
    yb = short_conv_branch(z, lp['conv_short_w'])
    yc = conformer_branch(z, lp['conv_conf_w'], lp['conv_conf_b'], lp['ln_conf_g'], lp['ln_conf_b'])
    x = x + gate * merge_branches(z, ya, yb, yc, lp['w_out_a'], lp['w_out_b'], lp['w_out_c'], lp['w_o'])

    if update_ctx:
        qc = na_query(zc, lp['q_norm_g'])
        yac = context_attention(qc, kc, vc) * jax.nn.silu(zc[..., A_Z:B_B])
        ybc = short_conv_branch(zc, lp['conv_short_w'])
        ycc = conformer_branch(zc, lp['conv_conf_w'], lp['conv_conf_b'], lp['ln_conf_g'], lp['ln_conf_b'])
        xc = xc + gate_c * merge_branches(zc, yac, ybc, ycc, lp['w_out_a'], lp['w_out_b'], lp['w_out_c'], lp['w_o'])
    return x, xc

def second_inputs(seed: int = 0) -> dict:
    key = jax.random.key(seed)
    ks = jax.random.split(key, 20)

    def nrm(k, shape, scale):
        return jax.random.normal(k, shape, jnp.float32) * scale

    return {
        'x': nrm(ks[0], (BATCH, SEQ, D_MODEL), 1.0),
        'c': nrm(ks[1], (BATCH, D_MODEL), 1.0),
        'ctx': nrm(ks[2], (BATCH, CTX_LEN, D_MODEL), 1.0),
        'c_ctx': nrm(ks[3], (D_MODEL,), 1.0),
        'norm_g': 1.0 + nrm(ks[4], (DEPTH, D_MODEL), 0.05),
        'w_ada': nrm(ks[5], (DEPTH, D_MODEL, 3 * D_MODEL), D_MODEL ** -0.5),
        'b_ada': nrm(ks[6], (DEPTH, 3 * D_MODEL), 0.02),
        'w_in': nrm(ks[7], (DEPTH, D_MODEL, D_IN), D_MODEL ** -0.5),
        'q_norm_g': 1.0 + nrm(ks[8], (DEPTH, NA_HEAD_DIM), 0.05),
        'k_norm_g': 1.0 + nrm(ks[9], (DEPTH, NA_HEAD_DIM), 0.05),
        'rpb': nrm(ks[10], (DEPTH, NA_HEADS, 2 * WIN_ROWS - 1, 2 * WIN_COLS - 1), 0.1),
        'conv_short_w': nrm(ks[11], (DEPTH, SHORT_CONV_W, D_BRANCH), SHORT_CONV_W ** -0.5),
        'conv_conf_w': nrm(ks[12], (DEPTH, CONF_CONV_W, D_BRANCH), CONF_CONV_W ** -0.5),
        'conv_conf_b': nrm(ks[13], (DEPTH, D_BRANCH), 0.02),
        'ln_conf_g': 1.0 + nrm(ks[14], (DEPTH, D_BRANCH), 0.05),
        'ln_conf_b': nrm(ks[15], (DEPTH, D_BRANCH), 0.02),
        'w_out_a': nrm(ks[16], (DEPTH, D_BRANCH, D_MODEL), D_BRANCH ** -0.5),
        'w_out_b': nrm(ks[17], (DEPTH, D_BRANCH, D_MODEL), D_BRANCH ** -0.5),
        'w_out_c': nrm(ks[18], (DEPTH, D_BRANCH, D_MODEL), D_BRANCH ** -0.5),
        'w_o': nrm(ks[19], (DEPTH, D_MODEL, D_MODEL), D_MODEL ** -0.5),
    }

def second_block(x, c, ctx, c_ctx, norm_g, w_ada, b_ada, w_in, q_norm_g, k_norm_g, rpb,
              conv_short_w, conv_conf_w, conv_conf_b, ln_conf_g, ln_conf_b,
              w_out_a, w_out_b, w_out_c, w_o):
    xc = ctx
    for l in range(DEPTH):
        lp = {
            'norm_g': norm_g[l], 'w_ada': w_ada[l], 'b_ada': b_ada[l], 'w_in': w_in[l],
            'q_norm_g': q_norm_g[l], 'k_norm_g': k_norm_g[l], 'rpb': rpb[l],
            'conv_short_w': conv_short_w[l], 'conv_conf_w': conv_conf_w[l],
            'conv_conf_b': conv_conf_b[l], 'ln_conf_g': ln_conf_g[l], 'ln_conf_b': ln_conf_b[l],
            'w_out_a': w_out_a[l], 'w_out_b': w_out_b[l], 'w_out_c': w_out_c[l], 'w_o': w_o[l],
        }
        x, xc = hybrid_layer(x, xc, c, c_ctx, lp, update_ctx=(l < DEPTH - 1))
    return x


def setup_inputs(seed=0):
    out = dict(first_inputs(seed))
    for name, value in second_inputs(seed + 1).items():
        if name != "x":
            out[name + "_2"] = value
    return out


def reference(
    x, mem, ffn1_w_gate, ffn1_w_up, ffn1_w_down, ln1_g, ln1_b, w_in, hg_lb_logits, hg_norm_g,
    sg_ln_g, sg_ln_b, sg_w_s, sg_b_s, w_out, ln2_g, ln2_b, mem_ln_g, mem_ln_b, xa_w_q, xa_w_k,
    xa_w_v, xa_w_o, ln3_g, ln3_b, ffn2_w_gate, ffn2_w_up, ffn2_w_down, ln4_g, ln4_b, c_2, ctx_2,
    c_ctx_2, norm_g_2, w_ada_2, b_ada_2, w_in_2, q_norm_g_2, k_norm_g_2, rpb_2, conv_short_w_2,
    conv_conf_w_2, conv_conf_b_2, ln_conf_g_2, ln_conf_b_2, w_out_a_2, w_out_b_2, w_out_c_2,
    w_o_2,
):
    x = first_block(
        x, mem, ffn1_w_gate, ffn1_w_up, ffn1_w_down, ln1_g, ln1_b, w_in, hg_lb_logits,
        hg_norm_g, sg_ln_g, sg_ln_b, sg_w_s, sg_b_s, w_out, ln2_g, ln2_b, mem_ln_g, mem_ln_b,
        xa_w_q, xa_w_k, xa_w_v, xa_w_o, ln3_g, ln3_b, ffn2_w_gate, ffn2_w_up, ffn2_w_down,
        ln4_g, ln4_b,
    )
    return second_block(
        x, c_2, ctx_2, c_ctx_2, norm_g_2, w_ada_2, b_ada_2, w_in_2, q_norm_g_2, k_norm_g_2,
        rpb_2, conv_short_w_2, conv_conf_w_2, conv_conf_b_2, ln_conf_g_2, ln_conf_b_2,
        w_out_a_2, w_out_b_2, w_out_c_2, w_o_2,
    )


_drawn_inputs = setup_inputs


def setup_inputs(seed=0):
    import zlib

    import numpy as np

    out = dict(_drawn_inputs(seed))
    spreads = {}
    factors = {'ln1_b': 3.6,
     'hg_norm_g': 3.753,
     'sg_ln_g': 5.224,
     'sg_ln_b': 8.0,
     'sg_b_s': 3.923,
     'ln2_b': 4.285,
     'mem_ln_g': 8.0,
     'mem_ln_b': 8.0,
     'ln3_b': 4.113,
     'ln4_b': 4.294,
     'ctx_2': 3.162,
     'q_norm_g_2': 8.0,
     'k_norm_g_2': 8.0,
     'rpb_2': 41.192,
     'conv_conf_b_2': 8.0,
     'ln_conf_g_2': 6.695,
     'ln_conf_b_2': 26.2}
    for name, (base, spread) in spreads.items():
        noise = np.random.default_rng([zlib.crc32(name.encode()), seed]).standard_normal(out[name].shape)
        drawn = base * np.exp(spread * noise) if base else spread * noise
        out[name] = __import__('jax').numpy.asarray(drawn.astype(out[name].dtype))
    for name, factor in factors.items():
        out[name] = (out[name] * factor).astype(out[name].dtype)
    return out
```

```python
from contextlib import ExitStack

import concourse.bass as bass
import numpy as np
from concourse import mybir

F32 = mybir.dt.float32
F32R = mybir.dt.float32r
I32 = mybir.dt.int32
ACT = mybir.ActivationFunctionType
ALU = mybir.AluOpType
AX = mybir.AxisListType.X

P = 128
T = 512
D = 1024
KD = D // P
TB = T // P
F_FF = 2816
KF = F_FF // P
M = 256
MB = M // P
HH = 4
W5 = 512
KW = W5 // P
ALPHA = 2.0 ** 0.25
LN_EPS = 1e-5
EPS = 1e-6
XH = 4
NH = 8
HD = 64
ROWS, GRID = 8, 64
QC, BAND = 16, 32
NCB = GRID // QC
BAND_AT = [0, 8, 24, 32]
BIAS_KIND = [0, 1, 1, 2]
BIAS_OFF = [0, -8, -16]
BIAS_AT = 16
RPB_W = BIAS_AT + BAND
TAPS = 31
NA_LINKS = 54
LEVELS = 7
RING = 4
SB = 8

S_FFN1 = 0
S_DOWN1 = S_FFN1 + 2 * KF
DOWN_STRIPS = 3
ADA_FIRST = 8
S_ADA = S_DOWN1 + DOWN_STRIPS * KD
S_MIX = S_ADA + ADA_FIRST
S_WOUT = S_MIX + 24
S_MEMK = S_WOUT + 3 * KD
S_MEMV = S_MEMK + KD
S_XQ = S_MEMV + KD
S_CTXK = S_XQ + KD
S_XO = S_CTXK + KW
S_CTXV = S_XO + KD
S_FFN2 = S_CTXV + KW
S_DOWN2 = S_FFN2 + 2 * KF
S_NA = S_DOWN2 + DOWN_STRIPS * KD
NA_STRIPS = 12
S_MERGE = S_NA + NA_STRIPS * KW
MERGE_STRIPS = 5
S_WO = S_MERGE + MERGE_STRIPS * KD
STRIPS = S_WO + KD
assert STRIPS % RING == 0

G_FFN1 = 0
G_DOWN1 = G_FFN1 + 2 * KF
G_ADA = G_DOWN1 + KD
G_MIX = G_ADA + ADA_FIRST
G_WOUT = G_MIX + 24
G_MEMK = G_WOUT + 3 * KD
G_MEMV = G_MEMK + KD
G_XQ = G_MEMV + 2 * MB
G_CTXK = G_XQ + KD
G_XO = G_CTXK + KW
G_CTXV = G_XO + KD
G_FFN2 = G_CTXV + MB
G_DOWN2 = G_FFN2 + 2 * KF
G_NA = G_DOWN2 + KD
NA_GROUPS = 12
G_MERGE = G_NA + NA_GROUPS * KW
MERGE_GROUPS = 6
G_WO = G_MERGE + MERGE_GROUPS * KD

COLS = {}
for _name, _n in [("ln1_g", KD), ("ln1_b", KD), ("ln2_g", KD), ("ln2_b", KD), ("ln3_g", KD), ("ln3_b", KD),
                  ("ln4_g", KD), ("ln4_b", KD), ("mem_g", KD), ("mem_b", KD), ("norm_g", KD), ("lb", 2 * HH),
                  ("hg_g", 1), ("b_ada", 3 * KD), ("cond", 2 * KD), ("qn_g", 1), ("kn_g", 1),
                  ("short_w", 3 * KW), ("conf_w", TAPS * KW), ("conf_b", KW), ("lnc_g", KW), ("lnc_b", KW)]:
    COLS[_name] = (sum(n for _, n in COLS.values()), _n)
NCOLS = sum(n for _, n in COLS.values())


class Nth:

    def __init__(self, base, per=0, i=0):
        assert per % RING == 0
        self.base, self.per, self.i = base, per, i
        self.slot = base % RING
        self.turn = base // RING + (per // RING) * i if per else base // RING
        self.n = base + per * i if per else base

    def plus(self, k):
        return Nth(self.base + k, self.per, self.i)


def ge(eng, sem, value):
    if not (isinstance(value, int) and value <= 0):
        eng.wait_ge(sem, value)


class Chain:

    def __init__(self, eng, sem):
        self.eng, self.sem, self.n, self.extra = eng, sem, 0, 0

    def link(self, ins):
        ins.then_inc(self.sem, 1)
        self.n += 1
        self.eng.wait_ge(self.sem, self.n + self.extra)

    def enter(self, per, i):
        self.per, self.start, self.extra = per, self.n, per * i

    def leave(self, times):
        assert self.n - self.start == self.per, (self.n, self.start, self.per)
        self.n += self.per * (times - 1)
        self.extra = 0


def hybrid_blocks(nc, stream, x_in, mem_in, ctx_in, cols_in, const_in, mask_in, rows_in, wst_in, band_in, rpb_in,
                  out):
    with ExitStack() as ctx:
        def sem(name):
            return ctx.enter_context(nc.semaphore(name))

        def sb(name, shape, dt=F32, scope=ctx):
            return scope.enter_context(nc.sbuf_tensor(name, shape, dt))

        proj = ctx.enter_context(nc.psum_tensor("proj", [P, RING, T], F32))
        aux = ctx.enter_context(nc.psum_tensor("aux", [P, 4, T], F32))

        raw = sb("raw", [P, RING, SB * P])
        w_hi = sb("w_hi", [P, RING, SB * P], F32R)
        w_lo = sb("w_lo", [P, RING, SB * P], F32R)
        h = sb("h", [P, KD, T])
        a_hi = sb("a_hi", [P, KD, T], F32R)
        a_lo = sb("a_lo", [P, KD, T], F32R)
        cols = sb("cols", [P, NCOLS])
        consts = sb("consts", [P, 2, P])
        ident = consts[:, 0]
        blk64 = consts[:, 1]
        ones_full = sb("ones_full", [P, P])
        mean_d = sb("mean_d", [P, P])
        mean_w = sb("mean_w", [P, P])
        mean_p = sb("mean_p", [P, P])
        eps_c = sb("eps_c", [P, 4])
        stat = sb("stat", [P, 2, TB])
        junk = sb("junk", [P, 2])
        modv = sb("modv", [P, 3 * KD, 2])
        mod_a = sb("mod_a", [P, 2, KD])
        cond_s = sb("cond_s", [P, KD, 2])
        cond_hi = sb("cond_hi", [P, KD, 2], F32R)
        cond_lo = sb("cond_lo", [P, KD, 2], F32R)
        qg8 = sb("qg8", [P, 1])
        lbv = sb("lbv", [P, 8, HH])
        work = sb("work", [P, 2, T])
        zsum, diag = work[:, 0], work[:, 1]
        sq = sb("sq", [P, 2, T])
        ctxk = sb("ctxk", [P, KW, M])
        ctxv = sb("ctxv", [P, MB, W5])

        def col(name, c=0, n=1):
            at, _ = COLS[name]
            return cols[:, at + c:at + c + n]

        with ExitStack() as ph:
            hid_hi = sb("hid_hi", [P, KF, T], F32R, ph)
            hid_lo = sb("hid_lo", [P, KF, T], F32R, ph)
        with ExitStack() as ph:
            mq, mk, mb, mv, md = (sb(n, [P, HH, T], F32, ph) for n in ("mq", "mk", "mb", "mv", "md"))
            qk = sb("qk", [P, 2, HH, T], F32, ph)
            score = sb("score", [P, TB, HH, P], F32, ph)
            sv, su = (sb(n, [P, HH, T], F32, ph) for n in ("sv", "su"))
            levmask = sb("levmask", [P, LEVELS, P // 2], I32, ph)
            idmask = sb("idmask", [P, P], I32, ph)
            wst = sb("wst", [P, HH, P], F32, ph)
            rows = sb("rows", [P, 3, W5], F32, ph)
            bnst = sb("bnst", [P, 16, 6], F32, ph)
            bnag = sb("bnag", [P, 16, 2], F32, ph)
            vstd = sb("vstd", [P, 2, 16], F32, ph)
            decay = sb("decay", [P, HH, TB], F32, ph)
        with ExitStack() as ph:
            xq = sb("xq", [P, KD, T], F32, ph)
            memk = sb("memk", [P, KD, M], F32, ph)
            memv = sb("memv", [P, MB, D], F32, ph)
            xp = sb("xp", [P, 2, 2, M], F32, ph)
            xpt = sb("xpt", [P, 2, MB, M], F32, ph)
            xs = sb("xs", [P, 3, 8, 2], F32, ph)
            side = sb("side", [P, KD, M], F32, ph)
            side_hi = sb("side_hi", [P, KD, M], F32R, ph)
            side_lo = sb("side_lo", [P, KD, M], F32R, ph)
            ksd = sb("ksd", [P, KW, M], F32, ph)
            krs = sb("krs", [P, KW, M], F32, ph)
        with ExitStack() as ph:
            with ExitStack() as part:
                y = sb("y", [P, 3, KW, T], F32, part)
                zc = sb("zc", [P, KW, T], F32, part)
            with ExitStack() as part:
                hm = sb("hm", [P, KD, T], F32, part)
            m_hi = sb("m_hi", [P, KD, T], F32R, ph)
            m_lo = sb("m_lo", [P, KD, T], F32R, ph)
            with ExitStack() as part:
                nq, nk, nza, nbg, ncg, nat, nsg, nzb = (
                    sb(n, [P, T], F32, part) for n in ("nq", "nk", "nza", "nbg", "ncg", "nat", "nsg", "nzb"))
                nvt = sb("nvt", [P, 2 * NCB, P], F32, part)
                nsq = sb("nsq", [P, 2, T], F32, part)
                vband = sb("vband", [P, 2 * NCB, P], F32, part)
                cv = sb("cv", [P, T + 2], F32, part)
                glu = sb("glu", [P, T + TAPS - 1], F32, part)
                ck_c = sb("ck_c", [P, M], F32, part)
                cv_c = sb("cv_c", [P, MB, P], F32, part)
                btab = sb("btab", [P, 2, ROWS * RPB_W], F32, part)
                bias = sb("bias", [P, 2, 3, ROWS * BAND], F32, part)
                band = sb("band", [P, 3, ROWS * BAND], F32, part)
                npr = sb("npr", [P, 2, T], F32, part)
                npt = sb("npt", [P, 2, T], F32, part)
                ns = sb("ns", [P, 3, 8], F32, part)
                wtap = sb("wtap", [P, TAPS + 4], F32, part)
            with ExitStack() as part:
                y_hi = sb("y_hi", [P, 3 * KW, T], F32R, part)
                y_lo = sb("y_lo", [P, 3 * KW, T], F32R, part)
                gate = sb("gate", [P, 3, T], F32, part)
                mrg = sb("mrg", [P, 2, T], F32, part)

        raw_in = [sem(f"raw_in{s}") for s in range(RING)]
        hi_ready, lo_ready = sem("hi_ready"), sem("lo_ready")
        strip_done = sem("strip_done")
        proj_read = [sem(f"proj_read{b}") for b in range(RING)]
        in_cols, in_const, in_mask, in_mem, in_ctx, in_band = (
            sem(n) for n in ("in_cols", "in_const", "in_mask", "in_mem", "in_ctx", "in_band"))
        in_x = [sem(f"in_x{n}") for n in range(4)]
        const_set = sem("const_set")
        dve_step, act_step, pool_step = sem("dve_step"), sem("act_step"), sem("pool_step")
        x_hi, x_lo = sem("x_hi"), sem("x_lo")
        cond_silu, cond_split = sem("cond_silu"), sem("cond_split")
        hid_h, hid_l = sem("hid_h"), sem("hid_l")
        zsum_step, n_mean, n_cent, n_sq, n_stat, n_std, n_diag, n_bc, n_xn, n_hi, n_raw, n_lo = (
            sem(n) for n in ("zsum_step", "n_mean", "n_cent", "n_sq", "n_stat", "n_std", "n_diag", "n_bc", "n_xn",
                             "n_hi", "n_raw", "n_lo"))
        mod_ready = sem("mod_ready")
        lb_max, lb_exp, lb_ready = sem("lb_max"), sem("lb_exp"), sem("lb_ready")
        m_sig, m_f, m_k, m_lf, m_b, m_fresh, m_zero = (
            sem(n) for n in ("m_sig", "m_f", "m_k", "m_lf", "m_b", "m_fresh", "m_zero"))
        l_diff, l_exp, l_lowk, l_fac, l_mm, l_put = (sem(n) for n in ("l_diff", "l_exp", "l_lowk", "l_fac", "l_mm", "l_put"))
        i_diff, i_expd, i_expb, i_ke, i_qe, i_tr, i_ket, i_kv, i_state, i_o, i_copy, i_osq, i_ms, i_std, i_on = (
            sem(n) for n in ("i_diff", "i_expd", "i_expb", "i_ke", "i_qe", "i_tr", "i_ket", "i_kv", "i_state", "i_o",
                             "i_copy", "i_osq", "i_ms", "i_std", "i_on"))
        v_var, v_std, v_norm, v_gain, v_mm, v_out, w_masked = (
            sem(n) for n in ("v_var", "v_std", "v_norm", "v_gain", "v_mm", "v_out", "w_masked"))
        mix_raw, mix_hi, mix_lo = sem("mix_raw"), sem("mix_hi"), sem("mix_lo")
        a_sc, a_max, a_exp, a_norm, a_tr, a_pt, a_pv, a_hi_s, a_lo_s = (
            sem(n) for n in ("a_sc", "a_max", "a_exp", "a_norm", "a_tr", "a_pt", "a_pv", "a_hi_s", "a_lo_s"))
        ck_sq, ck_ms, ck_std, ck_ready = sem("ck_sq"), sem("ck_ms"), sem("ck_std"), sem("ck_ready")
        b_tab, b_ready, b_ctx, b_edge = sem("b_tab"), sem("b_ready"), sem("b_ctx"), sem("b_edge")
        na_vb, na_ksq, na_kms, na_kstd, na_k, na_qsq, na_q, na_silu, na_ya, na_yb, na_conv, na_glu = (
            sem(n) for n in ("na_vb", "na_ksq", "na_kms", "na_kstd", "na_k", "na_qsq", "na_q", "na_silu",
                             "na_ya", "na_yb", "na_conv", "na_glu"))
        u_sc, u_max, u_exp, u_norm, u_tr, u_pt, u_pv = (
            sem(n) for n in ("u_sc", "u_max", "u_exp", "u_norm", "u_tr", "u_pt", "u_pv"))
        y_silu, y_c, y_hi_s, y_lo_s = sem("y_silu"), sem("y_c"), sem("y_hi_s"), sem("y_lo_s")
        m_raw, m_hi_s, m_lo_s, na_conv_b = (sem(n) for n in ("m_raw", "m_hi_s", "m_lo_s", "na_conv_b"))
        out_done = sem("out_done")

        def result(eng, st, g):
            eng.wait_ge(strip_done, st.n + 1)
            return proj[:, g.slot]

        def split_hi(act, st):
            if isinstance(st.n, int) and st.n >= STRIPS:
                return
            act.wait_ge(raw_in[st.slot], 16 * st.turn + 16)
            ge(act, strip_done, st.n - (RING - 1))
            nc.scalar.activation(w_hi[:, st.slot], raw[:, st.slot], ACT.Copy).then_inc(hi_ready, 1)

        def split_lo(dve, st):
            if isinstance(st.n, int) and st.n >= STRIPS:
                return
            dve.wait_ge(hi_ready, st.n + 1)
            nc.vector.tensor_tensor(w_lo[:, st.slot], raw[:, st.slot], w_hi[:, st.slot].bitcast(F32),
                                    ALU.subtract).then_inc(lo_ready, 1)

        def product(dst, wh, wl, xh, xl, start, stop, moving_weights=False):
            for n, (a, b) in enumerate(((wh, xh), (wh, xl), (wl, xh))):
                if moving_weights:
                    a, b = b, a
                mm = nc.tensor.matmul(dst, a, b, start=start and n == 0, stop=stop and n == 2)
            return mm

        def feature_strip(pe, st, g, xh, xl, first=0, blocks=SB, last=True, order=None, ready=None, n=T, blk0=0):
            pe.wait_ge(lo_ready, st.n + 1)
            if first == 0:
                ge(pe, proj_read[g.slot], g.turn)
            for j, k in enumerate(order or range(blocks)):
                if ready:
                    ready(k)
                at = (blk0 + k) * P
                mm = product(proj[:, g.slot, :n], w_hi[:, st.slot, at:at + P], w_lo[:, st.slot, at:at + P],
                             xh[:, first + k], xl[:, first + k], first == 0 and j == 0, last and j == blocks - 1)
            mm.then_inc(strip_done, 1)

        def token_strip(pe, st, q, groups, xh, xl, ready=None):
            pe.wait_ge(lo_ready, st.n + 1)
            for kk in range(2):
                k = 2 * q + kk
                if ready:
                    ready(k)
                for t, g in enumerate(groups):
                    if k == 0:
                        ge(pe, proj_read[g.slot], g.turn)
                    mm = product(proj[:, g.slot], w_hi[:, st.slot, kk * W5:(kk + 1) * W5],
                                 w_lo[:, st.slot, kk * W5:(kk + 1) * W5], xh[:, k, t * P:(t + 1) * P],
                                 xl[:, k, t * P:(t + 1) * P], k == 0, k == KD - 1, moving_weights=True)
            mm.then_inc(strip_done, 1)

        class Norm:
            def __init__(self, k, ck, n, chunks, src, dst, gain, shift, hi, lo, eps, mean, scale_by_mean=None):
                self.k, self.ck, self.n, self.chunks, self.src, self.dst = k, ck, n, chunks, src, dst
                self.gain, self.shift, self.hi, self.lo, self.eps, self.mean = gain, shift, hi, lo, eps, mean
                self.tb = n // P
                self.c0 = 8 * k
                self.z0 = 9 * (ck or 0)

        LN1 = Norm(0, 0, T, KD, h, h, lambda c: col("ln1_g", c), lambda c: col("ln1_b", c), a_hi, a_lo, 0, mean_d)
        MEMN = Norm(1, 1, M, KD, side, side, lambda c: col("mem_g", c), lambda c: col("mem_b", c), side_hi, side_lo,
                    1, mean_d)
        LN2 = Norm(2, 2, T, KD, h, h, lambda c: col("ln2_g", c), lambda c: col("ln2_b", c), a_hi, a_lo, 0, mean_d)
        CTXN = Norm(3, None, M, KD, side, side, lambda c: mod_a[:, 1, c:c + 1], lambda c: modv[:, c, 1:2],
                    side_hi, side_lo, 2, mean_d)
        LN3 = Norm(4, 3, T, KD, h, h, lambda c: col("ln3_g", c), lambda c: col("ln3_b", c), a_hi, a_lo, 0, mean_d)
        LN4 = Norm(5, 4, T, KD, h, h, lambda c: col("ln4_g", c), lambda c: col("ln4_b", c), None, None, 0, mean_d)
        MODN = Norm(6, None, T, KD, h, hm, lambda c: mod_a[:, 0, c:c + 1], lambda c: modv[:, c, 0:1], a_hi, a_lo, 2,
                    mean_d)
        CONFN = Norm(7, 5, T, KW, y[:, 2], y[:, 2], lambda c: col("lnc_g", c), lambda c: col("lnc_b", c), None, None,
                     2, mean_w)

        def pe_mean(pe, m):
            pe.wait_ge(zsum_step, m.z0 + 1 + m.chunks)
            nc.tensor.matmul(aux[:, 0, :m.n], m.mean[:], zsum[:, :m.n], start=True, stop=True).then_inc(n_mean, 1)

        def pe_stats(pe, m):
            for c in range(m.chunks):
                pe.wait_ge(n_sq, m.c0 + c + 1)
                for t in range(m.tb):
                    mm = nc.tensor.matmul(aux[:, 1, t:t + 1], sq[:, c % 2, t * P:(t + 1) * P], m.mean[:, 0:1],
                                          start=(c == 0 and t == 0), stop=(c == m.chunks - 1),
                                          skip_group_check=True)
                mm.then_inc(n_stat, 1)

        def pe_spread(pe, m):
            pe.wait_ge(n_diag, m.k + 1)
            nc.tensor.matmul(aux[:, 2, :m.n], ones_full[:], diag[:, :m.n], start=True, stop=True).then_inc(n_bc, 1)

        def dve_centre(dve, m):
            dve.wait_ge(n_mean, m.ck + 1)
            for c in range(m.chunks):
                nc.vector.tensor_tensor(m.src[:, c], m.src[:, c], aux[:, 0, :m.n], ALU.subtract).then_inc(n_cent, 1)

        def act_squares(act, m, ready=None):
            nc.scalar.activation(junk[:, 0:1], eps_c[:, 0:1], ACT.Sqrt)
            for c in range(m.chunks):
                if m.ck is None:
                    ready(c)
                else:
                    act.wait_ge(n_cent, 8 * m.ck + c + 1)
                if c >= 2:
                    act.wait_ge(n_stat, m.c0 + c - 1)
                nc.scalar.activation(sq[:, c % 2, :m.n], m.src[:, c], ACT.Square).then_inc(n_sq, 1)

        def act_std(act, m):
            act.wait_ge(n_stat, m.c0 + m.chunks)
            nc.scalar.activation(stat[:, 0, :m.tb], aux[:, 1, :m.tb], ACT.Sqrt,
                                 bias=eps_c[:, m.eps:m.eps + 1]).then_inc(n_std, 1)

        def dve_diag(dve, m, chain):
            dve.wait_ge(n_std, m.k + 1)
            chain.link(nc.vector.reciprocal(stat[:, 1, :m.tb], stat[:, 0, :m.tb]))
            nc.vector.tensor_tensor(diag[:, :m.n].rearrange("p (t q) -> p t q", t=m.tb),
                                    ident.unsqueeze(1).to_broadcast([P, m.tb, P]),
                                    stat[:, 1, :m.tb].unsqueeze(2).to_broadcast([P, m.tb, P]),
                                    ALU.mult).then_inc(n_diag, 1)

        def dve_normalise(dve, m):
            dve.wait_ge(n_bc, m.k + 1)
            for c in range(m.chunks + 2):
                if c < m.chunks:
                    nc.vector.tensor_tensor(m.dst[:, c], m.src[:, c], aux[:, 2, :m.n], ALU.mult).then_inc(n_xn, 1)
                if c >= 2 and m.lo is not None:
                    dve.wait_ge(n_raw, m.c0 + c - 1)
                    nc.vector.tensor_tensor(m.lo[:, c - 2], m.dst[:, c - 2], m.hi[:, c - 2].bitcast(F32),
                                            ALU.subtract).then_inc(n_lo, 1)

        def act_hi(act, m):
            for c in range(m.chunks):
                act.wait_ge(n_xn, m.c0 + c + 1)
                nc.scalar.activation(m.hi[:, c], m.dst[:, c], ACT.Identity, scale=m.gain(c),
                                     bias=m.shift(c)).then_inc(n_hi, 1)

        def pool_apply(pool, m, h0):
            for c in range(m.chunks):
                if m.hi is not None:
                    pool.wait_ge(n_hi, h0 + c + 1)
                else:
                    pool.wait_ge(n_xn, m.c0 + c + 1)
                nc.gpsimd.tensor_scalar(m.dst[:, c], m.dst[:, c], m.gain(c), m.shift(c), ALU.mult,
                                        ALU.add).then_inc(n_raw, 1)

        def pool_sum(pool, m, ready):
            ge(pool, n_mean, m.ck)
            nc.gpsimd.memset(zsum[:, :m.n], 0.0).then_inc(zsum_step, 1)
            for c in range(m.chunks):
                ready(c)
                pool.wait_ge(zsum_step, m.z0 + 1 + c)
                nc.gpsimd.tensor_tensor(zsum[:, :m.n], zsum[:, :m.n], m.src[:, c], ALU.add).then_inc(zsum_step, 1)

        def pool_sum_groups(pool, m, g0):
            ge(pool, n_mean, m.ck)
            nc.gpsimd.memset(zsum, 0.0).then_inc(zsum_step, 1)
            with pool.Fori(0, KD // RING) as i:
                for q in range(RING):
                    g = Nth(g0 + q, RING, i)
                    pool.wait_ge(proj_read[g.slot], g.turn + 1)
                    pool.wait_ge(zsum_step, m.z0 + 1 + q + RING * i)
                    nc.gpsimd.tensor_tensor(zsum, zsum, h[:, bass.ds(RING * i + q, 1)].rearrange("p a t -> p (a t)"),
                                            ALU.add).then_inc(zsum_step, 1)

        HI0 = {0: 0, 1: 8, 2: 16, 3: 24, 4: 32, 6: 40}

        def lo_ready_of(pe, m, h0):
            return lambda k: pe.wait_ge(n_lo, h0 + k + 1)

        def dve_residual(dve, s0, g0, factor, per_out=1):
            with dve.Fori(0, KD // RING) as i:
                for q in range(RING):
                    for j in range(per_out):
                        st = Nth(s0 + q * per_out + j, RING * per_out, i)
                        split_lo(dve, st.plus(3))
                    g = Nth(g0 + q, RING, i)
                    res = result(dve, st, g)
                    hc = h[:, bass.ds(RING * i + q, 1)].rearrange("p a t -> p (a t)")
                    nc.vector.scalar_tensor_tensor(hc, res, factor, hc, ALU.mult, ALU.add).then_inc(proj_read[g.slot], 1)

        def act_splits(act, s0, n):
            assert n % RING == 0
            with act.Fori(0, n // RING) as i:
                for q in range(RING):
                    split_hi(act, Nth(s0 + 3 + q, RING, i))

        def pe_ffn(pe, s0, g0, ready):
            def two(i, first):
                for j in range(4):
                    feature_strip(pe, Nth(s0 + j, 4, i), Nth(g0 + j, 4, i), a_hi, a_lo,
                                  ready=ready if first and j == 0 else None)
            two(0, True)
            with pe.Fori(1, KF // 2) as i:
                two(i, False)

        def pe_down(pe, s0, g0, hid0):
            pe.wait_ge(hid_l, hid0 + KF)
            with pe.Fori(0, KD // RING) as i:
                for q in range(RING):
                    for j in range(DOWN_STRIPS):
                        feature_strip(pe, Nth(s0 + q * DOWN_STRIPS + j, RING * DOWN_STRIPS, i), Nth(g0 + q, RING, i),
                                      hid_hi, hid_lo, first=SB * j, blocks=min(SB, KF - SB * j),
                                      last=(j == DOWN_STRIPS - 1))

        def act_ffn(act, s0, g0):
            def two(i, first):
                for j in range(4):
                    st, g = Nth(s0 + j, 4, i), Nth(g0 + j, 4, i)
                    split_hi(act, st.plus(3))
                    if j % 2 == 0:
                        res = result(act, st, g)
                        if not first:
                            act.wait_ge(proj_read[g.plus(1).slot], g.plus(1).turn)
                        nc.scalar.activation(sq[:, j // 2], res, ACT.Silu).then_inc(proj_read[g.slot], 1)
                    else:
                        act.wait_ge(proj_read[g.slot], g.turn + 1)
                        hc = hid_hi[:, bass.ds(2 * i + j // 2, 1)].rearrange("p a t -> p (a t)") if not first \
                            else hid_hi[:, j // 2]
                        nc.scalar.activation(hc, work[:, j // 2], ACT.Copy).then_inc(hid_h, 1)
            two(0, True)
            with act.Fori(1, KF // 2) as i:
                two(i, False)

        def dve_ffn(dve, s0, g0, hid0):
            def two(i, first):
                for j in range(4):
                    st, g = Nth(s0 + j, 4, i), Nth(g0 + j, 4, i)
                    split_lo(dve, st.plus(3))
                    if j % 2:
                        gate_g = Nth(g0 + j - 1, 4, i)
                        res = result(dve, st, g)
                        dve.wait_ge(proj_read[gate_g.slot], gate_g.turn + 1)
                        nc.vector.tensor_tensor(work[:, j // 2], sq[:, j // 2], res,
                                                ALU.mult).then_inc(proj_read[g.slot], 1)
                        dve.wait_ge(hid_h, hid0 + j // 2 + 1 + 2 * i)
                        a, b = (x[:, bass.ds(2 * i + j // 2, 1)].rearrange("p a t -> p (a t)") if not first
                                else x[:, j // 2] for x in (hid_lo, hid_hi))
                        nc.vector.tensor_tensor(a, work[:, j // 2], b.bitcast(F32), ALU.subtract).then_inc(hid_l, 1)
            two(0, True)
            with dve.Fori(1, KF // 2) as i:
                two(i, False)

        def ada_at(n):
            if n < ADA_FIRST:
                return Nth(S_ADA + n), Nth(G_ADA + n)
            m = n - ADA_FIRST
            at = 3 * (m // 2) + 1 + m % 2
            return Nth(S_WOUT + at), Nth(G_WOUT + at)

        def pe_ada(pe, lo, hi):
            for n in range(lo, hi):
                st, g = ada_at(n)
                if n == 0:
                    pe.wait_ge(cond_split, 1)
                feature_strip(pe, st, g, cond_hi, cond_lo, n=2)

        def dve_ada(dve, lo, hi):
            for n in range(lo, hi):
                st, g = ada_at(n)
                split_lo(dve, st.plus(3))
                res = result(dve, st, g)
                nc.vector.tensor_scalar(modv[:, n], res[:, 0:2], col("b_ada", n), None,
                                        ALU.add).then_inc(proj_read[g.slot], 1)

        def act_only_splits(act, s0, lo, hi):
            for n in range(lo, hi):
                split_hi(act, Nth(s0 + n + 3))

        def dve_only_splits(dve, s0, lo, hi):
            for n in range(lo, hi):
                split_lo(dve, Nth(s0 + n + 3))

        MIX_ORDER = [4, 5, 6, 7, 0, 1, 2, 3]

        def halves(x, lev, free=HH * T):
            n = 1 << lev
            flat = x.rearrange("p h t -> p (h t)")
            v = flat.rearrange("p (b two n) -> p b two n", two=2, n=n)
            return v[:, :, 0, :], v[:, :, 1, :]

        def level_ref(lev):
            n = 1 << lev
            lower, _ = halves(mb[:], lev)
            return lower[:, :, n - 1:n].to_broadcast([P, HH * T // (2 * n), n])

        def pe_level(pe, lev):
            if lev < LEVELS:
                pe.wait_ge(l_fac, lev + 1)
                pe.wait_ge(l_lowk, lev + 1)
            for cc in range(TB):
                for hd in range(HH):
                    if lev < LEVELS:
                        f = qk[:, lev % 2, hd, cc * P:(cc + 1) * P]
                        upper = f.rearrange("p (b two n) -> p b two n", two=2, n=1 << lev)[:, :, 1, :]
                        if cc % 2 == 0 and hd == 0 and lev:
                            pe.wait_ge(l_put, 2 * lev - 1 + cc // 2)
                        mm = nc.tensor.matmul(aux[:, cc // 2, (cc % 2) * 256 + hd * 64:(cc % 2) * 256 + hd * 64 + 64],
                                              f, upper, start=True, stop=True)
                        if cc % 2 and hd == HH - 1:
                            mm.then_inc(l_mm, 1)
                    else:
                        if cc < 2 and hd == 0:
                            pe.wait_ge(l_put, 2 * LEVELS - 1 + cc)
                        at = slice(cc * P, (cc + 1) * P)
                        mm = nc.tensor.matmul(aux[:, cc, hd * P:(hd + 1) * P], mk[:, hd, at], mq[:, hd, at],
                                              start=True, stop=True)
                        if hd == HH - 1:
                            mm.then_inc(l_mm, 1)

        def dve_put(dve, lev):
            if lev == 0:
                dve.wait_ge(m_zero, 1)
                dve.wait_ge(in_mask, 16 * 4)
            if lev < LEVELS:
                nb, n = P >> (lev + 1), 1 << lev
                for half in range(2):
                    dve.wait_ge(l_mm, 2 * lev + half + 1)
                    dst = score[:, 2 * half:2 * half + 2].rearrange("p c h (b two n) -> p (c h) b two n", two=2,
                                                                    n=n)[:, :, :, 1, :]
                    mask = levmask[:, lev].rearrange("p (b n) -> p b n", n=n).unsqueeze(1).to_broadcast(
                        [P, 2 * HH, nb, n])
                    data = aux[:, half].rearrange("p (c b n) -> p c b n", b=nb, n=n)
                    nc.vector.copy_predicated(dst, mask, data).then_inc(l_put, 1)
            else:
                for cc in range(TB):
                    dve.wait_ge(l_mm, 2 * LEVELS + cc + 1)
                    nc.vector.copy_predicated(score[:, cc], idmask[:].unsqueeze(1).to_broadcast([P, HH, P]),
                                              aux[:, cc].rearrange("p (h t) -> p h t", h=HH)).then_inc(l_put, 1)

        def dve_level(dve, lev):
            blo, bup = halves(mb[:], lev)
            dlo, dup = halves(md[:], lev)
            if lev >= 1:
                dve.wait_ge(l_lowk, lev)
                dve.wait_ge(l_fac, lev)
            if lev == 0:
                dve.wait_ge(m_b, HH)
            nc.vector.tensor_tensor(dlo, level_ref(lev), blo, ALU.subtract).then_inc(l_diff, 1)
            nc.vector.tensor_tensor(dup, bup, level_ref(lev), ALU.subtract).then_inc(l_diff, 1)

        def dve_level_mul(dve, lev):
            dve.wait_ge(l_exp, lev + 1)
            if lev >= 2:
                dve.wait_ge(l_mm, 2 * (lev - 1))
            _, dup = halves(md[:], lev)
            _, fup = halves(qk[:, lev % 2], lev)
            _, qup = halves(mq[:], lev)
            nc.vector.tensor_tensor(fup, dup, qup, ALU.mult).then_inc(l_fac, 1)

        def pool_level_mul(pool, lev):
            pool.wait_ge(l_exp, lev + 1)
            if lev == 0:
                pool.wait_ge(m_k, HH)
            if lev >= 2:
                pool.wait_ge(l_mm, 2 * (lev - 1))
            dlo, _ = halves(md[:], lev)
            flo, _ = halves(qk[:, lev % 2], lev)
            klo, _ = halves(mk[:], lev)
            nc.gpsimd.tensor_tensor(flo, dlo, klo, ALU.mult).then_inc(l_lowk, 1)

        def act_level(act, lev):
            act.wait_ge(l_diff, 2 * (lev + 1))
            nc.scalar.activation(md[:], md[:], ACT.Exp).then_inc(l_exp, 1)

        def pe_mix(pe):
            for i in range(24):
                st = Nth(S_MIX + i)
                ready = lo_ready_of(pe, LN1, HI0[0]) if i == 0 else None
                if 8 <= i < 16:
                    g0 = G_MIX + (i // 4) * 4
                    token_strip(pe, st, i % 4, [Nth(g0 + t) for t in range(TB)], a_hi, a_lo)
                else:
                    feature_strip(pe, st, Nth(G_MIX + i), a_hi, a_lo, ready=ready)
                if 7 <= i <= 14:
                    pe_level(pe, i - 7)
                if i == 15:
                    for cc in range(TB - 1):
                        if cc == 0:
                            pe.wait_ge(i_ke, 1)
                            pe.wait_ge(l_put, 2 * LEVELS + TB)
                        for hd in range(HH):
                            mm = nc.tensor.transpose(aux[:, cc, hd * P:(hd + 1) * P],
                                                     qk[:, 1, hd, cc * P:(cc + 1) * P], ident)
                        mm.then_inc(i_tr, 1)
                if i == 16:
                    ket = md[:, 0:3].rearrange("p c (h d) -> p c h d", h=HH)
                    for cc in range(TB - 1):
                        pe.wait_ge(i_ket, 3)
                        for hd in range(HH):
                            mm = nc.tensor.matmul(aux[:, cc, hd * P:(hd + 1) * P], ket[:, cc, hd],
                                                  mv[:, cc, hd * P:(hd + 1) * P], start=True, stop=True)
                        mm.then_inc(i_kv, 1)
                if i == 18:
                    pe.wait_ge(i_qe, 1)
                    pe.wait_ge(i_state, 9)
                    state = mk[:, 0:3].rearrange("p c (h d) -> p c h d", h=HH)
                    for hd in range(HH):
                        for cc in range(TB):
                            o = aux[:, hd, cc * P:(cc + 1) * P]
                            mm = nc.tensor.matmul(o, mv[:, cc, hd * P:(hd + 1) * P], score[:, cc, hd], start=True,
                                                  stop=(cc == 0))
                            if cc:
                                mm = nc.tensor.matmul(o, state[:, cc - 1, hd], qk[:, 0, hd, cc * P:(cc + 1) * P],
                                                      start=False, stop=True)
                        mm.then_inc(i_o, 1)
                if i == 19:
                    for hd in range(HH):
                        pe.wait_ge(i_osq, hd + 1)
                        nc.tensor.matmul(aux[:, hd], mean_p[:], mq[:, hd], start=True, stop=True).then_inc(i_ms, 1)
                if i == 21:
                    pe.wait_ge(v_gain, 2)
                    pe.wait_ge(w_masked, 1)
                    for g in range(HH):
                        pe.wait_ge(i_std, g + 1)
                        for t in range(TB):
                            mm = nc.tensor.matmul(aux[:, g, t * P:(t + 1) * P], sv[:, t, g * P:(g + 1) * P], wst[:, g],
                                                  start=True, stop=True)
                        mm.then_inc(v_mm, 1)

        def act_mix(act, chain):
            for i in range(24):
                st, g = Nth(S_MIX + i), Nth(G_MIX + i)
                split_hi(act, st.plus(3))
                if i < 4:
                    res = result(act, st, g)
                    nc.scalar.activation(md[:, i], res, ACT.Sigmoid).then_inc(m_sig, 1)
                    nc.scalar.activation(mk[:, i], res, ACT.Sigmoid, scale=-1.0).then_inc(proj_read[g.slot], 1)
                if i == 3:
                    act.wait_ge(m_f, HH)
                    nc.scalar.activation(md[:], md[:], ACT.Ln).then_inc(m_lf, 1)
                if 4 <= i < 8:
                    res = result(act, st, g)
                    nc.scalar.activation(mq[:, i - 4], res, ACT.Copy).then_inc(proj_read[g.slot], 1)
                if 6 <= i < 13:
                    act_level(act, i - 6)
                if i == 11:
                    for t in range(TB):
                        gt = Nth(G_MIX + 8 + t)
                        nc.scalar.activation(mv[:, t], result(act, st, gt), ACT.Copy).then_inc(proj_read[gt.slot], 1)
                if i == 13:
                    act.wait_ge(i_diff, 1)
                    nc.scalar.activation(md[:], md[:], ACT.Exp).then_inc(i_expd, 1)
                    nc.scalar.activation(mb[:], mb[:], ACT.Exp).then_inc(i_expb, 1)
                if i == 15:
                    for t in range(TB):
                        gt = Nth(G_MIX + 12 + t)
                        nc.scalar.activation(sv[:, t], result(act, st, gt),
                                             ACT.Gelu_apprx_tanh).then_inc(proj_read[gt.slot], 1)
                if i == 16:
                    for cc in range(TB - 1):
                        act.wait_ge(i_tr, cc + 1)
                        if cc == 0:
                            act.wait_ge(i_ke, 1)
                        nc.scalar.activation(md[:, cc], aux[:, cc], ACT.Copy).then_inc(i_ket, 1)
                if 16 <= i < 20:
                    res = result(act, st, g)
                    nc.scalar.activation(su[:, i - 16], res, ACT.Gelu_apprx_tanh).then_inc(proj_read[g.slot], 1)
                if i == 17:
                    act.wait_ge(v_var, 16)
                    nc.scalar.activation(vstd[:, 0], bnag[:, :, 1], ACT.Sqrt, bias=eps_c[:, 1:2]).then_inc(v_std, 1)
                if i == 19:
                    for hd in range(HH):
                        act.wait_ge(i_o, hd + 1)
                        nc.scalar.activation(mb[:, hd], aux[:, hd], ACT.Copy).then_inc(i_copy, 1)
                        nc.scalar.activation(mq[:, hd], aux[:, hd], ACT.Square).then_inc(i_osq, 1)
                if i == 20:
                    for hd in range(HH):
                        act.wait_ge(i_ms, hd + 1)
                        nc.scalar.activation(qk[:, 1, hd], aux[:, hd], ACT.Sqrt,
                                             bias=eps_c[:, 1:2]).then_inc(i_std, 1)
                if i >= 20:
                    res = result(act, st, g)
                    nc.scalar.activation(mk[:, i - 20], res, ACT.Silu).then_inc(proj_read[g.slot], 1)
            act.wait_ge(strip_done, S_MIX + 24)
            for n, k in enumerate(MIX_ORDER):
                src = mb[:, k] if k < HH else su[:, k - HH]
                if k < HH:
                    act.wait_ge(mix_raw, k + 1)
                else:
                    act.wait_ge(v_out, 2 * (k - HH + 1))
                nc.scalar.activation(a_hi[:, k], src, ACT.Copy).then_inc(mix_hi, 1)

        def dve_mix(dve, chain):
            link = chain.link
            for i in range(24):
                st, g = Nth(S_MIX + i), Nth(G_MIX + i)
                split_lo(dve, st.plus(3))
                if i < 4:
                    dve.wait_ge(m_sig, i + 1)
                    nc.vector.tensor_scalar(md[:, i], md[:, i], lbv[:, 5, i:i + 1], lbv[:, 4, i:i + 1], ALU.mult,
                                            ALU.add).then_inc(m_f, 1)
                    dve.wait_ge(proj_read[g.slot], g.turn + 1)
                    nc.vector.tensor_scalar(mk[:, i], mk[:, i], lbv[:, 5, i:i + 1], None, ALU.mult).then_inc(m_k, 1)
                if i == 4:
                    dve.wait_ge(m_lf, 1)
                    dve.wait_ge(m_fresh, 2)
                    for hd in range(HH):
                        nc.vector.tensor_tensor_scan(mb[:, hd], work[:, 0], md[:, hd], 0.0, ALU.mult,
                                                     ALU.add).then_inc(m_b, 1)
                if 8 <= i <= 14:
                    dve_put(dve, i - 8)
                if 6 <= i < 13:
                    dve_level(dve, i - 6)
                    if i == 6:
                        gq = Nth(G_MIX + 7)
                        dve.wait_ge(proj_read[gq.slot], gq.turn + 1)
                    dve_level_mul(dve, i - 6)
                if i == 13:
                    dve.wait_ge(l_lowk, LEVELS)
                    dve.wait_ge(l_fac, LEVELS)
                    bh = mb[:].rearrange("p h (c t) -> p (h c) t", c=TB)
                    nc.vector.tensor_tensor(md[:].rearrange("p h (c t) -> p (h c) t", c=TB),
                                            bh[:, :, P - 1:P].to_broadcast([P, HH * TB, P]), bh,
                                            ALU.subtract).then_inc(i_diff, 1)
                    dve.wait_ge(i_expd, 1)
                    dve.wait_ge(l_mm, 2 * 6)
                    nc.vector.tensor_tensor(qk[:, 1], mk[:], md[:], ALU.mult).then_inc(i_ke, 1)
                if i == 14:
                    dve.wait_ge(i_expb, 1)
                    dve.wait_ge(l_mm, 2 * 7)
                    link(nc.vector.tensor_copy(decay[:], mb[:].rearrange("p h (c t) -> p h c t", c=TB)[:, :, :, P - 1]))
                    nc.vector.tensor_tensor(qk[:, 0], mq[:], mb[:], ALU.mult).then_inc(i_qe, 1)
                if i == 15:
                    dve_put(dve, LEVELS)
                if i == 16:
                    for t in range(TB):
                        dve.wait_ge(proj_read[Nth(G_MIX + 12 + t).slot], Nth(G_MIX + 12 + t).turn + 1)
                        for gg in range(HH):
                            last = nc.vector.bn_stats(bnst[:, 4 * t + gg], sv[:, t, gg * P:(gg + 1) * P])
                    link(last)
                    for n in range(16):
                        nc.vector.bn_aggr(bnag[:, n], bnst[:, n]).then_inc(v_var, 1)
                if i == 17:
                    state = mk[:, 0:3].rearrange("p c (h d) -> p c h d", h=HH)
                    for cc in range(TB - 1):
                        dve.wait_ge(i_kv, cc + 1)
                        if cc == 0:
                            nc.vector.tensor_copy(mk[:, 0], aux[:, 0]).then_inc(i_state, 1)
                        else:
                            dve.wait_ge(i_state, 4 * cc - 3)
                            for hd in range(HH):
                                nc.vector.scalar_tensor_tensor(state[:, cc, hd], state[:, cc - 1, hd],
                                                               decay[:, hd, cc:cc + 1],
                                                               aux[:, cc, hd * P:(hd + 1) * P], ALU.mult,
                                                               ALU.add).then_inc(i_state, 1)
                    dve.wait_ge(v_std, 1)
                    link(nc.vector.reciprocal(vstd[:, 1], vstd[:, 0]))
                if i in (18, 19):
                    for t in range(2 * (i - 18), 2 * (i - 18) + 2):
                        for gg in range(HH):
                            n = 4 * t + gg
                            nc.vector.tensor_scalar(sv[:, t, gg * P:(gg + 1) * P], sv[:, t, gg * P:(gg + 1) * P],
                                                    bnag[:, n, 0:1], vstd[:, 1, n:n + 1], ALU.subtract,
                                                    ALU.mult).then_inc(v_norm, 1)
                if i >= 20:
                    hd = i - 20
                    dve.wait_ge(i_std, hd + 1)
                    link(nc.vector.reciprocal(md[:, hd], qk[:, 1, hd]))
                    dve.wait_ge(i_copy, hd + 1)
                    link(nc.vector.scalar_tensor_tensor(mb[:, hd], mb[:, hd], col("hg_g"), md[:, hd], ALU.mult,
                                                        ALU.mult))
                if i >= 22:
                    for gg in (2 * (i - 22), 2 * (i - 22) + 1):
                        dve.wait_ge(v_mm, gg + 1)
                        gu = Nth(G_MIX + 16 + gg)
                        dve.wait_ge(proj_read[gu.slot], gu.turn + 1)
                        dst = aux[:, gg].rearrange("p (c t) -> p c t", c=TB)
                        nc.vector.tensor_tensor(dst, dst, rows[:, 2, gg * P:(gg + 1) * P].unsqueeze(1).to_broadcast(
                            [P, TB, P]), ALU.add).then_inc(v_out, 1)
                        dve.wait_ge(v_out, 2 * gg + 1)
                        nc.vector.tensor_tensor(su[:, gg], su[:, gg], aux[:, gg], ALU.mult).then_inc(v_out, 1)
            for hd in range(HH):
                gh = Nth(G_MIX + 20 + hd)
                dve.wait_ge(proj_read[gh.slot], gh.turn + 1)
                nc.vector.tensor_tensor(mb[:, hd], mb[:, hd], mk[:, hd], ALU.mult).then_inc(mix_raw, 1)
            for n, k in enumerate(MIX_ORDER):
                src = mb[:, k] if k < HH else su[:, k - HH]
                dve.wait_ge(mix_hi, n + 1)
                nc.vector.tensor_tensor(a_lo[:, k], src, a_hi[:, k].bitcast(F32), ALU.subtract).then_inc(mix_lo, 1)

        def pool_mix(pool):
            pool.wait_ge(hid_l, KF)
            pool.wait_ge(strip_done, S_ADA)
            nc.gpsimd.memset(score[:].rearrange("p c h t -> p (c h t)"), 0.0).then_inc(m_zero, 1)
            pool.wait_ge(n_bc, 1)
            nc.gpsimd.memset(work[:, 0], 1.0).then_inc(m_fresh, 1)
            pool.wait_ge(m_fresh, 1)
            nc.gpsimd.memset(work[:, 0, 0:T:P], 0.0).then_inc(m_fresh, 1)
            for dst, src in ((levmask[:].rearrange("p l t -> p (l t)"), mask_in[:, 0:LEVELS * 64]),
                             (idmask[:], mask_in[:, LEVELS * 64:]),
                             (wst[:].rearrange("p g t -> p (g t)"), wst_in),
                             (rows[:].rearrange("p a t -> p (a t)"), rows_in.partition_broadcast(P))):
                pool.dma_start(dst, src).then_inc(in_mask, 16)
            pool.wait_ge(in_mask, 16 * 4)
            nc.gpsimd.affine_select(out=wst[:], in_=wst[:], compare_op=ALU.is_ge, fill=0.0, base=0,
                                    pattern=[[0, HH], [1, P]], channel_multiplier=-1).then_inc(w_masked, 1)
            for lev in range(LEVELS):
                pool_level_mul(pool, lev)
            for n in range(2):
                pool.wait_ge(v_norm, 16)
                if n:
                    pool.wait_ge(v_gain, 1)
                nc.gpsimd.tensor_tensor(sv[:], sv[:], rows[:, n].unsqueeze(1).to_broadcast([P, TB, W5]),
                                        (ALU.mult, ALU.add)[n]).then_inc(v_gain, 1)

        def pe_memkv(pe, lo, hi):
            for n in range(lo, hi):
                if n < KD:
                    feature_strip(pe, Nth(S_MEMK + n), Nth(G_MEMK + n), side_hi, side_lo, n=M,
                                  ready=lo_ready_of(pe, MEMN, HI0[1]) if n == 0 else None)
                else:
                    half = (n - KD) // 4
                    token_strip(pe, Nth(S_MEMK + n), n % 4, [Nth(G_MEMV + MB * half + t) for t in range(MB)],
                                side_hi, side_lo)

        def act_memkv(act, lo, hi):
            for n in range(lo, hi):
                st = Nth(S_MEMK + n)
                split_hi(act, st.plus(3))
                if n < KD:
                    g = Nth(G_MEMK + n)
                    nc.scalar.activation(memk[:, n], result(act, st, g)[:, :M],
                                         ACT.Copy).then_inc(proj_read[g.slot], 1)
                elif n % 4 == 3:
                    half = (n - KD) // 4
                    for t in range(MB):
                        g = Nth(G_MEMV + MB * half + t)
                        nc.scalar.activation(memv[:, t, half * W5:(half + 1) * W5], result(act, st, g),
                                             ACT.Copy).then_inc(proj_read[g.slot], 1)

        UNITS = 2 * XH

        def pe_attention(pe):
            def scores(u):
                hd, pr = u // 2, u % 2
                if u == 0:
                    pe.wait_ge(ck_std, 2)
                    for n in range(KD - RING, KD):
                        g = Nth(G_XQ + n)
                        pe.wait_ge(proj_read[g.slot], g.turn + 1)
                for t in range(2):
                    for kk in range(2):
                        at = (2 * pr + t) * P
                        mm = nc.tensor.matmul(aux[:, u % 2, t * M:(t + 1) * M], xq[:, 2 * hd + kk, at:at + P],
                                              memk[:, 2 * hd + kk], start=(kk == 0), stop=(kk == 1))
                mm.then_inc(a_sc, 1)

            def turn(u):
                pe.wait_ge(a_norm, 2 * u + 2)
                if u:
                    pe.wait_ge(a_pt, u)
                for mt in range(MB):
                    for t in range(2):
                        mm = nc.tensor.transpose(aux[:, 2, (2 * mt + t) * P:(2 * mt + t + 1) * P],
                                                 xp[:, u % 2, t, mt * P:(mt + 1) * P], ident)
                mm.then_inc(a_tr, 1)

            def values(u):
                pe.wait_ge(a_pt, u + 1)
                if u:
                    pe.wait_ge(a_lo_s, u)
                for dk in range(2):
                    for mt in range(MB):
                        at = (2 * (u // 2) + dk) * P
                        mm = nc.tensor.matmul(aux[:, 3, dk * M:(dk + 1) * M], memv[:, mt, at:at + P],
                                              xpt[:, u % 2, mt], start=(mt == 0), stop=(mt == MB - 1))
                mm.then_inc(a_pv, 1)

            scores(0)
            scores(1)
            for u in range(UNITS + 1):
                if u < UNITS:
                    turn(u)
                    if u + 2 < UNITS:
                        scores(u + 2)
                if u:
                    values(u - 1)

        def dve_attention(dve, chain):
            def top(u):
                dve.wait_ge(a_sc, u + 1)
                nc.vector.tensor_reduce(xs[:, 0, u], aux[:, u % 2].rearrange("p (t m) -> p t m", t=2), AX, ALU.max,
                                        negate=True).then_inc(a_max, 1)

            def norm(u):
                dve.wait_ge(a_exp, 2 * u + 2)
                chain.link(nc.vector.reciprocal(xs[:, 2, u], xs[:, 1, u]))
                for t in range(2):
                    nc.vector.tensor_scalar(xp[:, u % 2, t], xp[:, u % 2, t], xs[:, 2, u, t:t + 1], None,
                                            ALU.mult).then_inc(a_norm, 1)

            def take(u):
                dve.wait_ge(a_hi_s, u + 1)
                hd, pr = u // 2, u % 2
                dst = (x[:, 2 * hd:2 * hd + 2, pr * M:(pr + 1) * M] for x in (a_lo, a_hi))
                lo, hi = dst
                nc.vector.tensor_tensor(lo, aux[:, 3].rearrange("p (d t) -> p d t", d=2), hi.bitcast(F32),
                                        ALU.subtract).then_inc(a_lo_s, 1)

            top(0)
            for u in range(UNITS):
                if u + 1 < UNITS:
                    top(u + 1)
                norm(u)
                if u:
                    take(u - 1)
            take(UNITS - 1)

        def act_attention(act):
            def exps(u):
                act.wait_ge(a_max, u + 1)
                if u >= 2:
                    act.wait_ge(a_tr, u - 1)
                for t in range(2):
                    nc.scalar.activation(xp[:, u % 2, t], aux[:, u % 2, t * M:(t + 1) * M], ACT.Exp,
                                         bias=xs[:, 0, u, t:t + 1],
                                         accum_out=xs[:, 1, u, t:t + 1]).then_inc(a_exp, 1)

            def turned(u):
                act.wait_ge(a_tr, u + 1)
                if u >= 2:
                    act.wait_ge(a_pv, u - 1)
                nc.scalar.activation(xpt[:, u % 2].rearrange("p m t -> p (m t)"), aux[:, 2],
                                     ACT.Copy).then_inc(a_pt, 1)

            def take(u):
                act.wait_ge(a_pv, u + 1)
                hd, pr = u // 2, u % 2
                nc.scalar.activation(a_hi[:, 2 * hd:2 * hd + 2, pr * M:(pr + 1) * M],
                                     aux[:, 3].rearrange("p (d t) -> p d t", d=2), ACT.Copy).then_inc(a_hi_s, 1)

            exps(0)
            for u in range(UNITS):
                if u + 1 < UNITS:
                    exps(u + 1)
                turned(u)
                if u:
                    take(u - 1)
            take(UNITS - 1)

        def pe_ctxk(pe):
            for n in range(KW):
                feature_strip(pe, Nth(S_CTXK + n), Nth(G_CTXK + n), side_hi, side_lo, n=M,
                              ready=lo_ready_of(pe, CTXN, HI0[3]) if n == 0 else None)

        def act_ctxk(act):
            for n in range(KW):
                st, g = Nth(S_CTXK + n), Nth(G_CTXK + n)
                split_hi(act, st.plus(3))
                nc.scalar.activation(ksd[:, n], result(act, st, g)[:, :M], ACT.Square).then_inc(ck_sq, 1)
                nc.scalar.activation(ctxk[:, n], result(act, st, g)[:, :M], ACT.Copy).then_inc(proj_read[g.slot], 1)

        def pe_ctxk_norm(pe):
            pe.wait_ge(ck_sq, KW)
            for n in range(2):
                nc.tensor.matmul(aux[:, n], blk64, ksd[:, 2 * n:2 * n + 2].rearrange("p c t -> p (c t)"), start=True,
                                 stop=True).then_inc(ck_ms, 1)

        def act_ctxk_norm(act):
            for n in range(2):
                act.wait_ge(ck_ms, n + 1)
                nc.scalar.activation(krs[:, 2 * n:2 * n + 2].rearrange("p c t -> p (c t)"), aux[:, n], ACT.Sqrt,
                                     bias=eps_c[:, 2:3]).then_inc(ck_std, 1)

        def dve_ctxk_norm(dve, chain):
            dve.wait_ge(ck_std, 2)
            chain.link(nc.vector.reciprocal(ksd[:], krs[:]))
            dve.wait_ge(proj_read[Nth(G_CTXK + 3).slot], Nth(G_CTXK + 3).turn + 1)
            flat = [x[:].rearrange("p c t -> p (c t)") for x in (ctxk, ksd)]
            nc.vector.scalar_tensor_tensor(flat[0], flat[0], col("kn_g"), flat[1], ALU.mult,
                                           ALU.mult).then_inc(ck_ready, 1)

        def pe_ctxv(pe, lo, hi):
            for n in range(lo, hi):
                token_strip(pe, Nth(S_CTXV + n), n, [Nth(G_CTXV + t) for t in range(MB)], side_hi, side_lo)

        def act_ctxv_take(act):
            for t in range(MB):
                g = Nth(G_CTXV + t)
                nc.scalar.activation(ctxv[:, t], result(act, Nth(S_CTXV + 3), g),
                                     ACT.Copy).then_inc(proj_read[g.slot], 1)

        NA_G = [0, 1, 2, 3, 5, 6, 7, 8, 9, 10, 11, 11]
        UN = 2 * NCB

        def na_st(j, i):
            return Nth(S_NA + j, NA_STRIPS, i)

        def na_g(j, i):
            return Nth(G_NA + j, NA_GROUPS, i)

        def grid(x, rows, at, n, r0=0):
            return x.rearrange("p (r c) -> p r c", c=GRID)[:, r0:r0 + rows, at:at + n]

        def pe_na(pe, i, first):
            def scores(u):
                cb, lo = u // 2, HD * (u % 2)
                part = slice(lo, lo + HD)
                if u == 0:
                    pe.wait_ge(na_k, 1 + i)
                    pe.wait_ge(na_q, 1 + i)
                    pe.wait_ge(b_ctx, 2 + 2 * i)
                if u >= 2:
                    pe.wait_ge(u_exp, u - 1 + UN * i)
                q = nq[part, cb * P:(cb + 1) * P]
                nc.tensor.matmul(aux[:, u % 2, :M], q, grid(nk[part], ROWS, BAND_AT[cb], BAND), start=True, stop=True)
                nc.tensor.matmul(aux[:, u % 2, M:], q, ck_c[part], start=True, stop=True).then_inc(u_sc, 1)

            def turn(u):
                pe.wait_ge(u_norm, u + 1 + UN * i)
                if u or not first:
                    pe.wait_ge(u_pt, u + UN * i)
                for b in range(4):
                    mm = nc.tensor.transpose(aux[:, 2, b * P:(b + 1) * P], npr[:, u % 2, b * P:(b + 1) * P], ident)
                mm.then_inc(u_tr, 1)

            def values(u):
                cb, lo = u // 2, HD * (u % 2)
                pe.wait_ge(u_pt, u + 1 + UN * i)
                if u == 0 and not first:
                    pe.wait_ge(na_ya, i)
                for b in range(4):
                    v = vband[:, 2 * cb + b, lo:lo + HD] if b < 2 else cv_c[:, b - 2, lo:lo + HD]
                    mm = nc.tensor.matmul(aux[lo:lo + HD, 3, cb * P:(cb + 1) * P], v, npt[:, u % 2, b * P:(b + 1) * P],
                                          start=(b == 0), stop=(b == 3))
                mm.then_inc(u_pv, 1)

            for j in range(NA_STRIPS):
                st, g = na_st(j, i), na_g(NA_G[j], i)
                ready = lo_ready_of(pe, MODN, HI0[6]) if first and j == 0 else None
                if j < 10:
                    feature_strip(pe, st, g, a_hi, a_lo, ready=ready)
                else:
                    feature_strip(pe, st, g, a_hi, a_lo, first=4 * (j - 10), blocks=4, last=(j == 11))
                if j == 1:
                    pe.wait_ge(proj_read[na_g(0, i).slot], na_g(0, i).turn + 1)
                    for n in range(2 * NCB):
                        mm = nc.tensor.transpose(aux[:, n // 4, (n % 4) * P:(n % 4 + 1) * P],
                                                 nvt[:, n], ident)
                        if n % 4 == 3:
                            mm.then_inc(na_vb, 1)
                if j == 2:
                    pe.wait_ge(na_ksq, 1 + i)
                    nc.tensor.matmul(aux[:, 2], blk64, nsq[:, 0], start=True, stop=True).then_inc(na_kms, 1)
                if j == 3:
                    gq = na_g(4, i)
                    pe.wait_ge(na_qsq, 1 + i)
                    pe.wait_ge(proj_read[gq.slot], gq.turn)
                    nc.tensor.matmul(proj[:, gq.slot], blk64, nsq[:, 1], start=True, stop=True).then_inc(na_kms, 1)
                a = 2 * (j - 6)
                if 6 <= j <= 9:
                    turn(a)
                if 7 <= j <= 10:
                    values(a - 2)
                    values(a - 1)
                if 6 <= j <= 9:
                    turn(a + 1)
                if 5 <= j <= 8:
                    scores(a + 2)
                    scores(a + 3)

        def chunk(x, i):
            return x[:, i] if isinstance(i, int) else x[:, bass.ds(i, 1)].rearrange("p a t -> p (a t)")

        def act_na(act, i, first, chain):
            def exps(u):
                act.wait_ge(u_max, u + 1 + UN * i)
                if u >= 2 or not first:
                    act.wait_ge(u_tr, u - 1 + UN * i)
                nc.scalar.activation(npr[:, u % 2], aux[:, u % 2], ACT.Exp, bias=ns[:, 0, u:u + 1],
                                     accum_out=ns[:, 1, u:u + 1]).then_inc(u_exp, 1)

            def turned(u):
                act.wait_ge(u_tr, u + 1 + UN * i)
                if u >= 2 or not first:
                    act.wait_ge(u_pv, u - 1 + UN * i)
                nc.scalar.activation(npt[:, u % 2], aux[:, 2], ACT.Copy).then_inc(u_pt, 1)

            def take(j, dst, func=ACT.Copy):
                g = na_g(NA_G[j], i)
                nc.scalar.activation(dst, result(act, na_st(j, i), g), func).then_inc(proj_read[g.slot], 1)

            for j in range(NA_STRIPS):
                st, g = na_st(j, i), na_g(NA_G[j], i)
                split_hi(act, st.plus(3))
                if j == 0:
                    res = result(act, st, g)
                    if not first:
                        act.wait_ge(na_vb, 2 * i)
                    for cb in range(NCB):
                        act_in = grid(res, ROWS, BAND_AT[cb], BAND)
                        dst = nvt[:, 2 * cb:2 * cb + 2].rearrange("p b (r c) -> p (b r) c", c=BAND)
                        ins = nc.scalar.activation(dst, act_in, ACT.Copy)
                    ins.then_inc(proj_read[g.slot], 1)
                if j == 1:
                    res = result(act, st, g)
                    if not first:
                        act.wait_ge(u_sc, UN * i)
                        act.wait_ge(na_kms, 2 * i)
                    nc.scalar.activation(nsq[:, 0], res, ACT.Square).then_inc(na_ksq, 1)
                    take(1, nk[:])
                if j == 2:
                    for n in range(2):
                        act.wait_ge(na_vb, n + 1 + 2 * i)
                        chain.link(nc.scalar.activation(vband[:, 4 * n:4 * n + 4].rearrange("p b d -> p (b d)"),
                                                        aux[:, n], ACT.Copy))
                    res = result(act, st, g).rearrange("p (r b q) -> p r b q", b=NCB, q=QC)
                    by_block = [x.rearrange("p (b r q) -> p r b q", b=NCB, q=QC) for x in (nsq[:, 1], nq[:])]
                    nc.scalar.activation(by_block[0], res, ACT.Square).then_inc(na_qsq, 1)
                    nc.scalar.activation(by_block[1], res, ACT.Copy).then_inc(proj_read[g.slot], 1)
                if j == 3:
                    if not first:
                        act.wait_ge(na_ya, i)
                        act.wait_ge(na_yb, i)
                    take(3, nza[:])
                    act.wait_ge(na_kms, 1 + 2 * i)
                    nc.scalar.activation(nsq[:, 0], aux[:, 2], ACT.Sqrt, bias=eps_c[:, 2:3]).then_inc(na_kstd, 1)
                    gq = na_g(4, i)
                    act.wait_ge(na_kms, 2 + 2 * i)
                    nc.scalar.activation(nsq[:, 1], proj[:, gq.slot], ACT.Sqrt,
                                         bias=eps_c[:, 2:3]).then_inc(proj_read[gq.slot], 1)
                if j == 4:
                    take(4, nbg[:])
                if j == 5:
                    take(5, ncg[:])
                if j == 7:
                    take(7, nzb[:])
                if j == 8:
                    act.wait_ge(na_conv_b, 1 + i)
                    take(8, nat[:])
                a = 2 * (j - 6)
                if 6 <= j <= 9:
                    turned(a)
                    turned(a + 1)
                if 5 <= j <= 8:
                    exps(a + 2)
                    exps(a + 3)
                if j == 9:
                    take(9, nsg[:], ACT.Sigmoid)
                if j == 10:
                    nc.scalar.activation(nza[:], nza[:], ACT.Silu).then_inc(na_silu, 1)
                    nc.scalar.activation(nzb[:], nzb[:], ACT.Silu).then_inc(na_silu, 1)
                if j == 11:
                    take(11, chunk(zc, i))

        CONV_STEPS = [8, 8, 8, 7]

        def conv_start(c):
            at = COLS["conf_w"][0]
            if isinstance(c, int):
                return cols[:, at + TAPS * c:at + TAPS * (c + 1)], col("conf_b", c)
            return cols[:, bass.ds(at + TAPS * c, TAPS)], cols[:, bass.ds(COLS["conf_b"][0] + c, 1)]

        def dve_conv(dve, c, part, chain, done):
            dst = chunk(y[:, 2], c)
            if part == 0:
                w, b = conv_start(c)
                chain.link(nc.vector.tensor_copy(wtap[:, :TAPS], w))
                chain.link(nc.vector.tensor_copy(wtap[:, TAPS:TAPS + 1], b))
                dve.wait_ge(na_glu, done)
            t0 = sum(CONV_STEPS[:part])
            for tap in range(t0, t0 + CONV_STEPS[part]):
                src = glu[:, tap:tap + T]
                if tap == 0:
                    ins = nc.vector.tensor_scalar(dst, src, wtap[:, 0:1], wtap[:, TAPS:TAPS + 1], ALU.mult, ALU.add)
                else:
                    ins = nc.vector.scalar_tensor_tensor(dst, src, wtap[:, tap:tap + 1], dst, ALU.mult, ALU.add)
                if tap == TAPS - 1:
                    ins.then_inc(na_conv, 1)
                else:
                    chain.link(ins)

        def dve_na(dve, i, first, chain):
            link = chain.link

            def top(u):
                dve.wait_ge(u_sc, u + 1 + UN * i)
                if u == 0:
                    dve.wait_ge(b_ready, 6 + 6 * i)
                kind = BIAS_KIND[u // 2]
                link(nc.vector.tensor_tensor(aux[:, u % 2, :M], aux[:, u % 2, :M], bias[:, u % 2, kind], ALU.add))
                nc.vector.tensor_reduce(ns[:, 0, u:u + 1], aux[:, u % 2], AX, ALU.max, negate=True).then_inc(u_max, 1)

            def norm(u):
                dve.wait_ge(u_exp, u + 1 + UN * i)
                link(nc.vector.reciprocal(ns[:, 2, u:u + 1], ns[:, 1, u:u + 1]))
                nc.vector.tensor_scalar(npr[:, u % 2], npr[:, u % 2], ns[:, 2, u:u + 1], None,
                                        ALU.mult).then_inc(u_norm, 1)

            for j in range(NA_STRIPS):
                st, g = na_st(j, i), na_g(NA_G[j], i)
                split_lo(dve, st.plus(3))
                if j < 4 and not first:
                    dve_conv(dve, i - 1, j, chain, i)
                if j == 3:
                    dve.wait_ge(na_kstd, 1 + i)
                    link(nc.vector.reciprocal(npr[:, 0], nsq[:, 0]))
                    gk = na_g(1, i)
                    dve.wait_ge(proj_read[gk.slot], gk.turn + 1)
                    nc.vector.scalar_tensor_tensor(nk[:], nk[:], col("kn_g"), npr[:, 0], ALU.mult,
                                                   ALU.mult).then_inc(na_k, 1)
                if j == 4:
                    gs, gq = na_g(4, i), na_g(2, i)
                    dve.wait_ge(proj_read[gs.slot], gs.turn + 1)
                    link(nc.vector.reciprocal(npr[:, 1], nsq[:, 1]))
                    dve.wait_ge(proj_read[gq.slot], gq.turn + 1)
                    nc.vector.scalar_tensor_tensor(nq[:], nq[:], qg8[:], npr[:, 1], ALU.mult,
                                                   ALU.mult).then_inc(na_q, 1)
                if 6 <= j <= 9:
                    norm(2 * (j - 6))
                    norm(2 * (j - 6) + 1)
                if 5 <= j <= 8:
                    top(2 * (j - 5))
                    top(2 * (j - 5) + 1)
                if j == 6:
                    res = result(dve, st, g)
                    gc = na_g(NA_G[5], i)
                    dve.wait_ge(proj_read[gc.slot], gc.turn + 1)
                    if first:
                        dve.wait_ge(b_edge, 2)
                    nc.vector.tensor_tensor(cv[:, 1:T + 1], ncg[:], res, ALU.mult).then_inc(proj_read[g.slot], 1)
                    dve.wait_ge(proj_read[g.slot], g.turn + 1)
                    at = COLS["short_w"][0]
                    w = col("short_w", 3 * i, 3) if first else cols[:, bass.ds(at + 3 * i, 3)]
                    link(nc.vector.tensor_copy(wtap[:, TAPS + 1:TAPS + 4], w))
                    acc = nat[:]
                    link(nc.vector.tensor_scalar(acc, cv[:, 0:T], wtap[:, TAPS + 1:TAPS + 2], None, ALU.mult))
                    for k in (1, 2):
                        link(nc.vector.scalar_tensor_tensor(acc, cv[:, k:k + T], wtap[:, TAPS + 1 + k:TAPS + 2 + k],
                                                            acc, ALU.mult, ALU.add))
                    nc.vector.tensor_tensor(nbg[:], nbg[:], acc, ALU.mult).then_inc(na_conv_b, 1)
                if j == 10:
                    ga, gg = na_g(NA_G[8], i), na_g(NA_G[9], i)
                    dve.wait_ge(proj_read[ga.slot], ga.turn + 1)
                    dve.wait_ge(proj_read[gg.slot], gg.turn + 1)
                    nc.vector.tensor_tensor(glu[:, TAPS // 2:TAPS // 2 + T], nat[:], nsg[:], ALU.mult)\
                        .then_inc(na_glu, 1)
                    dve.wait_ge(na_silu, 2 + 2 * i)
                    dve.wait_ge(na_conv_b, 1 + i)
                    nc.vector.tensor_tensor(chunk(y[:, 1], i), nbg[:], nzb[:], ALU.mult).then_inc(na_yb, 1)
                if j == 11:
                    dve.wait_ge(u_pv, UN + UN * i)
                    dst = chunk(y[:, 0], i).rearrange("p (r b q) -> p r b q", b=NCB, q=QC)
                    src = aux[:, 3].rearrange("p (b r q) -> p r b q", b=NCB, q=QC)
                    nc.vector.tensor_tensor(dst, src, nza[:].rearrange("p (r b q) -> p r b q", b=NCB, q=QC),
                                            ALU.mult).then_inc(na_ya, 1)

        def pool_na(pool, i, first):
            if not first:
                pool.wait_ge(u_max, UN * i)
            src = rpb_in[:, 2 * i:2 * i + 2] if first else rpb_in[:, bass.ds(2 * i, 2)]
            pool.dma_start(btab[:], src).then_inc(b_tab, 16)
            if not first:
                pool.wait_ge(u_pv, UN * i)
            nc.gpsimd.tensor_copy(ck_c[:], chunk(ctxk, i)).then_inc(b_ctx, 1)
            v = ctxv[:, :, P * i:P * (i + 1)] if first else ctxv[:, :, bass.ds(P * i, P)]
            nc.gpsimd.tensor_copy(cv_c[:], v).then_inc(b_ctx, 1)
            pool.wait_ge(b_tab, 16 + 16 * i)
            for hd in range(2):
                for kind in range(3):
                    tab = btab[:, hd].rearrange("p (r m) -> p r m", m=RPB_W)[:, :, BIAS_AT + BIAS_OFF[kind]:
                                                                             BIAS_AT + BIAS_OFF[kind] + BAND]
                    nc.gpsimd.tensor_tensor(bias[:, hd, kind].rearrange("p (r m) -> p r m", m=BAND), tab,
                                            band[:, kind].rearrange("p (r m) -> p r m", m=BAND),
                                            ALU.add).then_inc(b_ready, 1)

        def pe_merge(pe, i, first, fill=None):
            for q in range(RING):
                n = RING * i + q
                for j in range(MERGE_STRIPS):
                    st = Nth(S_MERGE + MERGE_STRIPS * q + j, RING * MERGE_STRIPS, i)
                    g = Nth(G_MERGE + MERGE_GROUPS * q + j, RING * MERGE_GROUPS, i)
                    if j < 3:
                        feature_strip(pe, st, g, a_hi, a_lo)
                        if fill and q == 0:
                            fill[j]()
                        continue
                    pe.wait_ge(lo_ready, st.n + 1)
                    for br in ((0, 1), (2,))[j - 3]:
                        gb = g if j == 3 and br == 0 else g.plus(1)
                        ge(pe, proj_read[gb.slot], gb.turn)
                        if first and q == 0:
                            pe.wait_ge(y_lo_s, KW * (br + 1))
                        for k in range(KW):
                            at = ((br % 2) * KW + k) * P
                            mm = product(proj[:, gb.slot], w_hi[:, st.slot, at:at + P], w_lo[:, st.slot, at:at + P],
                                         y_hi[:, KW * br + k], y_lo[:, KW * br + k], k == 0, k == KW - 1)
                    mm.then_inc(strip_done, 1)

        def act_merge(act, i, first, fill=None):
            for q in range(RING):
                n = RING * i + q
                for j in range(MERGE_STRIPS):
                    st = Nth(S_MERGE + MERGE_STRIPS * q + j, RING * MERGE_STRIPS, i)
                    g = Nth(G_MERGE + MERGE_GROUPS * q + j, RING * MERGE_GROUPS, i)
                    split_hi(act, st.plus(3))
                    if j < 3:
                        if fill and q == 0:
                            fill[j]()
                        if q or not first:
                            act.wait_ge(m_raw, n)
                        nc.scalar.activation(gate[:, j], result(act, st, g), ACT.Sigmoid)\
                            .then_inc(proj_read[g.slot], 1)
                act.wait_ge(m_raw, n + 1)
                nc.scalar.activation(chunk(m_hi, n), mrg[:, 0], ACT.Copy).then_inc(m_hi_s, 1)

        def dve_merge(dve, i, first, chain, fill=None):
            link = chain.link
            for q in range(RING):
                n = RING * i + q
                for j in range(MERGE_STRIPS):
                    st = Nth(S_MERGE + MERGE_STRIPS * q + j, RING * MERGE_STRIPS, i)
                    split_lo(dve, st.plus(3))
                    if fill and q == 0 and j < 3:
                        fill[j]()
                    if j < 3:
                        continue
                    for br in ((0, 1), (2,))[j - 3]:
                        gg = Nth(G_MERGE + MERGE_GROUPS * q + br, RING * MERGE_GROUPS, i)
                        gb = gg.plus(3)
                        dve.wait_ge(proj_read[gg.slot], gg.turn + 1)
                        res = result(dve, st, gb)
                        nc.vector.tensor_tensor(gate[:, br], gate[:, br], res, ALU.mult)\
                            .then_inc(proj_read[gb.slot], 1)
                        dve.wait_ge(proj_read[gb.slot], gb.turn + 1)
                        if br == 1:
                            link(nc.vector.tensor_tensor(mrg[:, 1], gate[:, 0], gate[:, 1], ALU.add))
                        if br == 2:
                            nc.vector.tensor_tensor(mrg[:, 0], mrg[:, 1], gate[:, 2], ALU.add).then_inc(m_raw, 1)
                dve.wait_ge(m_hi_s, n + 1)
                nc.vector.tensor_tensor(chunk(m_lo, n), mrg[:, 0], chunk(m_hi, n).bitcast(F32),
                                        ALU.subtract).then_inc(m_lo_s, 1)

        block = ctx.enter_context(nc.Block())

        @block.sync
        def _(sp):
            def load(s, t, t_int):
                if t_int:
                    sp.wait_ge(lo_ready, RING * t + s - RING + 1)
                src = stream[RING * t + s] if isinstance(t, int) else \
                    stream[bass.ds(RING * t + s, 1)].rearrange("a p n -> (a p) n")
                sp.dma_start(raw[:, s], src).then_inc(raw_in[s], 16)
            for s in range(RING):
                load(s, 0, 0)
            with sp.Fori(1, STRIPS // RING) as t:
                for s in range(RING):
                    load(s, t, 1)

        @block.gpsimd
        def _(pool):
            for dst, value in ((ones_full, 1.0), (mean_d, 1.0 / D), (mean_w, 1.0 / W5), (mean_p, 1.0 / P)):
                nc.gpsimd.memset(dst[:], value).then_inc(const_set, 1)
            for n, value in enumerate((LN_EPS / ALPHA ** 2, LN_EPS, EPS, 0.0)):
                nc.gpsimd.memset(eps_c[:, n:n + 1], value).then_inc(const_set, 1)
            pool.wait_ge(hid_l, KF)
            pool_sum_groups(pool, LN1, G_DOWN1)
            pool.wait_ge(in_cols, 16)
            pool_apply(pool, LN1, HI0[0])
            pool_mix(pool)
            pool.wait_ge(mix_lo, KD)
            pool.dma_start(side[:], mem_in).then_inc(in_mem, 16)
            pool_sum(pool, MEMN, lambda c: pool.wait_ge(in_mem, 16) if c == 0 else None)
            ge(pool, n_mean, LN2.ck)
            nc.gpsimd.memset(zsum, 0.0).then_inc(zsum_step, 1)
            for n in range(KD):
                g = Nth(G_WOUT + 3 * n)
                pool.wait_ge(proj_read[g.slot], g.turn + 1)
                pool.wait_ge(zsum_step, LN2.z0 + 1 + n)
                nc.gpsimd.tensor_tensor(zsum, zsum, h[:, n], ALU.add).then_inc(zsum_step, 1)
                if n == 6:
                    pool_apply(pool, MEMN, HI0[1])
            pool_apply(pool, LN2, HI0[2])
            pool.wait_ge(n_lo, HI0[1] + KD)
            pool.dma_start(side[:], ctx_in).then_inc(in_ctx, 16)
            pool.wait_ge(mod_ready, 2)
            pool_apply(pool, CTXN, HI0[3])
            pool_sum_groups(pool, LN3, G_XO)
            pool_apply(pool, LN3, HI0[4])
            pool.wait_ge(hid_l, 2 * KF)
            pool_sum_groups(pool, LN4, G_DOWN2)
            pool_apply(pool, LN4, 0)
            pool_apply(pool, MODN, HI0[6])
            pool.wait_ge(n_lo, HI0[6] + KD)
            nc.gpsimd.memset(cv[:], 0.0).then_inc(b_edge, 1)
            nc.gpsimd.memset(glu[:], 0.0).then_inc(b_edge, 1)
            pool.dma_start(band[:].rearrange("p k t -> p (k t)"), band_in).then_inc(in_band, 16)
            pool.wait_ge(in_band, 16)
            pool.wait_ge(ck_ready, 1)
            for t in range(MB):
                g = Nth(G_CTXV + t)
                pool.wait_ge(proj_read[g.slot], g.turn + 1)
            pool_na(pool, 0, True)
            with pool.Fori(1, KW) as i:
                pool_na(pool, i, False)
            pool_sum(pool, CONFN, lambda c: pool.wait_ge(na_conv, c + 1))

        @block.scalar
        def _(act):
            chain = Chain(act, act_step)
            act.dma_start(cols[:], cols_in).then_inc(in_cols, 16)
            for n in range(4):
                act.dma_start(h[:, 2 * n:2 * n + 2], x_in[:, 2 * n:2 * n + 2]).then_inc(in_x[n], 16)
            act.dma_start(consts[:].rearrange("p a t -> p (a t)"), const_in).then_inc(in_const, 16)
            split_hi(act, Nth(0))
            for c in range(KD):
                act.wait_ge(in_x[c // 2], 16)
                nc.scalar.activation(a_hi[:, c], h[:, c], ACT.Copy).then_inc(x_hi, 1)
            split_hi(act, Nth(1))
            split_hi(act, Nth(2))
            act.wait_ge(lb_max, 2)
            nc.scalar.activation(lbv[:, 1:3], lbv[:, 1:3], ACT.Exp).then_inc(lb_exp, 1)
            act.wait_ge(in_cols, 16)
            chain.link(nc.scalar.activation(cond_s[:].rearrange("p k t -> p (k t)"), col("cond", 0, 2 * KD), ACT.Silu))
            nc.scalar.activation(cond_hi[:], cond_s[:], ACT.Copy).then_inc(cond_silu, 1)
            act.wait_ge(const_set, 8)
            act_ffn(act, S_FFN1, G_FFN1)
            act_splits(act, S_DOWN1, DOWN_STRIPS * KD)
            act_squares(act, LN1)
            act_only_splits(act, S_ADA, 0, 3)
            act_std(act, LN1)
            act_only_splits(act, S_ADA, 3, 6)
            act_hi(act, LN1)
            act_only_splits(act, S_ADA, 6, 8)
            act_mix(act, chain)
            for n in range(KD):
                act_only_splits(act, S_WOUT, 3 * n, 3 * n + 3)
                if n == 2:
                    act_squares(act, MEMN)
                if n == 4:
                    act_std(act, MEMN)
                if n == 6:
                    act_hi(act, MEMN)
            act_squares(act, LN2)
            act_memkv(act, 0, 3)
            act_std(act, LN2)
            act_memkv(act, 3, 6)
            act_hi(act, LN2)
            act_memkv(act, 6, 16)
            for n in range(KD):
                st, g = Nth(S_XQ + n), Nth(G_XQ + n)
                split_hi(act, st.plus(3))
                nc.scalar.activation(xq[:, n], result(act, st, g), ACT.Copy,
                                     scale=float(2 * P) ** -0.5).then_inc(proj_read[g.slot], 1)
                if n == 1:
                    act_squares(act, CTXN, ready=lambda c: act.wait_ge(in_ctx, 16))
                if n == 3:
                    act_std(act, CTXN)
                if n == 5:
                    act.wait_ge(mod_ready, 2)
                    act_hi(act, CTXN)
            act_ctxk(act)
            act_ctxk_norm(act)
            act_attention(act)
            act_only_splits(act, S_XO, 0, KD)
            act_squares(act, LN3)
            act_only_splits(act, S_CTXV, 0, 2)
            act_std(act, LN3)
            act_only_splits(act, S_CTXV, 2, 4)
            act_ctxv_take(act)
            act_hi(act, LN3)
            act_ffn(act, S_FFN2, G_FFN2)
            act_splits(act, S_DOWN2, DOWN_STRIPS * KD)
            act_squares(act, LN4)
            act_std(act, LN4)
            act_squares(act, MODN, ready=lambda c: act.wait_ge(n_raw, LN4.c0 + c + 1))
            act_std(act, MODN)
            act_hi(act, MODN)
            act_na(act, 0, True, chain)
            with act.Fori(1, KW) as i:
                chain.enter(2, i - 1)
                act_na(act, i, False, chain)
                chain.leave(KW - 1)

            def split_y(b):
                for k in range(KW):
                    if b == 2:
                        act.wait_ge(y_c, k + 1)
                    else:
                        act.wait_ge((na_ya, na_yb)[b], KW)
                    nc.scalar.activation(y_hi[:, KW * b + k], y[:, b, k], ACT.Copy).then_inc(y_hi_s, 1)

            def conf_end():
                act_std(act, CONFN)
                nc.scalar.activation(zc[:], zc[:], ACT.Silu).then_inc(y_silu, 1)
                for c in range(KW):
                    act.wait_ge(n_xn, CONFN.c0 + c + 1)
                    nc.scalar.activation(y[:, 2, c], y[:, 2, c], ACT.Silu, scale=CONFN.gain(c),
                                         bias=CONFN.shift(c)).then_inc(y_silu, 1)
                split_y(2)

            act.wait_ge(u_pv, UN * KW)
            act.wait_ge(na_conv, KW)
            split_y(0)
            split_y(1)
            act_squares(act, CONFN)
            act_merge(act, 0, True, [lambda: None, lambda: None, conf_end])
            with act.Fori(1, KD // RING) as i:
                act_merge(act, i, False)
            for n in range(KD):
                split_hi(act, Nth(S_WO + n + 3))
                g = Nth(G_WO + n)
                act.wait_ge(proj_read[g.slot], g.turn + 1)
                act.dma_start(out[n], h[:, n]).then_inc(out_done, 16)
            act.wait_ge(out_done, 16 * KD)

        @block.vector
        def _(dve):
            chain = Chain(dve, dve_step)
            link = chain.link
            dve.wait_ge(in_cols, 16)
            a, b = col("lb", 0, HH), col("lb", HH, HH)
            link(nc.vector.tensor_tensor(lbv[:, 0], a, b, ALU.max))
            nc.vector.tensor_tensor(lbv[:, 1], a, lbv[:, 0], ALU.subtract).then_inc(lb_max, 1)
            nc.vector.tensor_tensor(lbv[:, 2], b, lbv[:, 0], ALU.subtract).then_inc(lb_max, 1)
            link(nc.vector.tensor_scalar(qg8[:], col("qn_g"), float(HD) ** -0.5, None, ALU.mult))
            split_lo(dve, Nth(0))
            for c in range(KD):
                dve.wait_ge(x_hi, c + 1)
                nc.vector.tensor_tensor(a_lo[:, c], h[:, c], a_hi[:, c].bitcast(F32), ALU.subtract).then_inc(x_lo, 1)
            split_lo(dve, Nth(1))
            split_lo(dve, Nth(2))
            dve.wait_ge(lb_exp, 1)
            link(nc.vector.tensor_tensor(lbv[:, 3], lbv[:, 1], lbv[:, 2], ALU.add))
            link(nc.vector.reciprocal(lbv[:, 6], lbv[:, 3]))
            link(nc.vector.tensor_tensor(lbv[:, 4], lbv[:, 1], lbv[:, 6], ALU.mult))
            link(nc.vector.tensor_scalar(lbv[:, 5], lbv[:, 4], -1.0, 1.0, ALU.mult, ALU.add))
            dve.wait_ge(cond_silu, 1)
            nc.vector.tensor_tensor(cond_lo[:], cond_s[:], cond_hi[:].bitcast(F32), ALU.subtract)\
                .then_inc(cond_split, 1)
            dve_ffn(dve, S_FFN1, G_FFN1, 0)
            dve_residual(dve, S_DOWN1, G_DOWN1, 0.5 / ALPHA, DOWN_STRIPS)
            dve_centre(dve, LN1)
            dve_ada(dve, 0, 3)
            dve.wait_ge(in_const, 16)
            dve_diag(dve, LN1, chain)
            dve_ada(dve, 3, 6)
            dve_normalise(dve, LN1)
            dve_ada(dve, 6, 8)
            dve_mix(dve, chain)
            for n in range(KD):
                st, g = Nth(S_WOUT + 3 * n), Nth(G_WOUT + 3 * n)
                split_lo(dve, st.plus(3))
                nc.vector.scalar_tensor_tensor(h[:, n], result(dve, st, g), 1.0 / ALPHA, h[:, n], ALU.mult,
                                               ALU.add).then_inc(proj_read[g.slot], 1)
                dve_ada(dve, 8 + 2 * n, 10 + 2 * n)
                if n == 1:
                    dve_centre(dve, MEMN)
                if n == 4:
                    dve_diag(dve, MEMN, chain)
                if n == 6:
                    dve_normalise(dve, MEMN)
            dve_centre(dve, LN2)
            dve_only_splits(dve, S_MEMK, 0, 3)
            dve_diag(dve, LN2, chain)
            dve_only_splits(dve, S_MEMK, 3, 6)
            dve_normalise(dve, LN2)
            for which in range(2):
                nc.vector.scalar_tensor_tensor(mod_a[:, which], modv[:, KD:2 * KD, which], 1.0, col("norm_g", 0, KD),
                                               ALU.add, ALU.mult).then_inc(mod_ready, 1)
            dve_only_splits(dve, S_MEMK, 6, 16)
            for n in range(KD):
                split_lo(dve, Nth(S_XQ + n + 3))
                if n == 3:
                    dve_diag(dve, CTXN, chain)
                if n == 5:
                    dve_normalise(dve, CTXN)
            dve_only_splits(dve, S_CTXK, 0, KW)
            dve_ctxk_norm(dve, chain)
            dve_attention(dve, chain)
            dve_residual(dve, S_XO, G_XO, 1.0 / ALPHA)
            dve_centre(dve, LN3)
            dve_only_splits(dve, S_CTXV, 0, 2)
            dve_diag(dve, LN3, chain)
            dve_only_splits(dve, S_CTXV, 2, 4)
            dve_normalise(dve, LN3)
            dve_ffn(dve, S_FFN2, G_FFN2, KF)
            dve_residual(dve, S_DOWN2, G_DOWN2, 0.5 / ALPHA, DOWN_STRIPS)
            dve_centre(dve, LN4)
            dve_diag(dve, LN4, chain)
            dve_normalise(dve, LN4)
            dve_diag(dve, MODN, chain)
            dve_normalise(dve, MODN)
            dve_na(dve, 0, True, chain)
            with dve.Fori(1, KW) as i:
                chain.enter(NA_LINKS, i - 1)
                dve_na(dve, i, False, chain)
                chain.leave(KW - 1)
            for part in range(4):
                dve_conv(dve, KW - 1, part, chain, KW)

            def split_y(b):
                for k in range(KW):
                    dve.wait_ge(y_hi_s, KW * b + k + 1)
                    nc.vector.tensor_tensor(y_lo[:, KW * b + k], y[:, b, k], y_hi[:, KW * b + k].bitcast(F32),
                                            ALU.subtract).then_inc(y_lo_s, 1)

            def conf_end():
                dve_diag(dve, CONFN, chain)
                dve_normalise(dve, CONFN)
                for c in range(KW):
                    dve.wait_ge(y_silu, c + 2)
                    nc.vector.tensor_tensor(y[:, 2, c], y[:, 2, c], zc[:, c], ALU.mult).then_inc(y_c, 1)
                split_y(2)

            dve_centre(dve, CONFN)
            split_y(0)
            split_y(1)
            dve_merge(dve, 0, True, chain, [lambda: None, lambda: None, conf_end])
            with dve.Fori(1, KD // RING) as i:
                chain.enter(RING, i - 1)
                dve_merge(dve, i, False, chain)
                chain.leave(KD // RING - 1)
            for n in range(KD):
                st, g = Nth(S_WO + n), Nth(G_WO + n)
                split_lo(dve, st.plus(3))
                nc.vector.scalar_tensor_tensor(h[:, n], result(dve, st, g), modv[:, 2 * KD + n, 0:1], h[:, n],
                                               ALU.mult, ALU.add).then_inc(proj_read[g.slot], 1)

        @block.tensor
        def _(pe):
            pe.wait_ge(const_set, 8)
            pe_ffn(pe, S_FFN1, G_FFN1, lambda k: pe.wait_ge(x_lo, k + 1))
            pe_down(pe, S_DOWN1, G_DOWN1, 0)
            pe_mean(pe, LN1)
            pe_ada(pe, 0, 3)
            pe_stats(pe, LN1)
            pe_ada(pe, 3, 6)
            pe_spread(pe, LN1)
            pe_ada(pe, 6, 8)
            pe.wait_ge(in_const, 16)
            pe_mix(pe)
            for n in range(KD):
                ready = (lambda k: pe.wait_ge(mix_lo, MIX_ORDER.index(k) + 1)) if n == 0 else None
                feature_strip(pe, Nth(S_WOUT + 3 * n), Nth(G_WOUT + 3 * n), a_hi, a_lo, order=MIX_ORDER, ready=ready)
                pe_ada(pe, 8 + 2 * n, 10 + 2 * n)
                if n == 1:
                    pe_mean(pe, MEMN)
                if n == 3:
                    pe_stats(pe, MEMN)
                if n == 5:
                    pe_spread(pe, MEMN)
            pe_mean(pe, LN2)
            pe_memkv(pe, 0, 3)
            pe_stats(pe, LN2)
            pe_memkv(pe, 3, 6)
            pe_spread(pe, LN2)
            pe_memkv(pe, 6, 16)
            for n in range(KD):
                feature_strip(pe, Nth(S_XQ + n), Nth(G_XQ + n), a_hi, a_lo,
                              ready=lo_ready_of(pe, LN2, HI0[2]) if n == 0 else None)
                if n == 2:
                    pe_stats(pe, CTXN)
                if n == 4:
                    pe_spread(pe, CTXN)
            pe_ctxk(pe)
            pe_ctxk_norm(pe)
            pe_attention(pe)
            pe.wait_ge(a_lo_s, UNITS)
            with pe.Fori(0, KD // RING) as i:
                for q in range(RING):
                    feature_strip(pe, Nth(S_XO + q, RING, i), Nth(G_XO + q, RING, i), a_hi, a_lo)
            pe_mean(pe, LN3)
            pe_ctxv(pe, 0, 2)
            pe_stats(pe, LN3)
            pe_ctxv(pe, 2, 4)
            pe_spread(pe, LN3)
            pe_ffn(pe, S_FFN2, G_FFN2, lo_ready_of(pe, LN3, HI0[4]))
            pe_down(pe, S_DOWN2, G_DOWN2, KF)
            pe_mean(pe, LN4)
            pe_stats(pe, LN4)
            pe_spread(pe, LN4)
            pe_stats(pe, MODN)
            pe_spread(pe, MODN)
            pe_na(pe, 0, True)
            with pe.Fori(1, KW) as i:
                pe_na(pe, i, False)
            pe_merge(pe, 0, True, [lambda: pe_mean(pe, CONFN), lambda: pe_stats(pe, CONFN),
                                   lambda: pe_spread(pe, CONFN)])
            with pe.Fori(1, KD // RING) as i:
                pe_merge(pe, i, False)
            for n in range(KD):
                feature_strip(pe, Nth(S_WO + n), Nth(G_WO + n), m_hi, m_lo,
                              ready=(lambda k: pe.wait_ge(m_lo_s, k + 1)) if n == 0 else None)


def feature_major(w):
    k, n = w.shape
    return w.reshape(k // P, P, n // P, P).transpose(2, 1, 0, 3).reshape(n // P, P, k)


def token_major(w):
    return w.reshape(4, 2, P, W5).transpose(0, 2, 1, 3).reshape(4, P, 2 * W5)


def down_strips(w):
    blocks = feature_major(w)
    return np.pad(blocks, ((0, 0), (0, 0), (0, DOWN_STRIPS * SB * P - F_FF))).reshape(
        KD, P, DOWN_STRIPS, SB * P).transpose(0, 2, 1, 3).reshape(KD * DOWN_STRIPS, P, SB * P)


def vector_cols(v):
    return v.reshape(-1, P).T


def weight_stream(i):
    def ffn(tag):
        gate, up = feature_major(i[tag + "_w_gate"][0]), feature_major(i[tag + "_w_up"][0])
        return [np.stack([gate, up], 1).reshape(2 * KF, P, SB * P), down_strips(i[tag + "_w_down"][0])]

    ada = feature_major(i["w_ada_2"][0])
    w_in = i["w_in"][0]
    q, fz, iv, g, u, v = (w_in[:, n * W5:(n + 1) * W5] for n in range(6))
    parts = ffn("ffn1")
    parts += [ada[:8], feature_major(fz), feature_major(q), token_major(iv), token_major(v), feature_major(u),
              feature_major(g)]
    w_out = feature_major(i["w_out"][0])
    parts += [np.concatenate([w_out[:, None], ada[8:].reshape(KD, 2, P, SB * P)], 1).reshape(3 * KD, P, SB * P)]
    w_v = i["xa_w_v"][0]
    w2 = i["w_in_2"][0]
    part = [w2[:, n * W5:(n + 1) * W5] for n in range(11)]
    parts += [feature_major(i["xa_w_k"][0]), token_major(w_v[:, :W5]), token_major(w_v[:, W5:]),
              feature_major(i["xa_w_q"][0]), feature_major(part[1]), feature_major(i["xa_w_o"][0]),
              token_major(part[2])]
    parts += ffn("ffn2")
    na = [feature_major(part[n]) for n in (2, 1, 0, 3, 4, 5, 6, 7, 8, 9)]
    z = feature_major(part[10])
    zero = np.zeros_like(z[:, :, :4 * P])
    na += [np.concatenate([z[:, :, :4 * P], zero], 2), np.concatenate([z[:, :, 4 * P:], zero], 2)]
    parts += [np.stack(na, 1).reshape(KW * NA_STRIPS, P, SB * P)]
    gates = [feature_major(w2[:, 11 * W5 + n * D:11 * W5 + (n + 1) * D]) for n in range(3)]
    oa, ob, oc = (feature_major(i["w_out_" + n + "_2"][0]) for n in "abc")
    parts += [np.stack(gates + [np.concatenate([oa, ob], 2), np.concatenate([oc, np.zeros_like(oc)], 2)],
                       1).reshape(KD * MERGE_STRIPS, P, SB * P)]
    parts += [feature_major(i["w_o_2"][0])]
    whole = np.concatenate(parts, 0)
    assert whole.shape == (STRIPS, P, SB * P), whole.shape
    return whole


def column_table(i):
    named = {n: vector_cols(i[n]) for n in ("ln1_g", "ln1_b", "ln2_g", "ln2_b", "ln3_g", "ln3_b", "ln4_g", "ln4_b")}
    named["mem_g"], named["mem_b"] = vector_cols(i["mem_ln_g"]), vector_cols(i["mem_ln_b"])
    named["norm_g"] = vector_cols(i["norm_g_2"])
    named["lb"] = i["hg_lb_logits"].reshape(2 * HH, P).T
    named["hg_g"] = vector_cols(i["hg_norm_g"])
    named["b_ada"] = vector_cols(i["b_ada_2"])
    named["cond"] = np.stack([vector_cols(i["c_2"]), vector_cols(i["c_ctx_2"])], 2).reshape(P, 2 * KD)
    named["qn_g"] = np.tile(i["q_norm_g_2"].reshape(HD, 1), (2, 1))
    named["kn_g"] = np.tile(i["k_norm_g_2"].reshape(HD, 1), (2, 1))
    named["short_w"] = i["conv_short_w_2"][0].reshape(3, KW, P).transpose(2, 1, 0).reshape(P, 3 * KW)
    named["conf_w"] = i["conv_conf_w_2"][0].reshape(TAPS, KW, P).transpose(2, 1, 0).reshape(P, TAPS * KW)
    named["conf_b"] = vector_cols(i["conv_conf_b_2"])
    named["lnc_g"], named["lnc_b"] = vector_cols(i["ln_conf_g_2"]), vector_cols(i["ln_conf_b_2"])
    assert all(named[n].shape[1] == COLS[n][1] for n in COLS)
    return np.concatenate([named[n] for n in COLS], 1)


def shape_constants():
    p = np.arange(P)
    consts = np.concatenate([np.eye(P), (p[:, None] // HD == p // HD) / HD], 1).astype(np.float32)
    masks = []
    for lev in range(LEVELS):
        n = 1 << lev
        t = np.concatenate([np.arange(n) + 2 * n * b + n for b in range(P // (2 * n))])
        masks.append((p[:, None] // (2 * n) == t // (2 * n)) & (p[:, None] % (2 * n) < n))
    masks = np.concatenate(masks + [np.eye(P, dtype=bool)], 1).astype(np.int32)
    band = np.zeros((P, 3, ROWS, BAND), np.float32)
    for kind, cb in enumerate((0, 1, 3)):
        qcol = cb * QC + p % QC
        start = np.clip(qcol - 8, 0, GRID - 16)
        rel = BAND_AT[cb] + np.arange(BAND)[None] - start[:, None]
        band[:, kind] = np.where((rel >= 0) & (rel < 16), 0.0, -1e30)[:, None]
    return consts, masks, band.reshape(P, -1)


def bias_windows(rpb):
    pad = np.pad(rpb, ((0, 0), (0, 0), (BAND, BAND)))
    r, q = np.arange(P) // QC, np.arange(P) % QC
    rows = (ROWS - 1 - r)[:, None] + np.arange(ROWS)
    colsx = np.arange(RPB_W)[None] - BIAS_AT + (15 + BAND) - q[:, None]
    return pad[:, rows[:, :, None], colsx[:, None, :]].transpose(1, 0, 2, 3).reshape(P, NH, ROWS * RPB_W)


def token_chunks(a):
    return a.T.reshape(KD, P, -1).transpose(1, 0, 2)


def kernel(**inputs):
    import concourse.bacc as bacc
    from concourse.bass_utils import run_bass_kernel_spmd

    i = {n: np.asarray(a) for n, a in inputs.items()}
    consts, masks, band = shape_constants()
    rows = np.concatenate([i["sg_ln_g"].reshape(-1), i["sg_ln_b"].reshape(-1), i["sg_b_s"].reshape(-1)])
    arrays = {
        "stream": weight_stream(i), "x_in": token_chunks(i["x"][0]), "mem_in": token_chunks(i["mem"][0]),
        "ctx_in": token_chunks(i["ctx_2"][0]), "cols_in": column_table(i), "const_in": consts, "mask_in": masks,
        "rows_in": rows, "wst_in": i["sg_w_s"][0].transpose(2, 0, 1).reshape(P, HH * P), "band_in": band,
        "rpb_in": bias_windows(i["rpb_2"][0]),
    }
    nc = bacc.Bacc("TRN2", target_bir_lowering=False, num_devices=1)
    aps = []
    for name in arrays:
        a = arrays[name] = np.ascontiguousarray(arrays[name])
        aps.append(nc.dram_tensor(name, a.shape, mybir.dt.from_np(a.dtype), kind="ExternalInput").ap())
    out = nc.dram_tensor("out", (KD, P, T), F32, kind="ExternalOutput").ap()
    hybrid_blocks(nc, *aps, out)
    r = run_bass_kernel_spmd(nc, [arrays], core_ids=[0])
    return r.results[0]["out"].reshape(D, T).T.reshape(1, T, D)
```

```python
from contextlib import ExitStack

import concourse.bass as bass
import numpy as np
from concourse import mybir

F32 = mybir.dt.float32
F32R = mybir.dt.float32r
I32 = mybir.dt.int32
ACT = mybir.ActivationFunctionType
ALU = mybir.AluOpType
AX = mybir.AxisListType.X

P = 128
T = 512
D = 1024
KD = D // P
TB = T // P
F_FF = 2816
KF = F_FF // P
M = 256
MB = M // P
HH = 4
W5 = 512
KW = W5 // P
ALPHA = 2.0 ** 0.25
LN_EPS = 1e-5
EPS = 1e-6
XH = 4
NH = 8
HD = 64
ROWS, GRID = 8, 64
QC, BAND = 16, 32
NCB = GRID // QC
BAND_AT = [0, 8, 24, 32]
BIAS_KIND = [0, 1, 1, 2]
BIAS_OFF = [0, -8, -16]
BIAS_AT = 16
RPB_W = BIAS_AT + BAND
TAPS = 31
NA_LINKS = 52
LEVELS = 7
RING = 4
SB = 8

S_FFN1 = 0
S_DOWN1 = S_FFN1 + 2 * KF
DOWN_STRIPS = 3
S_MIX = S_DOWN1 + DOWN_STRIPS * KD
S_WOUT = S_MIX + 24
S_MEMK = S_WOUT + 4 * KD
S_MEMV = S_MEMK + KD
S_XQ = S_MEMV + KD
S_CTXK = S_XQ + KD
S_XO = S_CTXK + KW
S_CTXV = S_XO + KD
S_FFN2 = S_CTXV + KW
S_DOWN2 = S_FFN2 + 2 * KF
S_NA = S_DOWN2 + DOWN_STRIPS * KD
NA_STRIPS = 12
S_MERGE = S_NA + NA_STRIPS * KW
MERGE_STRIPS = 5
S_WO = S_MERGE + MERGE_STRIPS * KD
STRIPS = S_WO + KD
assert STRIPS % RING == 0

G_FFN1 = 0
G_DOWN1 = G_FFN1 + 2 * KF
G_MIX = G_DOWN1 + KD
G_WOUT = G_MIX + 24
WOUT_G = [1, 3, 5, 6, 8, 10, 12, 13]
ADA_G = [0, 2, 4, 7, 9, 11]
G_MEMK = G_WOUT + len(WOUT_G) + len(ADA_G)
G_MEMV = G_MEMK + KD
G_XQ = G_MEMV + 2 * MB
G_CTXK = G_XQ + KD
G_PV = G_CTXK + KW
UNITS = 2 * XH
G_XO = G_PV + UNITS
G_CTXV = G_XO + KD
G_FFN2 = G_CTXV + MB
G_DOWN2 = G_FFN2 + 2 * KF
G_NA = G_DOWN2 + KD
NA_GROUPS = 12
G_MERGE = G_NA + NA_GROUPS * KW
MERGE_GROUPS = 6
G_WO = G_MERGE + MERGE_GROUPS * KD

COLS = {}
for _name, _n in [("ln1_g", KD), ("ln1_b", KD), ("ln2_g", KD), ("ln2_b", KD), ("ln3_g", KD), ("ln3_b", KD),
                  ("ln4_g", KD), ("ln4_b", KD), ("mem_g", KD), ("mem_b", KD), ("norm_g", KD), ("lb", 2 * HH),
                  ("hg_g", 1), ("b_ada", 3 * KD), ("cond", 2 * KD), ("qn_g", 1), ("kn_g", 1),
                  ("short_w", 3 * KW), ("conf_w", TAPS * KW), ("conf_b", KW), ("lnc_g", KW), ("lnc_b", KW)]:
    COLS[_name] = (sum(n for _, n in COLS.values()), _n)
NCOLS = sum(n for _, n in COLS.values())


class Nth:

    def __init__(self, base, per=0, i=0):
        assert per % RING == 0
        self.base, self.per, self.i = base, per, i
        self.slot = base % RING
        self.turn = base // RING + (per // RING) * i if per else base // RING
        self.n = base + per * i if per else base

    def plus(self, k):
        return Nth(self.base + k, self.per, self.i)


def ge(eng, sem, value):
    if not (isinstance(value, int) and value <= 0):
        eng.wait_ge(sem, value)


class Chain:

    def __init__(self, eng, sem):
        self.eng, self.sem, self.n, self.extra = eng, sem, 0, 0

    def link(self, ins):
        ins.then_inc(self.sem, 1)
        self.n += 1
        self.eng.wait_ge(self.sem, self.n + self.extra)

    def enter(self, per, i):
        self.per, self.start, self.extra = per, self.n, per * i

    def leave(self, times):
        assert self.n - self.start == self.per, (self.n, self.start, self.per)
        self.n += self.per * (times - 1)
        self.extra = 0


def hybrid_blocks(nc, stream, x_in, mem_in, ctx_in, cols_in, const_in, mask_in, rows_in, wst_in, band_in, rpb_in,
                  out):
    with ExitStack() as ctx:
        def sem(name):
            return ctx.enter_context(nc.semaphore(name))

        def sb(name, shape, dt=F32, scope=ctx):
            return scope.enter_context(nc.sbuf_tensor(name, shape, dt))

        proj = ctx.enter_context(nc.psum_tensor("proj", [P, RING, T], F32))
        aux = ctx.enter_context(nc.psum_tensor("aux", [P, 4, T], F32))

        raw = sb("raw", [P, RING, SB * P])
        w_hi = sb("w_hi", [P, RING, SB * P], F32R)
        w_lo = sb("w_lo", [P, RING, SB * P], F32R)
        h = sb("h", [P, KD, T])
        a_hi = sb("a_hi", [P, KD, T], F32R)
        a_lo = sb("a_lo", [P, KD, T], F32R)
        cols = sb("cols", [P, NCOLS])
        consts = sb("consts", [P, 2, P])
        ident = consts[:, 0]
        blk64 = consts[:, 1]
        ones_full = sb("ones_full", [P, P])
        mean_d = sb("mean_d", [P, P])
        mean_w = sb("mean_w", [P, P])
        mean_p = sb("mean_p", [P, P])
        eps_c = sb("eps_c", [P, 4])
        cond4 = sb("cond4", [P, KD, 4], F32R)
        pair_sum = sb("pair_sum", [P, 2])
        modv = sb("modv", [P, 3 * KD, 2])
        mod_a = sb("mod_a", [P, 2, KD])
        cond_s = sb("cond_s", [P, KD, 2])
        qg8 = sb("qg8", [P, 1])
        lbv = sb("lbv", [P, 8, HH])
        work = sb("work", [P, 2, T])
        zsum, rstd = work[:, 0], work[:, 1]
        sq = sb("sq", [P, 2, T])
        ctxk = sb("ctxk", [P, KW, M])
        mod_row = ctxk[:, 0:2].rearrange("p c t -> p (c t)")
        ctxv = sb("ctxv", [P, MB, W5])

        def col(name, c=0, n=1):
            at, _ = COLS[name]
            return cols[:, at + c:at + c + n]

        with ExitStack() as ph:
            hid_hi = sb("hid_hi", [P, KF, T], F32R, ph)
            hid_lo = sb("hid_lo", [P, KF, T], F32R, ph)
        with ExitStack() as ph:
            mq, mk, mb, mv, md = (sb(n, [P, HH, T], F32, ph) for n in ("mq", "mk", "mb", "mv", "md"))
            qk = sb("qk", [P, 2, HH, T], F32, ph)
            score = sb("score", [P, TB, HH, P], F32, ph)
            sv, su = (sb(n, [P, HH, T], F32, ph) for n in ("sv", "su"))
            levmask = sb("levmask", [P, LEVELS, P // 2], I32, ph)
            idmask = sb("idmask", [P, P], I32, ph)
            wst = sb("wst", [P, HH, P], F32, ph)
            rows = sb("rows", [P, 3, W5], F32, ph)
            bnst = sb("bnst", [P, 16, 6], F32, ph)
            bnag = sb("bnag", [P, 16, 2], F32, ph)
            vstd = sb("vstd", [P, 2, 16], F32, ph)
            decay = sb("decay", [P, HH, TB], F32, ph)
        with ExitStack() as ph:
            xq = sb("xq", [P, KD, T], F32, ph)
            memk = sb("memk", [P, KD, M], F32, ph)
            memv = sb("memv", [P, MB, D], F32, ph)
            xp = sb("xp", [P, 2, 2, M], F32, ph)
            xpt = sb("xpt", [P, 2, MB, M], F32, ph)
            xs = sb("xs", [P, 3, 8, 2], F32, ph)
            side = sb("side", [P, KD, M], F32, ph)
            side_hi = sb("side_hi", [P, KD, M], F32R, ph)
            side_lo = sb("side_lo", [P, KD, M], F32R, ph)
            ksd = sb("ksd", [P, KW, M], F32, ph)
            krs = sb("krs", [P, KW, M], F32, ph)
        with ExitStack() as ph:
            with ExitStack() as part:
                y = sb("y", [P, 3, KW, T], F32, part)
                zc = sb("zc", [P, KW, T], F32, part)
            with ExitStack() as part:
                hm = sb("hm", [P, KD, T], F32, part)
            m_hi = sb("m_hi", [P, KD, T], F32R, ph)
            m_lo = sb("m_lo", [P, KD, T], F32R, ph)
            with ExitStack() as part:
                nq, nk, nza, nbg, ncg, nat, nsg, nzb = (
                    sb(n, [P, T], F32, part) for n in ("nq", "nk", "nza", "nbg", "ncg", "nat", "nsg", "nzb"))
                nvt = sb("nvt", [P, 2 * NCB, P], F32, part)
                nsq = sb("nsq", [P, 2, T], F32, part)
                vband = sb("vband", [P, 2 * NCB, P], F32, part)
                cv = sb("cv", [P, T + 2], F32, part)
                glu = sb("glu", [P, T + TAPS - 1], F32, part)
                ck_c = sb("ck_c", [P, M], F32, part)
                cv_c = sb("cv_c", [P, MB, P], F32, part)
                btab = sb("btab", [P, 2, ROWS * RPB_W], F32, part)
                bias = sb("bias", [P, 2, 3, ROWS * BAND], F32, part)
                band = sb("band", [P, 3, ROWS * BAND], F32, part)
                npr = sb("npr", [P, 2, T], F32, part)
                npt = sb("npt", [P, 2, T], F32, part)
                ns = sb("ns", [P, 3, 8], F32, part)
                wtap = sb("wtap", [P, TAPS + 4], F32, part)
            with ExitStack() as part:
                y_hi = sb("y_hi", [P, 3 * KW, T], F32R, part)
                y_lo = sb("y_lo", [P, 3 * KW, T], F32R, part)
                gate = sb("gate", [P, 3, T], F32, part)
                mrg = sb("mrg", [P, 2, T], F32, part)

        raw_in = [sem(f"raw_in{s}") for s in range(RING)]
        hi_ready, lo_ready = sem("hi_ready"), sem("lo_ready")
        strip_done = sem("strip_done")
        proj_read = [sem(f"proj_read{b}") for b in range(RING)]
        in_cols, in_const, in_mask, in_mem, in_ctx, in_band = (
            sem(n) for n in ("in_cols", "in_const", "in_mask", "in_mem", "in_ctx", "in_band"))
        in_x = [sem(f"in_x{n}") for n in range(4)]
        const_set = sem("const_set")
        dve_step, act_step, pool_step = sem("dve_step"), sem("act_step"), sem("pool_step")
        x_hi, x_lo = sem("x_hi"), sem("x_lo")
        cond_silu, cond_split = sem("cond_silu"), sem("cond_split")
        hid_h, hid_l = sem("hid_h"), sem("hid_l")
        zsum_step, n_mean, n_cent, n_sq, n_stat, n_std, n_xn, n_hi, n_raw, n_lo = (
            sem(n) for n in ("zsum_step", "n_mean", "n_cent", "n_sq", "n_stat", "n_std", "n_xn",
                             "n_hi", "n_raw", "n_lo"))
        ada_turned, ada_out = sem("ada_turned"), sem("ada_out")
        mod_ready = sem("mod_ready")
        lb_max, lb_exp, lb_ready = sem("lb_max"), sem("lb_exp"), sem("lb_ready")
        m_sig, m_f, m_k, m_lf, m_b, m_fresh, m_zero = (
            sem(n) for n in ("m_sig", "m_f", "m_k", "m_lf", "m_b", "m_fresh", "m_zero"))
        l_diff, l_exp, l_lowk, l_fac, l_mm, l_put = (sem(n) for n in ("l_diff", "l_exp", "l_lowk", "l_fac", "l_mm", "l_put"))
        i_diff, i_expd, i_expb, i_ke, i_qe, i_tr, i_ket, i_kv, i_state, i_o, i_copy, i_osq, i_ms, i_std, i_on = (
            sem(n) for n in ("i_diff", "i_expd", "i_expb", "i_ke", "i_qe", "i_tr", "i_ket", "i_kv", "i_state", "i_o",
                             "i_copy", "i_osq", "i_ms", "i_std", "i_on"))
        v_var, v_std, v_norm, v_gain, v_mm, v_out, w_masked = (
            sem(n) for n in ("v_var", "v_std", "v_norm", "v_gain", "v_mm", "v_out", "w_masked"))
        mix_raw, mix_hi, mix_lo = sem("mix_raw"), sem("mix_hi"), sem("mix_lo")
        a_sc, a_max, a_exp, a_norm, a_tr, a_pt, a_pv, a_hi_s = (
            sem(n) for n in ("a_sc", "a_max", "a_exp", "a_norm", "a_tr", "a_pt", "a_pv", "a_hi_s"))
        ck_sq, ck_ms, ck_std, ck_ready = sem("ck_sq"), sem("ck_ms"), sem("ck_std"), sem("ck_ready")
        b_tab, b_ready, b_ctx, b_edge = sem("b_tab"), sem("b_ready"), sem("b_ctx"), sem("b_edge")
        na_vb, na_ksq, na_kms, na_kstd, na_k, na_qsq, na_q, na_silu, na_ya, na_yb, na_conv, na_glu, na_vband = (
            sem(n) for n in ("na_vb", "na_ksq", "na_kms", "na_kstd", "na_k", "na_qsq", "na_q", "na_silu",
                             "na_ya", "na_yb", "na_conv", "na_glu", "na_vband"))
        u_sc, u_max, u_exp, u_norm, u_tr, u_pt, u_pv = (
            sem(n) for n in ("u_sc", "u_max", "u_exp", "u_norm", "u_tr", "u_pt", "u_pv"))
        y_silu, y_c, y_hi_s, y_lo_s = sem("y_silu"), sem("y_c"), sem("y_hi_s"), sem("y_lo_s")
        m_raw, m_hi_s, m_lo_s, na_conv_b = (sem(n) for n in ("m_raw", "m_hi_s", "m_lo_s", "na_conv_b"))
        out_done = sem("out_done")

        LN_EXP = "natural_log_exp_and_others"

        def inverse_root(chain, dst, src, eps):
            chain.link(nc.scalar.activation(dst, src, ACT.Ln, bias=eps_c[:, eps:eps + 1]))
            return nc.scalar.activation(dst, dst, ACT.Exp, scale=-0.5)

        def result(eng, st, g):
            eng.wait_ge(strip_done, st.n + 1)
            return proj[:, g.slot]

        def split_hi(act, st):
            if isinstance(st.n, int) and st.n >= STRIPS:
                return
            act.wait_ge(raw_in[st.slot], 16 * st.turn + 16)
            ge(act, strip_done, st.n - (RING - 1))
            nc.scalar.activation(w_hi[:, st.slot], raw[:, st.slot], ACT.Copy).then_inc(hi_ready, 1)

        def split_lo(dve, st):
            if isinstance(st.n, int) and st.n >= STRIPS:
                return
            dve.wait_ge(hi_ready, st.n + 1)
            nc.vector.tensor_tensor(w_lo[:, st.slot], raw[:, st.slot], w_hi[:, st.slot].bitcast(F32),
                                    ALU.subtract).then_inc(lo_ready, 1)

        def product(dst, wh, wl, xh, xl, start, stop, moving_weights=False):
            for n, (a, b) in enumerate(((wh, xh), (wh, xl), (wl, xh))):
                if moving_weights:
                    a, b = b, a
                mm = nc.tensor.matmul(dst, a, b, start=start and n == 0, stop=stop and n == 2)
            return mm

        def feature_strip(pe, st, g, xh, xl, first=0, blocks=SB, last=True, order=None, ready=None, n=T, blk0=0):
            pe.wait_ge(lo_ready, st.n + 1)
            if first == 0:
                ge(pe, proj_read[g.slot], g.turn)
            for j, k in enumerate(order or range(blocks)):
                if ready:
                    ready(k)
                at = (blk0 + k) * P
                mm = product(proj[:, g.slot, :n], w_hi[:, st.slot, at:at + P], w_lo[:, st.slot, at:at + P],
                             xh[:, first + k], xl[:, first + k], first == 0 and j == 0, last and j == blocks - 1)
            mm.then_inc(strip_done, 1)

        def token_strip(pe, st, q, groups, xh, xl, ready=None):
            pe.wait_ge(lo_ready, st.n + 1)
            for kk in range(2):
                k = 2 * q + kk
                if ready:
                    ready(k)
                for t, g in enumerate(groups):
                    if k == 0:
                        ge(pe, proj_read[g.slot], g.turn)
                    mm = product(proj[:, g.slot], w_hi[:, st.slot, kk * W5:(kk + 1) * W5],
                                 w_lo[:, st.slot, kk * W5:(kk + 1) * W5], xh[:, k, t * P:(t + 1) * P],
                                 xl[:, k, t * P:(t + 1) * P], k == 0, k == KD - 1, moving_weights=True)
            mm.then_inc(strip_done, 1)

        class Norm:
            def __init__(self, k, ck, n, chunks, src, dst, gain, shift, hi, lo, eps, mean):
                self.k, self.ck, self.n, self.chunks, self.src, self.dst = k, ck, n, chunks, src, dst
                self.gain, self.shift, self.hi, self.lo, self.eps, self.mean = gain, shift, hi, lo, eps, mean
                self.c0 = 8 * k
                self.z0 = 9 * (ck or 0)

        LN1 = Norm(0, 0, T, KD, h, h, lambda c: col("ln1_g", c), lambda c: col("ln1_b", c), a_hi, a_lo, 0, mean_d)
        MEMN = Norm(1, 1, M, KD, side, side, lambda c: col("mem_g", c), lambda c: col("mem_b", c), side_hi, side_lo,
                    1, mean_d)
        LN2 = Norm(2, 2, T, KD, h, h, lambda c: col("ln2_g", c), lambda c: col("ln2_b", c), a_hi, a_lo, 0, mean_d)
        CTXN = Norm(3, None, M, KD, side, side, lambda c: mod_a[:, 1, c:c + 1], lambda c: modv[:, c, 1:2],
                    side_hi, side_lo, 2, mean_d)
        LN3 = Norm(4, 3, T, KD, h, h, lambda c: col("ln3_g", c), lambda c: col("ln3_b", c), a_hi, a_lo, 0, mean_d)
        LN4 = Norm(5, 4, T, KD, h, h, lambda c: col("ln4_g", c), lambda c: col("ln4_b", c), None, None, 0, mean_d)
        MODN = Norm(6, None, T, KD, h, hm, lambda c: mod_a[:, 0, c:c + 1], lambda c: modv[:, c, 0:1], a_hi, a_lo, 2,
                    mean_d)
        CONFN = Norm(7, 5, T, KW, y[:, 2], y[:, 2], lambda c: col("lnc_g", c), lambda c: col("lnc_b", c), None, None,
                     2, mean_w)

        def pe_mean(pe, m):
            pe.wait_ge(zsum_step, m.z0 + 1 + m.chunks)
            nc.tensor.matmul(aux[:, 0, :m.n], m.mean[:], zsum[:, :m.n], start=True, stop=True).then_inc(n_mean, 1)

        def pe_stats(pe, m):
            for c in range(m.chunks):
                pe.wait_ge(n_sq, m.c0 + c + 1)
                nc.tensor.matmul(aux[:, 1, :m.n], m.mean[:], sq[:, c % 2, :m.n], start=(c == 0),
                                 stop=(c == m.chunks - 1)).then_inc(n_stat, 1)

        def dve_centre(dve, m):
            dve.wait_ge(n_mean, m.ck + 1)
            for c in range(m.chunks):
                nc.vector.tensor_tensor(m.src[:, c], m.src[:, c], aux[:, 0, :m.n], ALU.subtract).then_inc(n_cent, 1)

        def act_squares(act, m, ready=None):
            nc.scalar.preload_act_table_set(LN_EXP)
            for c in range(m.chunks):
                if m.ck is None:
                    ready(c)
                else:
                    act.wait_ge(n_cent, 8 * m.ck + c + 1)
                if c >= 2:
                    act.wait_ge(n_stat, m.c0 + c - 1)
                nc.scalar.activation(sq[:, c % 2, :m.n], m.src[:, c], ACT.Square).then_inc(n_sq, 1)

        def act_std(act, m, chain):
            act.wait_ge(n_stat, m.c0 + m.chunks)
            inverse_root(chain, rstd[:, :m.n], aux[:, 1, :m.n], m.eps).then_inc(n_std, 1)

        def dve_normalise(dve, m):
            dve.wait_ge(n_std, m.k + 1)
            for c in range(m.chunks + 2):
                if c < m.chunks:
                    nc.vector.tensor_tensor(m.dst[:, c], m.src[:, c], rstd[:, :m.n], ALU.mult).then_inc(n_xn, 1)
                if c >= 2 and m.lo is not None:
                    dve.wait_ge(n_raw, m.c0 + c - 1)
                    nc.vector.tensor_tensor(m.lo[:, c - 2], m.dst[:, c - 2], m.hi[:, c - 2].bitcast(F32),
                                            ALU.subtract).then_inc(n_lo, 1)

        def act_hi(act, m):
            for c in range(m.chunks):
                act.wait_ge(n_xn, m.c0 + c + 1)
                nc.scalar.activation(m.hi[:, c], m.dst[:, c], ACT.Identity, scale=m.gain(c),
                                     bias=m.shift(c)).then_inc(n_hi, 1)

        def pool_apply(pool, m, h0):
            for c in range(m.chunks):
                if m.hi is not None:
                    pool.wait_ge(n_hi, h0 + c + 1)
                else:
                    pool.wait_ge(n_xn, m.c0 + c + 1)
                nc.gpsimd.tensor_scalar(m.dst[:, c], m.dst[:, c], m.gain(c), m.shift(c), ALU.mult,
                                        ALU.add).then_inc(n_raw, 1)

        def pool_sum(pool, m, ready):
            ge(pool, n_mean, m.ck)
            nc.gpsimd.memset(zsum[:, :m.n], 0.0).then_inc(zsum_step, 1)
            for c in range(m.chunks):
                ready(c)
                pool.wait_ge(zsum_step, m.z0 + 1 + c)
                nc.gpsimd.tensor_tensor(zsum[:, :m.n], zsum[:, :m.n], m.src[:, c], ALU.add).then_inc(zsum_step, 1)

        def pool_sum_groups(pool, m, g0):
            ge(pool, n_mean, m.ck)
            nc.gpsimd.memset(zsum, 0.0).then_inc(zsum_step, 1)
            with pool.Fori(0, KD // RING) as i:
                for q in range(RING):
                    g = Nth(g0 + q, RING, i)
                    pool.wait_ge(proj_read[g.slot], g.turn + 1)
                    pool.wait_ge(zsum_step, m.z0 + 1 + q + RING * i)
                    nc.gpsimd.tensor_tensor(zsum, zsum, h[:, bass.ds(RING * i + q, 1)].rearrange("p a t -> p (a t)"),
                                            ALU.add).then_inc(zsum_step, 1)

        HI0 = {0: 0, 1: 8, 2: 16, 3: 24, 4: 32, 6: 40}

        def lo_ready_of(pe, m, h0):
            return lambda k: pe.wait_ge(n_lo, h0 + k + 1)

        def dve_residual(dve, s0, g0, factor, per_out=1):
            with dve.Fori(0, KD // RING) as i:
                for q in range(RING):
                    for j in range(per_out):
                        st = Nth(s0 + q * per_out + j, RING * per_out, i)
                        split_lo(dve, st.plus(3))
                    g = Nth(g0 + q, RING, i)
                    res = result(dve, st, g)
                    hc = h[:, bass.ds(RING * i + q, 1)].rearrange("p a t -> p (a t)")
                    nc.vector.scalar_tensor_tensor(hc, res, factor, hc, ALU.mult, ALU.add).then_inc(proj_read[g.slot], 1)

        def act_splits(act, s0, n):
            assert n % RING == 0
            with act.Fori(0, n // RING) as i:
                for q in range(RING):
                    split_hi(act, Nth(s0 + 3 + q, RING, i))

        def pe_ffn(pe, s0, g0, ready):
            def two(i, first):
                for j in range(4):
                    feature_strip(pe, Nth(s0 + j, 4, i), Nth(g0 + j, 4, i), a_hi, a_lo,
                                  ready=ready if first and j == 0 else None)
            two(0, True)
            with pe.Fori(1, KF // 2) as i:
                two(i, False)

        def pe_down(pe, s0, g0, hid0):
            pe.wait_ge(hid_l, hid0 + KF)
            with pe.Fori(0, KD // RING) as i:
                for q in range(RING):
                    for j in range(DOWN_STRIPS):
                        feature_strip(pe, Nth(s0 + q * DOWN_STRIPS + j, RING * DOWN_STRIPS, i), Nth(g0 + q, RING, i),
                                      hid_hi, hid_lo, first=SB * j, blocks=min(SB, KF - SB * j),
                                      last=(j == DOWN_STRIPS - 1))

        def act_ffn(act, s0, g0):
            def two(i, first):
                for j in range(4):
                    st, g = Nth(s0 + j, 4, i), Nth(g0 + j, 4, i)
                    split_hi(act, st.plus(3))
                    if j % 2 == 0:
                        res = result(act, st, g)
                        if not first:
                            act.wait_ge(proj_read[g.plus(1).slot], g.plus(1).turn)
                        nc.scalar.activation(sq[:, j // 2], res, ACT.Silu).then_inc(proj_read[g.slot], 1)
                    else:
                        act.wait_ge(proj_read[g.slot], g.turn + 1)
                        hc = hid_hi[:, bass.ds(2 * i + j // 2, 1)].rearrange("p a t -> p (a t)") if not first \
                            else hid_hi[:, j // 2]
                        nc.scalar.activation(hc, work[:, j // 2], ACT.Copy).then_inc(hid_h, 1)
            two(0, True)
            with act.Fori(1, KF // 2) as i:
                two(i, False)

        def dve_ffn(dve, s0, g0, hid0):
            def two(i, first):
                for j in range(4):
                    st, g = Nth(s0 + j, 4, i), Nth(g0 + j, 4, i)
                    split_lo(dve, st.plus(3))
                    if j % 2:
                        gate_g = Nth(g0 + j - 1, 4, i)
                        res = result(dve, st, g)
                        dve.wait_ge(proj_read[gate_g.slot], gate_g.turn + 1)
                        nc.vector.tensor_tensor(work[:, j // 2], sq[:, j // 2], res,
                                                ALU.mult).then_inc(proj_read[g.slot], 1)
                        dve.wait_ge(hid_h, hid0 + j // 2 + 1 + 2 * i)
                        a, b = (x[:, bass.ds(2 * i + j // 2, 1)].rearrange("p a t -> p (a t)") if not first
                                else x[:, j // 2] for x in (hid_lo, hid_hi))
                        nc.vector.tensor_tensor(a, work[:, j // 2], b.bitcast(F32), ALU.subtract).then_inc(hid_l, 1)
            two(0, True)
            with dve.Fori(1, KF // 2) as i:
                two(i, False)

        def wout_at(n):
            return Nth(S_WOUT + 4 * n + 3), Nth(G_WOUT + WOUT_G[n])

        def ada_at(n):
            return Nth(S_WOUT + 4 * (n // 3) + n % 3), Nth(G_WOUT + ADA_G[n // 4])

        def pe_ada(pe, step):
            for n in range(3 * step, 3 * step + 3):
                st, g = ada_at(n)
                pe.wait_ge(lo_ready, st.n + 1)
                if n == 0:
                    pe.wait_ge(cond_split, 1)
                if n % 4 == 0:
                    ge(pe, proj_read[g.slot], g.turn)
                for kk in range(2):
                    k = 2 * (n % 4) + kk
                    for half in (w_hi, w_lo):
                        mm = nc.tensor.matmul(proj[0:4, g.slot], cond4[:, k], half[:, st.slot, kk * W5:(kk + 1) * W5],
                                              start=(k == 0 and half is w_hi), stop=(k == KD - 1 and half is w_lo))
                mm.then_inc(strip_done, 1)

        def pe_ada_turn(pe, a):
            _, g = ada_at(4 * a)
            pe.wait_ge(proj_read[g.slot], g.turn + 1)
            ge(pe, ada_out, a)
            for n in range(4):
                mm = nc.tensor.matmul(aux[:, 3, 2 * n:2 * n + 2], mod_row[0:4, n * P:(n + 1) * P], pair_sum[0:4],
                                      start=True, stop=True)
            mm.then_inc(ada_turned, 1)

        def dve_ada(dve, step):
            for n in range(3 * step, 3 * step + 3):
                st, g = ada_at(n)
                split_lo(dve, st.plus(3))
                if n % 4 == 3:
                    res = result(dve, st, g)
                    ge(dve, ada_turned, n // 4)
                    nc.vector.tensor_copy(mod_row[0:4], res[0:4]).then_inc(proj_read[g.slot], 1)

        def dve_ada_take(dve, a):
            dve.wait_ge(ada_turned, a + 1)
            nc.vector.tensor_tensor(modv[:, 4 * a:4 * a + 4], aux[:, 3, 0:8].rearrange("p (n t) -> p n t", t=2),
                                    col("b_ada", 4 * a, 4).unsqueeze(2).to_broadcast([P, 4, 2]),
                                    ALU.add).then_inc(ada_out, 1)

        def act_only_splits(act, s0, lo, hi):
            for n in range(lo, hi):
                split_hi(act, Nth(s0 + n + 3))

        def dve_only_splits(dve, s0, lo, hi):
            for n in range(lo, hi):
                split_lo(dve, Nth(s0 + n + 3))

        MIX_ORDER = [4, 5, 6, 7, 0, 1, 2, 3]

        def halves(x, lev, free=HH * T):
            n = 1 << lev
            flat = x.rearrange("p h t -> p (h t)")
            v = flat.rearrange("p (b two n) -> p b two n", two=2, n=n)
            return v[:, :, 0, :], v[:, :, 1, :]

        def level_ref(lev):
            n = 1 << lev
            lower, _ = halves(mb[:], lev)
            return lower[:, :, n - 1:n].to_broadcast([P, HH * T // (2 * n), n])

        def pe_level(pe, lev):
            if lev < LEVELS:
                pe.wait_ge(l_fac, lev + 1)
                pe.wait_ge(l_lowk, lev + 1)
            for cc in range(TB):
                for hd in range(HH):
                    if lev < LEVELS:
                        f = qk[:, lev % 2, hd, cc * P:(cc + 1) * P]
                        upper = f.rearrange("p (b two n) -> p b two n", two=2, n=1 << lev)[:, :, 1, :]
                        if cc % 2 == 0 and hd == 0 and lev:
                            pe.wait_ge(l_put, 2 * lev - 1 + cc // 2)
                        mm = nc.tensor.matmul(aux[:, cc // 2, (cc % 2) * 256 + hd * 64:(cc % 2) * 256 + hd * 64 + 64],
                                              f, upper, start=True, stop=True)
                        if cc % 2 and hd == HH - 1:
                            mm.then_inc(l_mm, 1)
                    else:
                        if cc < 2 and hd == 0:
                            pe.wait_ge(l_put, 2 * LEVELS - 1 + cc)
                        at = slice(cc * P, (cc + 1) * P)
                        mm = nc.tensor.matmul(aux[:, cc, hd * P:(hd + 1) * P], mk[:, hd, at], mq[:, hd, at],
                                              start=True, stop=True)
                        if hd == HH - 1:
                            mm.then_inc(l_mm, 1)

        def dve_put(dve, lev):
            if lev == 0:
                dve.wait_ge(m_zero, 1)
                dve.wait_ge(in_mask, 16 * 4)
            if lev < LEVELS:
                nb, n = P >> (lev + 1), 1 << lev
                for half in range(2):
                    dve.wait_ge(l_mm, 2 * lev + half + 1)
                    dst = score[:, 2 * half:2 * half + 2].rearrange("p c h (b two n) -> p (c h) b two n", two=2,
                                                                    n=n)[:, :, :, 1, :]
                    mask = levmask[:, lev].rearrange("p (b n) -> p b n", n=n).unsqueeze(1).to_broadcast(
                        [P, 2 * HH, nb, n])
                    data = aux[:, half].rearrange("p (c b n) -> p c b n", b=nb, n=n)
                    nc.vector.copy_predicated(dst, mask, data).then_inc(l_put, 1)
            else:
                for cc in range(TB):
                    dve.wait_ge(l_mm, 2 * LEVELS + cc + 1)
                    nc.vector.copy_predicated(score[:, cc], idmask[:].unsqueeze(1).to_broadcast([P, HH, P]),
                                              aux[:, cc].rearrange("p (h t) -> p h t", h=HH)).then_inc(l_put, 1)

        def dve_level(dve, lev):
            blo, bup = halves(mb[:], lev)
            dlo, dup = halves(md[:], lev)
            if lev >= 1:
                dve.wait_ge(l_lowk, lev)
                dve.wait_ge(l_fac, lev)
            if lev == 0:
                dve.wait_ge(m_b, HH)
            nc.vector.tensor_tensor(dlo, level_ref(lev), blo, ALU.subtract).then_inc(l_diff, 1)
            nc.vector.tensor_tensor(dup, bup, level_ref(lev), ALU.subtract).then_inc(l_diff, 1)

        def dve_level_mul(dve, lev):
            dve.wait_ge(l_exp, lev + 1)
            if lev >= 2:
                dve.wait_ge(l_mm, 2 * (lev - 1))
            _, dup = halves(md[:], lev)
            _, fup = halves(qk[:, lev % 2], lev)
            _, qup = halves(mq[:], lev)
            nc.vector.tensor_tensor(fup, dup, qup, ALU.mult).then_inc(l_fac, 1)

        def pool_level_mul(pool, lev):
            pool.wait_ge(l_exp, lev + 1)
            if lev == 0:
                pool.wait_ge(m_k, HH)
            if lev >= 2:
                pool.wait_ge(l_mm, 2 * (lev - 1))
            dlo, _ = halves(md[:], lev)
            flo, _ = halves(qk[:, lev % 2], lev)
            klo, _ = halves(mk[:], lev)
            nc.gpsimd.tensor_tensor(flo, dlo, klo, ALU.mult).then_inc(l_lowk, 1)

        def act_level(act, lev):
            act.wait_ge(l_diff, 2 * (lev + 1))
            nc.scalar.activation(md[:], md[:], ACT.Exp).then_inc(l_exp, 1)

        def pe_mix(pe):
            for i in range(24):
                st = Nth(S_MIX + i)
                ready = lo_ready_of(pe, LN1, HI0[0]) if i == 0 else None
                if 8 <= i < 16:
                    g0 = G_MIX + (i // 4) * 4
                    token_strip(pe, st, i % 4, [Nth(g0 + t) for t in range(TB)], a_hi, a_lo)
                else:
                    feature_strip(pe, st, Nth(G_MIX + i), a_hi, a_lo, ready=ready)
                if 7 <= i <= 14:
                    pe_level(pe, i - 7)
                if i == 15:
                    for cc in range(TB - 1):
                        if cc == 0:
                            pe.wait_ge(i_ke, 1)
                            pe.wait_ge(l_put, 2 * LEVELS + TB)
                        for hd in range(HH):
                            mm = nc.tensor.transpose(aux[:, cc, hd * P:(hd + 1) * P],
                                                     qk[:, 1, hd, cc * P:(cc + 1) * P], ident)
                        mm.then_inc(i_tr, 1)
                if i == 16:
                    ket = md[:, 0:3].rearrange("p c (h d) -> p c h d", h=HH)
                    for cc in range(TB - 1):
                        pe.wait_ge(i_ket, 3)
                        for hd in range(HH):
                            mm = nc.tensor.matmul(aux[:, cc, hd * P:(hd + 1) * P], ket[:, cc, hd],
                                                  mv[:, cc, hd * P:(hd + 1) * P], start=True, stop=True)
                        mm.then_inc(i_kv, 1)
                if i == 18:
                    pe.wait_ge(i_qe, 1)
                    pe.wait_ge(i_state, 9)
                    state = mk[:, 0:3].rearrange("p c (h d) -> p c h d", h=HH)
                    for hd in range(HH):
                        for cc in range(TB):
                            o = aux[:, hd, cc * P:(cc + 1) * P]
                            mm = nc.tensor.matmul(o, mv[:, cc, hd * P:(hd + 1) * P], score[:, cc, hd], start=True,
                                                  stop=(cc == 0))
                            if cc:
                                mm = nc.tensor.matmul(o, state[:, cc - 1, hd], qk[:, 0, hd, cc * P:(cc + 1) * P],
                                                      start=False, stop=True)
                        mm.then_inc(i_o, 1)
                if i == 19:
                    for hd in range(HH):
                        pe.wait_ge(i_osq, hd + 1)
                        nc.tensor.matmul(aux[:, hd], mean_p[:], mq[:, hd], start=True, stop=True).then_inc(i_ms, 1)
                if i == 21:
                    pe.wait_ge(v_gain, 2)
                    pe.wait_ge(w_masked, 1)
                    for g in range(HH):
                        pe.wait_ge(i_std, g + 1)
                        for t in range(TB):
                            mm = nc.tensor.matmul(aux[:, g, t * P:(t + 1) * P], sv[:, t, g * P:(g + 1) * P], wst[:, g],
                                                  start=True, stop=True)
                        mm.then_inc(v_mm, 1)

        def act_mix(act, chain):
            for i in range(24):
                st, g = Nth(S_MIX + i), Nth(G_MIX + i)
                split_hi(act, st.plus(3))
                if i < 4:
                    res = result(act, st, g)
                    nc.scalar.activation(md[:, i], res, ACT.Sigmoid).then_inc(m_sig, 1)
                    nc.scalar.activation(mk[:, i], res, ACT.Sigmoid, scale=-1.0).then_inc(proj_read[g.slot], 1)
                if i == 3:
                    act.wait_ge(m_f, HH)
                    nc.scalar.activation(md[:], md[:], ACT.Ln).then_inc(m_lf, 1)
                if 4 <= i < 8:
                    res = result(act, st, g)
                    nc.scalar.activation(mq[:, i - 4], res, ACT.Copy).then_inc(proj_read[g.slot], 1)
                if 6 <= i < 13:
                    act_level(act, i - 6)
                if i == 11:
                    for t in range(TB):
                        gt = Nth(G_MIX + 8 + t)
                        nc.scalar.activation(mv[:, t], result(act, st, gt), ACT.Copy).then_inc(proj_read[gt.slot], 1)
                if i == 13:
                    act.wait_ge(i_diff, 1)
                    nc.scalar.activation(md[:], md[:], ACT.Exp).then_inc(i_expd, 1)
                    nc.scalar.activation(mb[:], mb[:], ACT.Exp).then_inc(i_expb, 1)
                if i == 15:
                    for t in range(TB):
                        gt = Nth(G_MIX + 12 + t)
                        nc.scalar.activation(sv[:, t], result(act, st, gt),
                                             ACT.Gelu_apprx_tanh).then_inc(proj_read[gt.slot], 1)
                if i == 16:
                    for cc in range(TB - 1):
                        act.wait_ge(i_tr, cc + 1)
                        if cc == 0:
                            act.wait_ge(i_ke, 1)
                        nc.scalar.activation(md[:, cc], aux[:, cc], ACT.Copy).then_inc(i_ket, 1)
                if 16 <= i < 20:
                    res = result(act, st, g)
                    nc.scalar.activation(su[:, i - 16], res, ACT.Gelu_apprx_tanh).then_inc(proj_read[g.slot], 1)
                if i == 17:
                    act.wait_ge(v_var, 16)
                    nc.scalar.activation(vstd[:, 0], bnag[:, :, 1], ACT.Sqrt, bias=eps_c[:, 1:2]).then_inc(v_std, 1)
                if i == 19:
                    for hd in range(HH):
                        act.wait_ge(i_o, hd + 1)
                        nc.scalar.activation(mb[:, hd], aux[:, hd], ACT.Copy).then_inc(i_copy, 1)
                        nc.scalar.activation(mq[:, hd], aux[:, hd], ACT.Square).then_inc(i_osq, 1)
                if i == 20:
                    nc.scalar.preload_act_table_set(LN_EXP)
                    for hd in range(HH):
                        act.wait_ge(i_ms, hd + 1)
                        inverse_root(chain, qk[:, 1, hd], aux[:, hd], 1).then_inc(i_std, 1)
                if i >= 20:
                    res = result(act, st, g)
                    nc.scalar.activation(mk[:, i - 20], res, ACT.Silu).then_inc(proj_read[g.slot], 1)
            act.wait_ge(strip_done, S_MIX + 24)
            for n, k in enumerate(MIX_ORDER):
                src = mb[:, k] if k < HH else su[:, k - HH]
                if k < HH:
                    act.wait_ge(mix_raw, k + 1)
                else:
                    act.wait_ge(v_out, 2 * (k - HH + 1))
                nc.scalar.activation(a_hi[:, k], src, ACT.Copy).then_inc(mix_hi, 1)

        def dve_mix(dve, chain):
            link = chain.link
            for i in range(24):
                st, g = Nth(S_MIX + i), Nth(G_MIX + i)
                split_lo(dve, st.plus(3))
                if i < 4:
                    dve.wait_ge(m_sig, i + 1)
                    nc.vector.tensor_scalar(md[:, i], md[:, i], lbv[:, 5, i:i + 1], lbv[:, 4, i:i + 1], ALU.mult,
                                            ALU.add).then_inc(m_f, 1)
                    dve.wait_ge(proj_read[g.slot], g.turn + 1)
                    nc.vector.tensor_scalar(mk[:, i], mk[:, i], lbv[:, 5, i:i + 1], None, ALU.mult).then_inc(m_k, 1)
                if i == 4:
                    dve.wait_ge(m_lf, 1)
                    dve.wait_ge(m_fresh, 2)
                    for hd in range(HH):
                        nc.vector.tensor_tensor_scan(mb[:, hd], work[:, 0], md[:, hd], 0.0, ALU.mult,
                                                     ALU.add).then_inc(m_b, 1)
                if 8 <= i <= 14:
                    dve_put(dve, i - 8)
                if 6 <= i < 13:
                    dve_level(dve, i - 6)
                    if i == 6:
                        gq = Nth(G_MIX + 7)
                        dve.wait_ge(proj_read[gq.slot], gq.turn + 1)
                    dve_level_mul(dve, i - 6)
                if i == 13:
                    dve.wait_ge(l_lowk, LEVELS)
                    dve.wait_ge(l_fac, LEVELS)
                    bh = mb[:].rearrange("p h (c t) -> p (h c) t", c=TB)
                    nc.vector.tensor_tensor(md[:].rearrange("p h (c t) -> p (h c) t", c=TB),
                                            bh[:, :, P - 1:P].to_broadcast([P, HH * TB, P]), bh,
                                            ALU.subtract).then_inc(i_diff, 1)
                    dve.wait_ge(i_expd, 1)
                    dve.wait_ge(l_mm, 2 * 6)
                    nc.vector.tensor_tensor(qk[:, 1], mk[:], md[:], ALU.mult).then_inc(i_ke, 1)
                if i == 14:
                    dve.wait_ge(i_expb, 1)
                    dve.wait_ge(l_mm, 2 * 7)
                    link(nc.vector.tensor_copy(decay[:], mb[:].rearrange("p h (c t) -> p h c t", c=TB)[:, :, :, P - 1]))
                    nc.vector.tensor_tensor(qk[:, 0], mq[:], mb[:], ALU.mult).then_inc(i_qe, 1)
                if i == 15:
                    dve_put(dve, LEVELS)
                if i == 16:
                    for t in range(TB):
                        dve.wait_ge(proj_read[Nth(G_MIX + 12 + t).slot], Nth(G_MIX + 12 + t).turn + 1)
                        for gg in range(HH):
                            last = nc.vector.bn_stats(bnst[:, 4 * t + gg], sv[:, t, gg * P:(gg + 1) * P])
                    link(last)
                    for n in range(16):
                        nc.vector.bn_aggr(bnag[:, n], bnst[:, n]).then_inc(v_var, 1)
                if i == 17:
                    state = mk[:, 0:3].rearrange("p c (h d) -> p c h d", h=HH)
                    for cc in range(TB - 1):
                        dve.wait_ge(i_kv, cc + 1)
                        if cc == 0:
                            nc.vector.tensor_copy(mk[:, 0], aux[:, 0]).then_inc(i_state, 1)
                        else:
                            dve.wait_ge(i_state, 4 * cc - 3)
                            for hd in range(HH):
                                nc.vector.scalar_tensor_tensor(state[:, cc, hd], state[:, cc - 1, hd],
                                                               decay[:, hd, cc:cc + 1],
                                                               aux[:, cc, hd * P:(hd + 1) * P], ALU.mult,
                                                               ALU.add).then_inc(i_state, 1)
                    dve.wait_ge(v_std, 1)
                    link(nc.vector.reciprocal(vstd[:, 1], vstd[:, 0]))
                if i in (18, 19):
                    for t in range(2 * (i - 18), 2 * (i - 18) + 2):
                        for gg in range(HH):
                            n = 4 * t + gg
                            nc.vector.tensor_scalar(sv[:, t, gg * P:(gg + 1) * P], sv[:, t, gg * P:(gg + 1) * P],
                                                    bnag[:, n, 0:1], vstd[:, 1, n:n + 1], ALU.subtract,
                                                    ALU.mult).then_inc(v_norm, 1)
                if i >= 20:
                    hd = i - 20
                    dve.wait_ge(i_std, hd + 1)
                    dve.wait_ge(i_copy, hd + 1)
                    link(nc.vector.scalar_tensor_tensor(mb[:, hd], mb[:, hd], col("hg_g"), qk[:, 1, hd], ALU.mult,
                                                        ALU.mult))
                if i >= 22:
                    for gg in (2 * (i - 22), 2 * (i - 22) + 1):
                        dve.wait_ge(v_mm, gg + 1)
                        gu = Nth(G_MIX + 16 + gg)
                        dve.wait_ge(proj_read[gu.slot], gu.turn + 1)
                        dst = aux[:, gg].rearrange("p (c t) -> p c t", c=TB)
                        nc.vector.tensor_tensor(dst, dst, rows[:, 2, gg * P:(gg + 1) * P].unsqueeze(1).to_broadcast(
                            [P, TB, P]), ALU.add).then_inc(v_out, 1)
                        dve.wait_ge(v_out, 2 * gg + 1)
                        nc.vector.tensor_tensor(su[:, gg], su[:, gg], aux[:, gg], ALU.mult).then_inc(v_out, 1)
            for hd in range(HH):
                gh = Nth(G_MIX + 20 + hd)
                dve.wait_ge(proj_read[gh.slot], gh.turn + 1)
                nc.vector.tensor_tensor(mb[:, hd], mb[:, hd], mk[:, hd], ALU.mult).then_inc(mix_raw, 1)
            for n, k in enumerate(MIX_ORDER):
                src = mb[:, k] if k < HH else su[:, k - HH]
                dve.wait_ge(mix_hi, n + 1)
                nc.vector.tensor_tensor(a_lo[:, k], src, a_hi[:, k].bitcast(F32), ALU.subtract).then_inc(mix_lo, 1)

        def pool_mix(pool):
            pool.wait_ge(hid_l, KF)
            pool.wait_ge(strip_done, S_MIX)
            nc.gpsimd.memset(score[:].rearrange("p c h t -> p (c h t)"), 0.0).then_inc(m_zero, 1)
            pool.wait_ge(n_mean, 1)
            nc.gpsimd.memset(work[:, 0], 1.0).then_inc(m_fresh, 1)
            pool.wait_ge(m_fresh, 1)
            nc.gpsimd.memset(work[:, 0, 0:T:P], 0.0).then_inc(m_fresh, 1)
            for dst, src in ((levmask[:].rearrange("p l t -> p (l t)"), mask_in[:, 0:LEVELS * 64]),
                             (idmask[:], mask_in[:, LEVELS * 64:]),
                             (wst[:].rearrange("p g t -> p (g t)"), wst_in),
                             (rows[:].rearrange("p a t -> p (a t)"), rows_in.partition_broadcast(P))):
                pool.dma_start(dst, src).then_inc(in_mask, 16)
            pool.wait_ge(in_mask, 16 * 4)
            nc.gpsimd.affine_select(out=wst[:], in_=wst[:], compare_op=ALU.is_ge, fill=0.0, base=0,
                                    pattern=[[0, HH], [1, P]], channel_multiplier=-1).then_inc(w_masked, 1)
            for lev in range(LEVELS):
                pool_level_mul(pool, lev)
            for n in range(2):
                pool.wait_ge(v_norm, 16)
                if n:
                    pool.wait_ge(v_gain, 1)
                nc.gpsimd.tensor_tensor(sv[:], sv[:], rows[:, n].unsqueeze(1).to_broadcast([P, TB, W5]),
                                        (ALU.mult, ALU.add)[n]).then_inc(v_gain, 1)

        def pe_memkv(pe, lo, hi):
            for n in range(lo, hi):
                if n < KD:
                    feature_strip(pe, Nth(S_MEMK + n), Nth(G_MEMK + n), side_hi, side_lo, n=M,
                                  ready=lo_ready_of(pe, MEMN, HI0[1]) if n == 0 else None)
                else:
                    half = (n - KD) // 4
                    token_strip(pe, Nth(S_MEMK + n), n % 4, [Nth(G_MEMV + MB * half + t) for t in range(MB)],
                                side_hi, side_lo)

        def act_memkv(act, lo, hi):
            for n in range(lo, hi):
                st = Nth(S_MEMK + n)
                split_hi(act, st.plus(3))
                if n < KD:
                    g = Nth(G_MEMK + n)
                    nc.scalar.activation(memk[:, n], result(act, st, g)[:, :M],
                                         ACT.Copy).then_inc(proj_read[g.slot], 1)
                elif n % 4 == 3:
                    half = (n - KD) // 4
                    for t in range(MB):
                        g = Nth(G_MEMV + MB * half + t)
                        nc.scalar.activation(memv[:, t, half * W5:(half + 1) * W5], result(act, st, g),
                                             ACT.Copy).then_inc(proj_read[g.slot], 1)

        def pe_attention(pe):
            def scores(u):
                hd, pr = u // 2, u % 2
                if u == 0:
                    pe.wait_ge(ck_std, 2)
                if u >= 2:
                    pe.wait_ge(a_exp, 2 * (u - 1))
                if u == 0:
                    for n in range(KD - RING, KD):
                        g = Nth(G_XQ + n)
                        pe.wait_ge(proj_read[g.slot], g.turn + 1)
                for t in range(2):
                    for kk in range(2):
                        at = (2 * pr + t) * P
                        mm = nc.tensor.matmul(aux[:, u % 2, t * M:(t + 1) * M], xq[:, 2 * hd + kk, at:at + P],
                                              memk[:, 2 * hd + kk], start=(kk == 0), stop=(kk == 1))
                mm.then_inc(a_sc, 1)

            def turn(u):
                pe.wait_ge(a_norm, 2 * u + 2)
                if u >= 2:
                    pe.wait_ge(a_pt, u - 1)
                for mt in range(MB):
                    for t in range(2):
                        mm = nc.tensor.transpose(aux[:, 2 + u % 2, (2 * mt + t) * P:(2 * mt + t + 1) * P],
                                                 xp[:, u % 2, t, mt * P:(mt + 1) * P], ident)
                mm.then_inc(a_tr, 1)

            def values(u):
                pe.wait_ge(a_pt, u + 1)
                g = Nth(G_PV + u)
                ge(pe, proj_read[g.slot], g.turn)
                for dk in range(2):
                    for mt in range(MB):
                        at = (2 * (u // 2) + dk) * P
                        mm = nc.tensor.matmul(proj[:, g.slot, dk * M:(dk + 1) * M], memv[:, mt, at:at + P],
                                              xpt[:, u % 2, mt], start=(mt == 0), stop=(mt == MB - 1))
                mm.then_inc(a_pv, 1)

            scores(0)
            scores(1)
            for u in range(UNITS + 1):
                if u < UNITS:
                    turn(u)
                    if u + 2 < UNITS:
                        scores(u + 2)
                if u:
                    values(u - 1)

        def dve_attention(dve, chain):
            def top(u):
                dve.wait_ge(a_sc, u + 1)
                nc.vector.tensor_reduce(xs[:, 0, u], aux[:, u % 2].rearrange("p (t m) -> p t m", t=2), AX, ALU.max,
                                        negate=True).then_inc(a_max, 1)

            def norm(u):
                dve.wait_ge(a_exp, 2 * u + 2)
                chain.link(nc.vector.reciprocal(xs[:, 2, u], xs[:, 1, u]))
                for t in range(2):
                    nc.vector.tensor_scalar(xp[:, u % 2, t], xp[:, u % 2, t], xs[:, 2, u, t:t + 1], None,
                                            ALU.mult).then_inc(a_norm, 1)

            def take(u):
                dve.wait_ge(a_hi_s, u + 1)
                hd, pr = u // 2, u % 2
                dst = (x[:, 2 * hd:2 * hd + 2, pr * M:(pr + 1) * M] for x in (a_lo, a_hi))
                lo, hi = dst
                g = Nth(G_PV + u)
                nc.vector.tensor_tensor(lo, proj[:, g.slot].rearrange("p (d t) -> p d t", d=2), hi.bitcast(F32),
                                        ALU.subtract).then_inc(proj_read[g.slot], 1)

            top(0)
            for u in range(UNITS):
                if u + 1 < UNITS:
                    top(u + 1)
                norm(u)
                if u >= 2:
                    take(u - 2)
            take(UNITS - 2)
            take(UNITS - 1)

        def act_attention(act):
            def exps(u):
                act.wait_ge(a_max, u + 1)
                if u >= 2:
                    act.wait_ge(a_tr, u - 1)
                for t in range(2):
                    nc.scalar.activation(xp[:, u % 2, t], aux[:, u % 2, t * M:(t + 1) * M], ACT.Exp,
                                         bias=xs[:, 0, u, t:t + 1],
                                         accum_out=xs[:, 1, u, t:t + 1]).then_inc(a_exp, 1)

            def turned(u):
                act.wait_ge(a_tr, u + 1)
                if u >= 2:
                    act.wait_ge(a_pv, u - 1)
                nc.scalar.activation(xpt[:, u % 2].rearrange("p m t -> p (m t)"), aux[:, 2 + u % 2],
                                     ACT.Copy).then_inc(a_pt, 1)

            def take(u):
                act.wait_ge(a_pv, u + 1)
                hd, pr = u // 2, u % 2
                nc.scalar.activation(a_hi[:, 2 * hd:2 * hd + 2, pr * M:(pr + 1) * M],
                                     proj[:, Nth(G_PV + u).slot].rearrange("p (d t) -> p d t", d=2),
                                     ACT.Copy).then_inc(a_hi_s, 1)

            exps(0)
            for u in range(UNITS):
                if u + 1 < UNITS:
                    exps(u + 1)
                turned(u)
                if u >= 2:
                    take(u - 2)
            take(UNITS - 2)
            take(UNITS - 1)

        def pe_ctxk(pe):
            for n in range(KW):
                feature_strip(pe, Nth(S_CTXK + n), Nth(G_CTXK + n), side_hi, side_lo, n=M,
                              ready=lo_ready_of(pe, CTXN, HI0[3]) if n == 0 else None)

        def act_ctxk(act):
            for n in range(KW):
                st, g = Nth(S_CTXK + n), Nth(G_CTXK + n)
                split_hi(act, st.plus(3))
                nc.scalar.activation(ksd[:, n], result(act, st, g)[:, :M], ACT.Square).then_inc(ck_sq, 1)
                nc.scalar.activation(ctxk[:, n], result(act, st, g)[:, :M], ACT.Copy).then_inc(proj_read[g.slot], 1)

        def pe_ctxk_norm(pe):
            pe.wait_ge(ck_sq, KW)
            for n in range(2):
                nc.tensor.matmul(aux[:, n], blk64, ksd[:, 2 * n:2 * n + 2].rearrange("p c t -> p (c t)"), start=True,
                                 stop=True).then_inc(ck_ms, 1)

        def act_ctxk_norm(act, chain):
            nc.scalar.preload_act_table_set(LN_EXP)
            for n in range(2):
                act.wait_ge(ck_ms, n + 1)
                inverse_root(chain, krs[:, 2 * n:2 * n + 2].rearrange("p c t -> p (c t)"), aux[:, n],
                             2).then_inc(ck_std, 1)

        def dve_ctxk_norm(dve):
            dve.wait_ge(ck_std, 2)
            dve.wait_ge(proj_read[Nth(G_CTXK + 3).slot], Nth(G_CTXK + 3).turn + 1)
            flat = [x[:].rearrange("p c t -> p (c t)") for x in (ctxk, krs)]
            nc.vector.scalar_tensor_tensor(flat[0], flat[0], col("kn_g"), flat[1], ALU.mult,
                                           ALU.mult).then_inc(ck_ready, 1)

        def pe_ctxv(pe, lo, hi):
            for n in range(lo, hi):
                token_strip(pe, Nth(S_CTXV + n), n, [Nth(G_CTXV + t) for t in range(MB)], side_hi, side_lo)

        def act_ctxv_take(act):
            for t in range(MB):
                g = Nth(G_CTXV + t)
                nc.scalar.activation(ctxv[:, t], result(act, Nth(S_CTXV + 3), g),
                                     ACT.Copy).then_inc(proj_read[g.slot], 1)

        NA_G = [0, 1, 2, 4, 5, 6, 7, 8, 9, 10, 11, 11]
        Q_MS = 3
        UN = 2 * NCB

        def na_st(j, i):
            return Nth(S_NA + j, NA_STRIPS, i)

        def na_g(j, i):
            return Nth(G_NA + j, NA_GROUPS, i)

        def grid(x, rows, at, n, r0=0):
            return x.rearrange("p (r c) -> p r c", c=GRID)[:, r0:r0 + rows, at:at + n]

        def pe_na(pe, i, first):
            def scores(u):
                cb, lo = u // 2, HD * (u % 2)
                part = slice(lo, lo + HD)
                if u == 0:
                    pe.wait_ge(na_k, 1 + i)
                    pe.wait_ge(na_q, 1 + i)
                    pe.wait_ge(na_vband, 2 + 2 * i)
                    pe.wait_ge(b_ctx, 2 + 2 * i)
                if u >= 2:
                    pe.wait_ge(u_exp, u - 1 + UN * i)
                q = nq[part, cb * P:(cb + 1) * P]
                nc.tensor.matmul(aux[:, u % 2, :M], q, grid(nk[part], ROWS, BAND_AT[cb], BAND), start=True, stop=True)
                nc.tensor.matmul(aux[:, u % 2, M:], q, ck_c[part], start=True, stop=True).then_inc(u_sc, 1)

            def turn(u):
                pe.wait_ge(u_norm, u + 1 + UN * i)
                if u or not first:
                    pe.wait_ge(u_pt, u + UN * i)
                for b in range(4):
                    mm = nc.tensor.transpose(aux[:, 2, b * P:(b + 1) * P], npr[:, u % 2, b * P:(b + 1) * P], ident)
                mm.then_inc(u_tr, 1)

            def values(u):
                cb, lo = u // 2, HD * (u % 2)
                pe.wait_ge(u_pt, u + 1 + UN * i)
                if u == 0 and not first:
                    pe.wait_ge(na_ya, i)
                for b in range(4):
                    v = vband[:, 2 * cb + b, lo:lo + HD] if b < 2 else cv_c[:, b - 2, lo:lo + HD]
                    mm = nc.tensor.matmul(aux[lo:lo + HD, 3, cb * P:(cb + 1) * P], v, npt[:, u % 2, b * P:(b + 1) * P],
                                          start=(b == 0), stop=(b == 3))
                mm.then_inc(u_pv, 1)

            for j in range(NA_STRIPS):
                st, g = na_st(j, i), na_g(NA_G[j], i)
                ready = lo_ready_of(pe, MODN, HI0[6]) if first and j == 0 else None
                if j < 10:
                    feature_strip(pe, st, g, a_hi, a_lo, ready=ready)
                else:
                    feature_strip(pe, st, g, a_hi, a_lo, first=4 * (j - 10), blocks=4, last=(j == 11))
                if j == 1:
                    pe.wait_ge(na_ksq, 1 + i)
                    nc.tensor.matmul(aux[:, 2], blk64, nsq[:, 0], start=True, stop=True).then_inc(na_kms, 1)
                if j == 2:
                    gq = na_g(Q_MS, i)
                    pe.wait_ge(na_qsq, 1 + i)
                    pe.wait_ge(proj_read[gq.slot], gq.turn)
                    nc.tensor.matmul(proj[:, gq.slot], blk64, nsq[:, 1], start=True, stop=True).then_inc(na_kms, 1)
                if j == 3:
                    pe.wait_ge(proj_read[na_g(2, i).slot], na_g(2, i).turn + 1)
                    for n in range(2 * NCB):
                        mm = nc.tensor.transpose(aux[:, n // 4, (n % 4) * P:(n % 4 + 1) * P],
                                                 nvt[:, n], ident)
                        if n % 4 == 3:
                            mm.then_inc(na_vb, 1)
                a = 2 * (j - 5)
                if 5 <= j <= 8:
                    turn(a)
                if 6 <= j <= 9:
                    values(a - 2)
                    values(a - 1)
                if 5 <= j <= 8:
                    turn(a + 1)
                if 4 <= j <= 7:
                    scores(a + 2)
                    scores(a + 3)

        def chunk(x, i):
            return x[:, i] if isinstance(i, int) else x[:, bass.ds(i, 1)].rearrange("p a t -> p (a t)")

        def act_na(act, i, first, chain):
            def exps(u):
                act.wait_ge(u_max, u + 1 + UN * i)
                if u >= 2 or not first:
                    act.wait_ge(u_tr, u - 1 + UN * i)
                nc.scalar.activation(npr[:, u % 2], aux[:, u % 2], ACT.Exp, bias=ns[:, 0, u:u + 1],
                                     accum_out=ns[:, 1, u:u + 1]).then_inc(u_exp, 1)

            def turned(u):
                act.wait_ge(u_tr, u + 1 + UN * i)
                if u >= 2 or not first:
                    act.wait_ge(u_pv, u - 1 + UN * i)
                nc.scalar.activation(npt[:, u % 2], aux[:, 2], ACT.Copy).then_inc(u_pt, 1)

            def take(j, dst, func=ACT.Copy):
                g = na_g(NA_G[j], i)
                nc.scalar.activation(dst, result(act, na_st(j, i), g), func).then_inc(proj_read[g.slot], 1)

            for j in range(NA_STRIPS):
                st, g = na_st(j, i), na_g(NA_G[j], i)
                split_hi(act, st.plus(3))
                if j == 0:
                    res = result(act, st, g)
                    if not first:
                        act.wait_ge(u_sc, UN * i)
                        act.wait_ge(na_kms, 2 * i)
                    nc.scalar.activation(nsq[:, 0], res, ACT.Square).then_inc(na_ksq, 1)
                    take(0, nk[:])
                if j == 1:
                    res = result(act, st, g).rearrange("p (r b q) -> p r b q", b=NCB, q=QC)
                    by_block = [x.rearrange("p (b r q) -> p r b q", b=NCB, q=QC) for x in (nsq[:, 1], nq[:])]
                    nc.scalar.activation(by_block[0], res, ACT.Square).then_inc(na_qsq, 1)
                    nc.scalar.activation(by_block[1], res, ACT.Copy).then_inc(proj_read[g.slot], 1)
                if j == 2:
                    nc.scalar.preload_act_table_set(LN_EXP)
                    act.wait_ge(na_kms, 1 + 2 * i)
                    inverse_root(chain, nsq[:, 0], aux[:, 2], 2).then_inc(na_kstd, 1)
                    res = result(act, st, g)
                    if not first:
                        act.wait_ge(na_vb, 2 * i)
                    for cb in range(NCB):
                        dst = nvt[:, 2 * cb:2 * cb + 2].rearrange("p b (r c) -> p (b r) c", c=BAND)
                        ins = nc.scalar.activation(dst, grid(res, ROWS, BAND_AT[cb], BAND), ACT.Copy)
                    ins.then_inc(proj_read[g.slot], 1)
                if j == 3:
                    if not first:
                        act.wait_ge(na_conv_b, i)
                    take(3, nat[:])
                    gq = na_g(Q_MS, i)
                    act.wait_ge(na_kms, 2 + 2 * i)
                    inverse_root(chain, nsq[:, 1], proj[:, gq.slot], 2).then_inc(proj_read[gq.slot], 1)
                    for n in range(2):
                        act.wait_ge(na_vb, n + 1 + 2 * i)
                        nc.scalar.activation(vband[:, 4 * n:4 * n + 4].rearrange("p b d -> p (b d)"),
                                             aux[:, n], ACT.Copy).then_inc(na_vband, 1)
                if j == 4:
                    take(4, nsg[:], ACT.Sigmoid)
                    nc.scalar.preload_act_table_set(LN_EXP)
                if j == 5:
                    if not first:
                        act.wait_ge(na_ya, i)
                        act.wait_ge(na_yb, i)
                    take(5, nza[:])
                if j == 6:
                    take(6, nbg[:])
                if j == 7:
                    take(7, ncg[:])
                if j == 9:
                    take(9, nzb[:])
                a = 2 * (j - 5)
                if 5 <= j <= 8:
                    turned(a)
                    turned(a + 1)
                if 4 <= j <= 7:
                    exps(a + 2)
                    exps(a + 3)
                if j == 10:
                    for z in (5, 9):
                        gz = na_g(NA_G[z], i)
                        act.wait_ge(proj_read[gz.slot], gz.turn + 1)
                    nc.scalar.activation(nza[:], nza[:], ACT.Silu).then_inc(na_silu, 1)
                    nc.scalar.activation(nzb[:], nzb[:], ACT.Silu).then_inc(na_silu, 1)
                if j == 11:
                    take(11, chunk(zc, i))

        CONV_TAPS = {5: 4, 6: 5, 7: 5, 8: 2, 9: 5, 10: 5, 11: 5}

        def conv_start(c):
            at = COLS["conf_w"][0]
            if isinstance(c, int):
                return cols[:, at + TAPS * c:at + TAPS * (c + 1)], col("conf_b", c)
            return cols[:, bass.ds(at + TAPS * c, TAPS)], cols[:, bass.ds(COLS["conf_b"][0] + c, 1)]

        def dve_conv(dve, c, step, chain):
            dst = chunk(y[:, 2], c)
            if step == min(CONV_TAPS):
                w, b = conv_start(c)
                chain.link(nc.vector.tensor_copy(wtap[:, :TAPS], w))
                chain.link(nc.vector.tensor_copy(wtap[:, TAPS:TAPS + 1], b))
                dve.wait_ge(na_glu, c + 1)
            t0 = sum(n for s, n in CONV_TAPS.items() if s < step)
            for tap in range(t0, t0 + CONV_TAPS[step]):
                src = glu[:, tap:tap + T]
                if tap == 0:
                    ins = nc.vector.tensor_scalar(dst, src, wtap[:, 0:1], wtap[:, TAPS:TAPS + 1], ALU.mult, ALU.add)
                else:
                    ins = nc.vector.scalar_tensor_tensor(dst, src, wtap[:, tap:tap + 1], dst, ALU.mult, ALU.add)
                if tap == TAPS - 1:
                    ins.then_inc(na_conv, 1)
                else:
                    chain.link(ins)

        def dve_na(dve, i, first, chain):
            link = chain.link

            def top(u):
                dve.wait_ge(u_sc, u + 1 + UN * i)
                if u == 0:
                    dve.wait_ge(b_ready, 6 + 6 * i)
                kind = BIAS_KIND[u // 2]
                link(nc.vector.tensor_tensor(aux[:, u % 2, :M], aux[:, u % 2, :M], bias[:, u % 2, kind], ALU.add))
                nc.vector.tensor_reduce(ns[:, 0, u:u + 1], aux[:, u % 2], AX, ALU.max, negate=True).then_inc(u_max, 1)

            def norm(u):
                dve.wait_ge(u_exp, u + 1 + UN * i)
                link(nc.vector.reciprocal(ns[:, 2, u:u + 1], ns[:, 1, u:u + 1]))
                nc.vector.tensor_scalar(npr[:, u % 2], npr[:, u % 2], ns[:, 2, u:u + 1], None,
                                        ALU.mult).then_inc(u_norm, 1)

            for j in range(NA_STRIPS):
                st, g = na_st(j, i), na_g(NA_G[j], i)
                split_lo(dve, st.plus(3))
                if j == 2:
                    dve.wait_ge(na_kstd, 1 + i)
                    gk = na_g(0, i)
                    dve.wait_ge(proj_read[gk.slot], gk.turn + 1)
                    nc.vector.scalar_tensor_tensor(nk[:], nk[:], col("kn_g"), nsq[:, 0], ALU.mult,
                                                   ALU.mult).then_inc(na_k, 1)
                if j == 3:
                    gs, gq = na_g(Q_MS, i), na_g(1, i)
                    dve.wait_ge(proj_read[gs.slot], gs.turn + 1)
                    dve.wait_ge(proj_read[gq.slot], gq.turn + 1)
                    nc.vector.scalar_tensor_tensor(nq[:], nq[:], qg8[:], nsq[:, 1], ALU.mult,
                                                   ALU.mult).then_inc(na_q, 1)
                if 5 <= j <= 8:
                    norm(2 * (j - 5))
                    norm(2 * (j - 5) + 1)
                if j == 5:
                    ga, gg = na_g(NA_G[3], i), na_g(NA_G[4], i)
                    dve.wait_ge(proj_read[ga.slot], ga.turn + 1)
                    dve.wait_ge(proj_read[gg.slot], gg.turn + 1)
                    if first:
                        dve.wait_ge(b_edge, 2)
                    else:
                        dve.wait_ge(na_conv, i)
                    nc.vector.tensor_tensor(glu[:, TAPS // 2:TAPS // 2 + T], nat[:], nsg[:], ALU.mult)\
                        .then_inc(na_glu, 1)
                if j in CONV_TAPS:
                    dve_conv(dve, i, j, chain)
                if 4 <= j <= 7:
                    top(2 * (j - 4))
                    top(2 * (j - 4) + 1)
                if j == 8:
                    res = result(dve, st, g)
                    gc = na_g(NA_G[7], i)
                    dve.wait_ge(proj_read[gc.slot], gc.turn + 1)
                    nc.vector.tensor_tensor(cv[:, 1:T + 1], ncg[:], res, ALU.mult).then_inc(proj_read[g.slot], 1)
                    dve.wait_ge(proj_read[g.slot], g.turn + 1)
                    at = COLS["short_w"][0]
                    w = col("short_w", 3 * i, 3) if first else cols[:, bass.ds(at + 3 * i, 3)]
                    link(nc.vector.tensor_copy(wtap[:, TAPS + 1:TAPS + 4], w))
                    acc = nat[:]
                    link(nc.vector.tensor_scalar(acc, cv[:, 0:T], wtap[:, TAPS + 1:TAPS + 2], None, ALU.mult))
                    for k in (1, 2):
                        link(nc.vector.scalar_tensor_tensor(acc, cv[:, k:k + T], wtap[:, TAPS + 1 + k:TAPS + 2 + k],
                                                            acc, ALU.mult, ALU.add))
                    nc.vector.tensor_tensor(nbg[:], nbg[:], acc, ALU.mult).then_inc(na_conv_b, 1)
                if j == 10:
                    dve.wait_ge(na_silu, 2 + 2 * i)
                    dve.wait_ge(na_conv_b, 1 + i)
                    nc.vector.tensor_tensor(chunk(y[:, 1], i), nbg[:], nzb[:], ALU.mult).then_inc(na_yb, 1)
                if j == 11:
                    dve.wait_ge(u_pv, UN + UN * i)
                    dst = chunk(y[:, 0], i).rearrange("p (r b q) -> p r b q", b=NCB, q=QC)
                    src = aux[:, 3].rearrange("p (b r q) -> p r b q", b=NCB, q=QC)
                    nc.vector.tensor_tensor(dst, src, nza[:].rearrange("p (r b q) -> p r b q", b=NCB, q=QC),
                                            ALU.mult).then_inc(na_ya, 1)

        def pool_na(pool, i, first):
            if not first:
                pool.wait_ge(u_max, UN * i)
            src = rpb_in[:, 2 * i:2 * i + 2] if first else rpb_in[:, bass.ds(2 * i, 2)]
            pool.dma_start(btab[:], src).then_inc(b_tab, 16)
            if not first:
                pool.wait_ge(u_pv, UN * i)
            nc.gpsimd.tensor_copy(ck_c[:], chunk(ctxk, i)).then_inc(b_ctx, 1)
            v = ctxv[:, :, P * i:P * (i + 1)] if first else ctxv[:, :, bass.ds(P * i, P)]
            nc.gpsimd.tensor_copy(cv_c[:], v).then_inc(b_ctx, 1)
            pool.wait_ge(b_tab, 16 + 16 * i)
            for hd in range(2):
                for kind in range(3):
                    tab = btab[:, hd].rearrange("p (r m) -> p r m", m=RPB_W)[:, :, BIAS_AT + BIAS_OFF[kind]:
                                                                             BIAS_AT + BIAS_OFF[kind] + BAND]
                    nc.gpsimd.tensor_tensor(bias[:, hd, kind].rearrange("p (r m) -> p r m", m=BAND), tab,
                                            band[:, kind].rearrange("p (r m) -> p r m", m=BAND),
                                            ALU.add).then_inc(b_ready, 1)

        def pe_merge(pe, i, first, fill=None):
            for q in range(RING):
                n = RING * i + q
                for j in range(MERGE_STRIPS):
                    st = Nth(S_MERGE + MERGE_STRIPS * q + j, RING * MERGE_STRIPS, i)
                    g = Nth(G_MERGE + MERGE_GROUPS * q + j, RING * MERGE_GROUPS, i)
                    if j < 3:
                        feature_strip(pe, st, g, a_hi, a_lo)
                        if fill and q == 0:
                            fill[j]()
                        continue
                    pe.wait_ge(lo_ready, st.n + 1)
                    for br in ((0, 1), (2,))[j - 3]:
                        gb = g if j == 3 and br == 0 else g.plus(1)
                        ge(pe, proj_read[gb.slot], gb.turn)
                        if first and q == 0:
                            pe.wait_ge(y_lo_s, KW * (br + 1))
                        for k in range(KW):
                            at = ((br % 2) * KW + k) * P
                            mm = product(proj[:, gb.slot], w_hi[:, st.slot, at:at + P], w_lo[:, st.slot, at:at + P],
                                         y_hi[:, KW * br + k], y_lo[:, KW * br + k], k == 0, k == KW - 1)
                    mm.then_inc(strip_done, 1)

        def act_merge(act, i, first, fill=None):
            for q in range(RING):
                n = RING * i + q
                for j in range(MERGE_STRIPS):
                    st = Nth(S_MERGE + MERGE_STRIPS * q + j, RING * MERGE_STRIPS, i)
                    g = Nth(G_MERGE + MERGE_GROUPS * q + j, RING * MERGE_GROUPS, i)
                    split_hi(act, st.plus(3))
                    if j < 3:
                        if fill and q == 0:
                            fill[j]()
                        if q or not first:
                            act.wait_ge(m_raw, n)
                        nc.scalar.activation(gate[:, j], result(act, st, g), ACT.Sigmoid)\
                            .then_inc(proj_read[g.slot], 1)
                act.wait_ge(m_raw, n + 1)
                nc.scalar.activation(chunk(m_hi, n), mrg[:, 0], ACT.Copy).then_inc(m_hi_s, 1)

        def dve_merge(dve, i, first, chain, fill=None):
            link = chain.link
            for q in range(RING):
                n = RING * i + q
                for j in range(MERGE_STRIPS):
                    st = Nth(S_MERGE + MERGE_STRIPS * q + j, RING * MERGE_STRIPS, i)
                    split_lo(dve, st.plus(3))
                    if fill and q == 0 and j < 3:
                        fill[j]()
                    if j < 3:
                        continue
                    for br in ((0, 1), (2,))[j - 3]:
                        gg = Nth(G_MERGE + MERGE_GROUPS * q + br, RING * MERGE_GROUPS, i)
                        gb = gg.plus(3)
                        dve.wait_ge(proj_read[gg.slot], gg.turn + 1)
                        res = result(dve, st, gb)
                        nc.vector.tensor_tensor(gate[:, br], gate[:, br], res, ALU.mult)\
                            .then_inc(proj_read[gb.slot], 1)
                        dve.wait_ge(proj_read[gb.slot], gb.turn + 1)
                        if br == 1:
                            link(nc.vector.tensor_tensor(mrg[:, 1], gate[:, 0], gate[:, 1], ALU.add))
                        if br == 2:
                            nc.vector.tensor_tensor(mrg[:, 0], mrg[:, 1], gate[:, 2], ALU.add).then_inc(m_raw, 1)
                dve.wait_ge(m_hi_s, n + 1)
                nc.vector.tensor_tensor(chunk(m_lo, n), mrg[:, 0], chunk(m_hi, n).bitcast(F32),
                                        ALU.subtract).then_inc(m_lo_s, 1)

        block = ctx.enter_context(nc.Block())

        @block.sync
        def _(sp):
            def load(s, t, t_int):
                if t_int:
                    sp.wait_ge(lo_ready, RING * t + s - RING + 1)
                src = stream[RING * t + s] if isinstance(t, int) else \
                    stream[bass.ds(RING * t + s, 1)].rearrange("a p n -> (a p) n")
                sp.dma_start(raw[:, s], src).then_inc(raw_in[s], 16)
            load(0, 0, 0)
            for n in range(4):
                sp.dma_start(h[:, 2 * n:2 * n + 2], x_in[:, 2 * n:2 * n + 2]).then_inc(in_x[n], 16)
            for s in range(1, RING):
                load(s, 0, 0)
            with sp.Fori(1, STRIPS // RING) as t:
                for s in range(RING):
                    load(s, t, 1)

        @block.gpsimd
        def _(pool):
            for dst, value in ((ones_full, 1.0), (mean_d, 1.0 / D), (mean_w, 1.0 / W5), (mean_p, 1.0 / P)):
                nc.gpsimd.memset(dst[:], value).then_inc(const_set, 1)
            for n, value in enumerate((LN_EPS / ALPHA ** 2, LN_EPS, EPS, 0.0)):
                nc.gpsimd.memset(eps_c[:, n:n + 1], value).then_inc(const_set, 1)
            pool.wait_ge(hid_l, KF)
            pool_sum_groups(pool, LN1, G_DOWN1)
            pool.wait_ge(in_cols, 16)
            pool_apply(pool, LN1, HI0[0])
            pool_mix(pool)
            pool.wait_ge(mix_lo, KD)
            pool.dma_start(side[:], mem_in).then_inc(in_mem, 16)
            pool_sum(pool, MEMN, lambda c: pool.wait_ge(in_mem, 16) if c == 0 else None)
            ge(pool, n_mean, LN2.ck)
            nc.gpsimd.memset(zsum, 0.0).then_inc(zsum_step, 1)
            for n in range(KD):
                _, g = wout_at(n)
                pool.wait_ge(proj_read[g.slot], g.turn + 1)
                pool.wait_ge(zsum_step, LN2.z0 + 1 + n)
                nc.gpsimd.tensor_tensor(zsum, zsum, h[:, n], ALU.add).then_inc(zsum_step, 1)
                if n == 5:
                    pool_apply(pool, MEMN, HI0[1])
            pool_apply(pool, LN2, HI0[2])
            pool.wait_ge(n_lo, HI0[1] + KD)
            pool.dma_start(side[:], ctx_in).then_inc(in_ctx, 16)
            pool.wait_ge(mod_ready, 2)
            pool_apply(pool, CTXN, HI0[3])
            pool_sum_groups(pool, LN3, G_XO)
            pool_apply(pool, LN3, HI0[4])
            pool.wait_ge(hid_l, 2 * KF)
            pool_sum_groups(pool, LN4, G_DOWN2)
            pool_apply(pool, LN4, 0)
            pool_apply(pool, MODN, HI0[6])
            pool.wait_ge(n_lo, HI0[6] + KD)
            nc.gpsimd.memset(cv[:], 0.0).then_inc(b_edge, 1)
            nc.gpsimd.memset(glu[:], 0.0).then_inc(b_edge, 1)
            pool.dma_start(band[:].rearrange("p k t -> p (k t)"), band_in).then_inc(in_band, 16)
            pool.wait_ge(in_band, 16)
            pool.wait_ge(ck_ready, 1)
            for t in range(MB):
                g = Nth(G_CTXV + t)
                pool.wait_ge(proj_read[g.slot], g.turn + 1)
            pool_na(pool, 0, True)
            with pool.Fori(1, KW) as i:
                pool_na(pool, i, False)
            pool_sum(pool, CONFN, lambda c: pool.wait_ge(na_conv, c + 1))

        @block.scalar
        def _(act):
            chain = Chain(act, act_step)
            act.dma_start(cols[:], cols_in).then_inc(in_cols, 16)
            act.dma_start(consts[:].rearrange("p a t -> p (a t)"), const_in).then_inc(in_const, 16)
            nc.scalar.preload_act_table_set(LN_EXP)
            act.wait_ge(const_set, 8)
            split_hi(act, Nth(0))
            for c in range(KD):
                act.wait_ge(in_x[c // 2], 16)
                nc.scalar.activation(a_hi[:, c], h[:, c], ACT.Copy).then_inc(x_hi, 1)
            split_hi(act, Nth(1))
            split_hi(act, Nth(2))
            act.wait_ge(lb_max, 2)
            nc.scalar.activation(lbv[:, 1:3], lbv[:, 1:3], ACT.Exp).then_inc(lb_exp, 1)
            act.wait_ge(in_cols, 16)
            chain.link(nc.scalar.activation(cond_s[:].rearrange("p k t -> p (k t)"), col("cond", 0, 2 * KD), ACT.Silu))
            nc.scalar.activation(cond4[:, :, 0:2], cond_s[:], ACT.Copy).then_inc(cond_silu, 1)
            act_ffn(act, S_FFN1, G_FFN1)
            act_splits(act, S_DOWN1, DOWN_STRIPS * KD)
            act_squares(act, LN1)
            act_std(act, LN1, chain)
            act_hi(act, LN1)
            act_mix(act, chain)
            for n in range(KD):
                act_only_splits(act, S_WOUT, 4 * n, 4 * n + 4)
                if n == 2:
                    act_squares(act, MEMN)
                if n == 4:
                    act_std(act, MEMN, chain)
                if n == 5:
                    act_hi(act, MEMN)
            act_squares(act, LN2)
            act_memkv(act, 0, 3)
            act_std(act, LN2, chain)
            act_memkv(act, 3, 6)
            act_hi(act, LN2)
            act_memkv(act, 6, 16)
            for n in range(KD):
                st, g = Nth(S_XQ + n), Nth(G_XQ + n)
                split_hi(act, st.plus(3))
                nc.scalar.activation(xq[:, n], result(act, st, g), ACT.Copy,
                                     scale=float(2 * P) ** -0.5).then_inc(proj_read[g.slot], 1)
                if n == 1:
                    act_squares(act, CTXN, ready=lambda c: act.wait_ge(in_ctx, 16))
                if n == 3:
                    act_std(act, CTXN, chain)
                if n == 4:
                    act.wait_ge(mod_ready, 2)
                    act_hi(act, CTXN)
            act_ctxk(act)
            act_ctxk_norm(act, chain)
            act_attention(act)
            act_only_splits(act, S_XO, 0, KD)
            act_squares(act, LN3)
            act_only_splits(act, S_CTXV, 0, 2)
            act_std(act, LN3, chain)
            act_only_splits(act, S_CTXV, 2, 4)
            act_ctxv_take(act)
            act_hi(act, LN3)
            act_ffn(act, S_FFN2, G_FFN2)
            act_splits(act, S_DOWN2, DOWN_STRIPS * KD)
            act_squares(act, LN4)
            act_std(act, LN4, chain)
            act_squares(act, MODN, ready=lambda c: act.wait_ge(n_raw, LN4.c0 + c + 1))
            act_std(act, MODN, chain)
            act_hi(act, MODN)
            act_na(act, 0, True, chain)
            with act.Fori(1, KW) as i:
                chain.enter(2, i - 1)
                act_na(act, i, False, chain)
                chain.leave(KW - 1)

            def split_y(b):
                for k in range(KW):
                    if b == 2:
                        act.wait_ge(y_c, k + 1)
                    else:
                        act.wait_ge((na_ya, na_yb)[b], KW)
                    nc.scalar.activation(y_hi[:, KW * b + k], y[:, b, k], ACT.Copy).then_inc(y_hi_s, 1)

            def conf_end():
                act_std(act, CONFN, chain)
                nc.scalar.activation(zc[:], zc[:], ACT.Silu).then_inc(y_silu, 1)
                for c in range(KW):
                    act.wait_ge(n_xn, CONFN.c0 + c + 1)
                    nc.scalar.activation(y[:, 2, c], y[:, 2, c], ACT.Silu, scale=CONFN.gain(c),
                                         bias=CONFN.shift(c)).then_inc(y_silu, 1)
                split_y(2)

            act.wait_ge(u_pv, UN * KW)
            act.wait_ge(na_conv, KW)
            split_y(0)
            split_y(1)
            act_squares(act, CONFN)
            act_merge(act, 0, True, [lambda: None, lambda: None, conf_end])
            with act.Fori(1, KD // RING) as i:
                act_merge(act, i, False)
            for n in range(KD):
                split_hi(act, Nth(S_WO + n + 3))
                g = Nth(G_WO + n)
                act.wait_ge(proj_read[g.slot], g.turn + 1)
                act.dma_start(out[n], h[:, n]).then_inc(out_done, 16)
            act.wait_ge(out_done, 16 * KD)

        @block.vector
        def _(dve):
            chain = Chain(dve, dve_step)
            link = chain.link
            dve.wait_ge(in_cols, 16)
            a, b = col("lb", 0, HH), col("lb", HH, HH)
            link(nc.vector.tensor_tensor(lbv[:, 0], a, b, ALU.max))
            nc.vector.tensor_tensor(lbv[:, 1], a, lbv[:, 0], ALU.subtract).then_inc(lb_max, 1)
            nc.vector.tensor_tensor(lbv[:, 2], b, lbv[:, 0], ALU.subtract).then_inc(lb_max, 1)
            link(nc.vector.tensor_scalar(qg8[:], col("qn_g"), float(HD) ** -0.5, None, ALU.mult))
            split_lo(dve, Nth(0))
            for c in range(KD):
                dve.wait_ge(x_hi, c + 1)
                nc.vector.tensor_tensor(a_lo[:, c], h[:, c], a_hi[:, c].bitcast(F32), ALU.subtract).then_inc(x_lo, 1)
            split_lo(dve, Nth(1))
            split_lo(dve, Nth(2))
            dve.wait_ge(lb_exp, 1)
            link(nc.vector.tensor_tensor(lbv[:, 3], lbv[:, 1], lbv[:, 2], ALU.add))
            link(nc.vector.reciprocal(lbv[:, 6], lbv[:, 3]))
            link(nc.vector.tensor_tensor(lbv[:, 4], lbv[:, 1], lbv[:, 6], ALU.mult))
            link(nc.vector.tensor_scalar(lbv[:, 5], lbv[:, 4], -1.0, 1.0, ALU.mult, ALU.add))
            dve.wait_ge(cond_silu, 1)
            nc.vector.tensor_tensor(cond4[:, :, 2:4], cond_s[:], cond4[:, :, 0:2].bitcast(F32), ALU.subtract)\
                .then_inc(cond_split, 1)
            dve.wait_ge(in_const, 16)
            link(nc.vector.tensor_tensor(pair_sum[:], ident[:, 0:2], ident[:, 2:4], ALU.add))
            dve_ffn(dve, S_FFN1, G_FFN1, 0)
            dve_residual(dve, S_DOWN1, G_DOWN1, 0.5 / ALPHA, DOWN_STRIPS)
            dve_centre(dve, LN1)
            dve_normalise(dve, LN1)
            dve_mix(dve, chain)
            for n in range(KD):
                dve_ada(dve, n)
                st, g = wout_at(n)
                split_lo(dve, st.plus(3))
                nc.vector.scalar_tensor_tensor(h[:, n], result(dve, st, g), 1.0 / ALPHA, h[:, n], ALU.mult,
                                               ALU.add).then_inc(proj_read[g.slot], 1)
                if n % 4:
                    dve_ada_take(dve, n - 1 - n // 4)
                if n == 1:
                    dve_centre(dve, MEMN)
                if n == 5:
                    dve_normalise(dve, MEMN)
            dve_centre(dve, LN2)
            dve_only_splits(dve, S_MEMK, 0, 3)
            dve_only_splits(dve, S_MEMK, 3, 6)
            dve_normalise(dve, LN2)
            for which in range(2):
                nc.vector.scalar_tensor_tensor(mod_a[:, which], modv[:, KD:2 * KD, which], 1.0, col("norm_g", 0, KD),
                                               ALU.add, ALU.mult).then_inc(mod_ready, 1)
            dve_only_splits(dve, S_MEMK, 6, 16)
            for n in range(KD):
                split_lo(dve, Nth(S_XQ + n + 3))
                if n == 4:
                    dve_normalise(dve, CTXN)
            dve_only_splits(dve, S_CTXK, 0, KW)
            dve_ctxk_norm(dve)
            dve_attention(dve, chain)
            dve_residual(dve, S_XO, G_XO, 1.0 / ALPHA)
            dve_centre(dve, LN3)
            dve_only_splits(dve, S_CTXV, 0, 2)
            dve_only_splits(dve, S_CTXV, 2, 4)
            dve_normalise(dve, LN3)
            dve_ffn(dve, S_FFN2, G_FFN2, KF)
            dve_residual(dve, S_DOWN2, G_DOWN2, 0.5 / ALPHA, DOWN_STRIPS)
            dve_centre(dve, LN4)
            dve_normalise(dve, LN4)
            dve_normalise(dve, MODN)
            dve_na(dve, 0, True, chain)
            with dve.Fori(1, KW) as i:
                chain.enter(NA_LINKS, i - 1)
                dve_na(dve, i, False, chain)
                chain.leave(KW - 1)

            def split_y(b):
                for k in range(KW):
                    dve.wait_ge(y_hi_s, KW * b + k + 1)
                    nc.vector.tensor_tensor(y_lo[:, KW * b + k], y[:, b, k], y_hi[:, KW * b + k].bitcast(F32),
                                            ALU.subtract).then_inc(y_lo_s, 1)

            def conf_end():
                dve_normalise(dve, CONFN)
                for c in range(KW):
                    dve.wait_ge(y_silu, c + 2)
                    nc.vector.tensor_tensor(y[:, 2, c], y[:, 2, c], zc[:, c], ALU.mult).then_inc(y_c, 1)
                split_y(2)

            dve_centre(dve, CONFN)
            split_y(0)
            split_y(1)
            dve_merge(dve, 0, True, chain, [lambda: None, lambda: None, conf_end])
            with dve.Fori(1, KD // RING) as i:
                chain.enter(RING, i - 1)
                dve_merge(dve, i, False, chain)
                chain.leave(KD // RING - 1)
            for n in range(KD):
                st, g = Nth(S_WO + n), Nth(G_WO + n)
                split_lo(dve, st.plus(3))
                nc.vector.scalar_tensor_tensor(h[:, n], result(dve, st, g), modv[:, 2 * KD + n, 0:1], h[:, n],
                                               ALU.mult, ALU.add).then_inc(proj_read[g.slot], 1)

        @block.tensor
        def _(pe):
            pe.wait_ge(const_set, 8)
            pe_ffn(pe, S_FFN1, G_FFN1, lambda k: pe.wait_ge(x_lo, k + 1))
            pe_down(pe, S_DOWN1, G_DOWN1, 0)
            pe_mean(pe, LN1)
            pe_stats(pe, LN1)
            pe.wait_ge(in_const, 16)
            pe_mix(pe)
            for n in range(KD):
                ready = (lambda k: pe.wait_ge(mix_lo, MIX_ORDER.index(k) + 1)) if n == 0 else None
                pe_ada(pe, n)
                st, g = wout_at(n)
                feature_strip(pe, st, g, a_hi, a_lo, order=MIX_ORDER, ready=ready)
                if n % 4:
                    pe_ada_turn(pe, n - 1 - n // 4)
                if n == 1:
                    pe_mean(pe, MEMN)
                if n == 2:
                    pe_stats(pe, MEMN)
            pe_mean(pe, LN2)
            pe_memkv(pe, 0, 3)
            pe_stats(pe, LN2)
            pe_memkv(pe, 3, 6)
            pe_memkv(pe, 6, 16)
            for n in range(KD):
                feature_strip(pe, Nth(S_XQ + n), Nth(G_XQ + n), a_hi, a_lo,
                              ready=lo_ready_of(pe, LN2, HI0[2]) if n == 0 else None)
                if n == 2:
                    pe_stats(pe, CTXN)
            pe_ctxk(pe)
            pe_ctxk_norm(pe)
            pe_attention(pe)
            for u in range(UNITS - RING, UNITS):
                g = Nth(G_PV + u)
                pe.wait_ge(proj_read[g.slot], g.turn + 1)
            with pe.Fori(0, KD // RING) as i:
                for q in range(RING):
                    feature_strip(pe, Nth(S_XO + q, RING, i), Nth(G_XO + q, RING, i), a_hi, a_lo)
            pe_mean(pe, LN3)
            pe_ctxv(pe, 0, 2)
            pe_stats(pe, LN3)
            pe_ctxv(pe, 2, 4)
            pe_ffn(pe, S_FFN2, G_FFN2, lo_ready_of(pe, LN3, HI0[4]))
            pe_down(pe, S_DOWN2, G_DOWN2, KF)
            pe_mean(pe, LN4)
            pe_stats(pe, LN4)
            pe_stats(pe, MODN)
            pe_na(pe, 0, True)
            with pe.Fori(1, KW) as i:
                pe_na(pe, i, False)
            pe_merge(pe, 0, True, [lambda: pe_mean(pe, CONFN), lambda: pe_stats(pe, CONFN), lambda: None])
            with pe.Fori(1, KD // RING) as i:
                pe_merge(pe, i, False)
            for n in range(KD):
                feature_strip(pe, Nth(S_WO + n), Nth(G_WO + n), m_hi, m_lo,
                              ready=(lambda k: pe.wait_ge(m_lo_s, k + 1)) if n == 0 else None)


def feature_major(w):
    k, n = w.shape
    return w.reshape(k // P, P, n // P, P).transpose(2, 1, 0, 3).reshape(n // P, P, k)


def token_major(w):
    return w.reshape(4, 2, P, W5).transpose(0, 2, 1, 3).reshape(4, P, 2 * W5)


def down_strips(w):
    blocks = feature_major(w)
    return np.pad(blocks, ((0, 0), (0, 0), (0, DOWN_STRIPS * SB * P - F_FF))).reshape(
        KD, P, DOWN_STRIPS, SB * P).transpose(0, 2, 1, 3).reshape(KD * DOWN_STRIPS, P, SB * P)


def vector_cols(v):
    return v.reshape(-1, P).T


def weight_stream(i):
    def ffn(tag):
        gate, up = feature_major(i[tag + "_w_gate"][0]), feature_major(i[tag + "_w_up"][0])
        return [np.stack([gate, up], 1).reshape(2 * KF, P, SB * P), down_strips(i[tag + "_w_down"][0])]

    w_ada = i["w_ada_2"][0]
    ada = np.concatenate([token_major(w_ada[:, n * W5:(n + 1) * W5]) for n in range(6)], 0)
    w_in = i["w_in"][0]
    q, fz, iv, g, u, v = (w_in[:, n * W5:(n + 1) * W5] for n in range(6))
    parts = ffn("ffn1")
    parts += [feature_major(fz), feature_major(q), token_major(iv), token_major(v), feature_major(u),
              feature_major(g)]
    w_out = feature_major(i["w_out"][0])
    parts += [np.concatenate([ada.reshape(KD, 3, P, SB * P), w_out[:, None]], 1).reshape(4 * KD, P, SB * P)]
    w_v = i["xa_w_v"][0]
    w2 = i["w_in_2"][0]
    part = [w2[:, n * W5:(n + 1) * W5] for n in range(11)]
    parts += [feature_major(i["xa_w_k"][0]), token_major(w_v[:, :W5]), token_major(w_v[:, W5:]),
              feature_major(i["xa_w_q"][0]), feature_major(part[1]), feature_major(i["xa_w_o"][0]),
              token_major(part[2])]
    parts += ffn("ffn2")
    na = [feature_major(part[n]) for n in (1, 0, 2, 8, 9, 3, 4, 5, 6, 7)]
    z = feature_major(part[10])
    zero = np.zeros_like(z[:, :, :4 * P])
    na += [np.concatenate([z[:, :, :4 * P], zero], 2), np.concatenate([z[:, :, 4 * P:], zero], 2)]
    parts += [np.stack(na, 1).reshape(KW * NA_STRIPS, P, SB * P)]
    gates = [feature_major(w2[:, 11 * W5 + n * D:11 * W5 + (n + 1) * D]) for n in range(3)]
    oa, ob, oc = (feature_major(i["w_out_" + n + "_2"][0]) for n in "abc")
    parts += [np.stack(gates + [np.concatenate([oa, ob], 2), np.concatenate([oc, np.zeros_like(oc)], 2)],
                       1).reshape(KD * MERGE_STRIPS, P, SB * P)]
    parts += [feature_major(i["w_o_2"][0])]
    whole = np.concatenate(parts, 0)
    assert whole.shape == (STRIPS, P, SB * P), whole.shape
    return whole


def column_table(i):
    named = {n: vector_cols(i[n]) for n in ("ln1_g", "ln1_b", "ln2_g", "ln2_b", "ln3_g", "ln3_b", "ln4_g", "ln4_b")}
    named["mem_g"], named["mem_b"] = vector_cols(i["mem_ln_g"]), vector_cols(i["mem_ln_b"])
    named["norm_g"] = vector_cols(i["norm_g_2"])
    named["lb"] = i["hg_lb_logits"].reshape(2 * HH, P).T
    named["hg_g"] = vector_cols(i["hg_norm_g"])
    named["b_ada"] = vector_cols(i["b_ada_2"])
    named["cond"] = np.stack([vector_cols(i["c_2"]), vector_cols(i["c_ctx_2"])], 2).reshape(P, 2 * KD)
    named["qn_g"] = np.tile(i["q_norm_g_2"].reshape(HD, 1), (2, 1))
    named["kn_g"] = np.tile(i["k_norm_g_2"].reshape(HD, 1), (2, 1))
    named["short_w"] = i["conv_short_w_2"][0].reshape(3, KW, P).transpose(2, 1, 0).reshape(P, 3 * KW)
    named["conf_w"] = i["conv_conf_w_2"][0].reshape(TAPS, KW, P).transpose(2, 1, 0).reshape(P, TAPS * KW)
    named["conf_b"] = vector_cols(i["conv_conf_b_2"])
    named["lnc_g"], named["lnc_b"] = vector_cols(i["ln_conf_g_2"]), vector_cols(i["ln_conf_b_2"])
    assert all(named[n].shape[1] == COLS[n][1] for n in COLS)
    return np.concatenate([named[n] for n in COLS], 1)


def shape_constants():
    p = np.arange(P)
    consts = np.concatenate([np.eye(P), (p[:, None] // HD == p // HD) / HD], 1).astype(np.float32)
    masks = []
    for lev in range(LEVELS):
        n = 1 << lev
        t = np.concatenate([np.arange(n) + 2 * n * b + n for b in range(P // (2 * n))])
        masks.append((p[:, None] // (2 * n) == t // (2 * n)) & (p[:, None] % (2 * n) < n))
    masks = np.concatenate(masks + [np.eye(P, dtype=bool)], 1).astype(np.int32)
    band = np.zeros((P, 3, ROWS, BAND), np.float32)
    for kind, cb in enumerate((0, 1, 3)):
        qcol = cb * QC + p % QC
        start = np.clip(qcol - 8, 0, GRID - 16)
        rel = BAND_AT[cb] + np.arange(BAND)[None] - start[:, None]
        band[:, kind] = np.where((rel >= 0) & (rel < 16), 0.0, -1e30)[:, None]
    return consts, masks, band.reshape(P, -1)


def bias_windows(rpb):
    pad = np.pad(rpb, ((0, 0), (0, 0), (BAND, BAND)))
    r, q = np.arange(P) // QC, np.arange(P) % QC
    rows = (ROWS - 1 - r)[:, None] + np.arange(ROWS)
    colsx = np.arange(RPB_W)[None] - BIAS_AT + (15 + BAND) - q[:, None]
    return pad[:, rows[:, :, None], colsx[:, None, :]].transpose(1, 0, 2, 3).reshape(P, NH, ROWS * RPB_W)


def token_chunks(a):
    return a.T.reshape(KD, P, -1).transpose(1, 0, 2)


def kernel(**inputs):
    import concourse.bacc as bacc
    from concourse.bass_utils import run_bass_kernel_spmd

    i = {n: np.asarray(a) for n, a in inputs.items()}
    consts, masks, band = shape_constants()
    rows = np.concatenate([i["sg_ln_g"].reshape(-1), i["sg_ln_b"].reshape(-1), i["sg_b_s"].reshape(-1)])
    arrays = {
        "stream": weight_stream(i), "x_in": token_chunks(i["x"][0]), "mem_in": token_chunks(i["mem"][0]),
        "ctx_in": token_chunks(i["ctx_2"][0]), "cols_in": column_table(i), "const_in": consts, "mask_in": masks,
        "rows_in": rows, "wst_in": i["sg_w_s"][0].transpose(2, 0, 1).reshape(P, HH * P), "band_in": band,
        "rpb_in": bias_windows(i["rpb_2"][0]),
    }
    nc = bacc.Bacc("TRN2", target_bir_lowering=False, num_devices=1)
    aps = []
    for name in arrays:
        a = arrays[name] = np.ascontiguousarray(arrays[name])
        aps.append(nc.dram_tensor(name, a.shape, mybir.dt.from_np(a.dtype), kind="ExternalInput").ap())
    out = nc.dram_tensor("out", (KD, P, T), F32, kind="ExternalOutput").ap()
    hybrid_blocks(nc, *aps, out)
    r = run_bass_kernel_spmd(nc, [arrays], core_ids=[0])
    return r.results[0]["out"].reshape(D, T).T.reshape(1, T, D)
```

```python
from contextlib import ExitStack

import concourse.bass as bass
import numpy as np
from concourse import mybir

F32 = mybir.dt.float32
F32R = mybir.dt.float32r
I32 = mybir.dt.int32
ACT = mybir.ActivationFunctionType
ALU = mybir.AluOpType
AX = mybir.AxisListType.X

P = 128
T = 512
D = 1024
KD = D // P
TB = T // P
F_FF = 2816
KF = F_FF // P
M = 256
MB = M // P
HH = 4
W5 = 512
KW = W5 // P
ALPHA = 2.0 ** 0.25
LN_EPS = 1e-5
EPS = 1e-6
XH = 4
NH = 8
HD = 64
ROWS, GRID = 8, 64
QC, BAND = 16, 32
NCB = GRID // QC
BAND_AT = [0, 8, 24, 32]
BIAS_KIND = [0, 1, 1, 2]
BIAS_OFF = [0, -8, -16]
BIAS_AT = 16
RPB_W = BIAS_AT + BAND
TAPS = 31
NA_LINKS = 52
LEVELS = 7
RING = 4
SB = 8

S_FFN1 = 0
S_DOWN1 = S_FFN1 + 2 * KF
DOWN_STRIPS = 3
S_MIX = S_DOWN1 + DOWN_STRIPS * KD
S_WOUT = S_MIX + 24
S_MEMK = S_WOUT + 4 * KD
S_MEMV = S_MEMK + KD
S_XQ = S_MEMV + KD
S_CTXK = S_XQ + KD
S_XO = S_CTXK + KW
S_CTXV = S_XO + KD
S_FFN2 = S_CTXV + KW
S_DOWN2 = S_FFN2 + 2 * KF
S_NA = S_DOWN2 + DOWN_STRIPS * KD
NA_STRIPS = 12
S_MERGE = S_NA + NA_STRIPS * KW
MERGE_STRIPS = 5
S_WO = S_MERGE + MERGE_STRIPS * KD
STRIPS = S_WO + KD
assert STRIPS % RING == 0

G_FFN1 = 0
G_DOWN1 = G_FFN1 + 2 * KF
G_MIX = G_DOWN1 + KD
G_WOUT = G_MIX + 24
WOUT_G = [1, 3, 5, 6, 8, 10, 12, 13]
ADA_G = [0, 2, 4, 7, 9, 11]
G_MEMK = G_WOUT + len(WOUT_G) + len(ADA_G)
G_MEMV = G_MEMK + KD
G_XQ = G_MEMV + 2 * MB
G_CTXK = G_XQ + KD
G_PV = G_CTXK + KW
UNITS = 2 * XH
G_XO = G_PV + UNITS
G_CTXV = G_XO + KD
G_FFN2 = G_CTXV + MB
G_DOWN2 = G_FFN2 + 2 * KF
G_NA = G_DOWN2 + KD
NA_GROUPS = 12
G_MERGE = G_NA + NA_GROUPS * KW
MERGE_GROUPS = 6
G_WO = G_MERGE + MERGE_GROUPS * KD

COLS = {}
for _name, _n in [("ln1_g", KD), ("ln1_b", KD), ("ln2_g", KD), ("ln2_b", KD), ("ln3_g", KD), ("ln3_b", KD),
                  ("ln4_g", KD), ("ln4_b", KD), ("mem_g", KD), ("mem_b", KD), ("norm_g", KD), ("lb", 2 * HH),
                  ("hg_g", 1), ("b_ada", 3 * KD), ("cond", 2 * KD), ("qn_g", 1), ("kn_g", 1),
                  ("short_w", 3 * KW), ("conf_w", TAPS * KW), ("conf_b", KW), ("lnc_g", KW), ("lnc_b", KW)]:
    COLS[_name] = (sum(n for _, n in COLS.values()), _n)
NCOLS = sum(n for _, n in COLS.values())


class Nth:

    def __init__(self, base, per=0, i=0):
        assert per % RING == 0
        self.base, self.per, self.i = base, per, i
        self.slot = base % RING
        self.turn = base // RING + (per // RING) * i if per else base // RING
        self.n = base + per * i if per else base

    def plus(self, k):
        return Nth(self.base + k, self.per, self.i)


def ge(eng, sem, value):
    if not (isinstance(value, int) and value <= 0):
        eng.wait_ge(sem, value)


class Chain:

    def __init__(self, eng, sem):
        self.eng, self.sem, self.n, self.extra = eng, sem, 0, 0

    def link(self, ins):
        ins.then_inc(self.sem, 1)
        self.n += 1
        self.eng.wait_ge(self.sem, self.n + self.extra)

    def enter(self, per, i):
        self.per, self.start, self.extra = per, self.n, per * i

    def leave(self, times):
        assert self.n - self.start == self.per, (self.n, self.start, self.per)
        self.n += self.per * (times - 1)
        self.extra = 0


def hybrid_blocks(nc, stream, x_in, mem_in, ctx_in, cols_in, const_in, mask_in, rows_in, wst_in, band_in, rpb_in,
                  out):
    with ExitStack() as ctx:
        def sem(name):
            return ctx.enter_context(nc.semaphore(name))

        def sb(name, shape, dt=F32, scope=ctx):
            return scope.enter_context(nc.sbuf_tensor(name, shape, dt))

        proj = ctx.enter_context(nc.psum_tensor("proj", [P, RING, T], F32))
        aux = ctx.enter_context(nc.psum_tensor("aux", [P, 4, T], F32))

        raw = sb("raw", [P, RING, SB * P])
        w_hi = sb("w_hi", [P, RING, SB * P], F32R)
        w_lo = sb("w_lo", [P, RING, SB * P], F32R)
        h = sb("h", [P, KD, T])
        a_hi = sb("a_hi", [P, KD, T], F32R)
        a_lo = sb("a_lo", [P, KD, T], F32R)
        cols = sb("cols", [P, NCOLS])
        consts = sb("consts", [P, 2, P])
        ident = consts[:, 0]
        blk64 = consts[:, 1]
        ones_full = sb("ones_full", [P, P])
        mean_d = sb("mean_d", [P, P])
        mean_w = sb("mean_w", [P, P])
        mean_p = sb("mean_p", [P, P])
        eps_c = sb("eps_c", [P, 4])
        cond4 = sb("cond4", [P, KD, 4], F32R)
        pair_sum = sb("pair_sum", [P, 2])
        modv = sb("modv", [P, 3 * KD, 2])
        mod_a = sb("mod_a", [P, 2, KD])
        cond_s = sb("cond_s", [P, KD, 2])
        qg8 = sb("qg8", [P, 1])
        lbv = sb("lbv", [P, 8, HH])
        work = sb("work", [P, 2, T])
        zsum, rstd = work[:, 0], work[:, 1]
        sq = sb("sq", [P, 2, T])
        ctxk = sb("ctxk", [P, KW, M])
        mod_row = ctxk[:, 0:2].rearrange("p c t -> p (c t)")
        ctxv = sb("ctxv", [P, MB, W5])

        def col(name, c=0, n=1):
            at, _ = COLS[name]
            return cols[:, at + c:at + c + n]

        with ExitStack() as ph:
            hid_hi = sb("hid_hi", [P, KF, T], F32R, ph)
            hid_lo = sb("hid_lo", [P, KF, T], F32R, ph)
        with ExitStack() as ph:
            mq, mk, mb, mv, md = (sb(n, [P, HH, T], F32, ph) for n in ("mq", "mk", "mb", "mv", "md"))
            qk = sb("qk", [P, 2, HH, T], F32, ph)
            score = sb("score", [P, TB, HH, P], F32, ph)
            sv, su = (sb(n, [P, HH, T], F32, ph) for n in ("sv", "su"))
            levmask = sb("levmask", [P, LEVELS, P // 2], I32, ph)
            idmask = sb("idmask", [P, P], I32, ph)
            wst = sb("wst", [P, HH, P], F32, ph)
            rows = sb("rows", [P, 3, W5], F32, ph)
            bnst = sb("bnst", [P, 16, 6], F32, ph)
            bnag = sb("bnag", [P, 16, 2], F32, ph)
            vstd = sb("vstd", [P, 2, 16], F32, ph)
            decay = sb("decay", [P, HH, TB], F32, ph)
        with ExitStack() as ph:
            sb("under_mq_mk_mb_mv", [P, 4, HH * T], F32, ph)
            mix_h = sb("mix_h", [P, KD, T], F32R, ph)
            sb("under_qk", [P, HH * T], F32, ph)
            mix_l = sb("mix_l", [P, KD, T], F32R, ph)
        with ExitStack() as ph:
            side = sb("side", [P, KD, M], F32, ph)
            side_hi = sb("side_hi", [P, KD, M], F32R, ph)
            side_lo = sb("side_lo", [P, KD, M], F32R, ph)
            xq = sb("xq", [P, KD, T], F32, ph)
            memk = sb("memk", [P, KD, M], F32, ph)
            memv = sb("memv", [P, MB, D], F32, ph)
            xp = sb("xp", [P, 2, 2, M], F32, ph)
            xpt = sb("xpt", [P, 2, MB, M], F32, ph)
            xs = sb("xs", [P, 3, 8, 2], F32, ph)
            ksd = sb("ksd", [P, KW, M], F32, ph)
            krs = sb("krs", [P, KW, M], F32, ph)
        with ExitStack() as ph:
            with ExitStack() as part:
                y = sb("y", [P, 3, KW, T], F32, part)
                zc = sb("zc", [P, KW, T], F32, part)
            with ExitStack() as part:
                hm = sb("hm", [P, KD, T], F32, part)
            m_hi = sb("m_hi", [P, KD, T], F32R, ph)
            m_lo = sb("m_lo", [P, KD, T], F32R, ph)
            with ExitStack() as part:
                nq, nk, nza, nbg, ncg, nat, nsg, nzb = (
                    sb(n, [P, T], F32, part) for n in ("nq", "nk", "nza", "nbg", "ncg", "nat", "nsg", "nzb"))
                nvt = sb("nvt", [P, 2 * NCB, P], F32, part)
                nsq = sb("nsq", [P, 2, T], F32, part)
                vband = sb("vband", [P, 2 * NCB, P], F32, part)
                cv = sb("cv", [P, T + 2], F32, part)
                glu = sb("glu", [P, T + TAPS - 1], F32, part)
                ck_c = sb("ck_c", [P, M], F32, part)
                cv_c = sb("cv_c", [P, MB, P], F32, part)
                btab = sb("btab", [P, 2, ROWS * RPB_W], F32, part)
                bias = sb("bias", [P, 2, 3, ROWS * BAND], F32, part)
                band = sb("band", [P, 3, ROWS * BAND], F32, part)
                npr = sb("npr", [P, 2, T], F32, part)
                npt = sb("npt", [P, 2, T], F32, part)
                ns = sb("ns", [P, 3, 8], F32, part)
                wtap = sb("wtap", [P, TAPS + 4], F32, part)
            with ExitStack() as part:
                y_hi = sb("y_hi", [P, 3 * KW, T], F32R, part)
                y_lo = sb("y_lo", [P, 3 * KW, T], F32R, part)
                gate = sb("gate", [P, 3, T], F32, part)
                mrg = sb("mrg", [P, 2, T], F32, part)

        raw_in = [sem(f"raw_in{s}") for s in range(RING)]
        hi_ready, lo_ready = sem("hi_ready"), sem("lo_ready")
        strip_done = sem("strip_done")
        proj_read = [sem(f"proj_read{b}") for b in range(RING)]
        in_cols, in_const, in_mask, in_mem, in_ctx, in_band = (
            sem(n) for n in ("in_cols", "in_const", "in_mask", "in_mem", "in_ctx", "in_band"))
        in_x = [sem(f"in_x{n}") for n in range(4)]
        const_set = sem("const_set")
        dve_step, act_step = sem("dve_step"), sem("act_step")
        x_hi, x_lo = sem("x_hi"), sem("x_lo")
        cond_silu, cond_split = sem("cond_silu"), sem("cond_split")
        hid_h, hid_l = sem("hid_h"), sem("hid_l")
        zsum_step, n_mean, n_cent, n_sq, n_acc, n_stat, n_std, n_xn, n_hi, n_raw, n_lo = (
            sem(n) for n in ("zsum_step", "n_mean", "n_cent", "n_sq", "n_acc", "n_stat", "n_std", "n_xn",
                             "n_hi", "n_raw", "n_lo"))
        ada_turned, ada_out = sem("ada_turned"), sem("ada_out")
        mod_ready = sem("mod_ready")
        lb_max, lb_exp = sem("lb_max"), sem("lb_exp")
        m_sig, m_f, m_k, m_lf, m_b, m_fresh, m_zero = (
            sem(n) for n in ("m_sig", "m_f", "m_k", "m_lf", "m_b", "m_fresh", "m_zero"))
        l_diff, l_exp, l_lowk, l_fac, l_mm, l_put = (
            sem(n) for n in ("l_diff", "l_exp", "l_lowk", "l_fac", "l_mm", "l_put"))
        i_diff, i_expd, i_expb, i_ke, i_qe, i_tr, i_ket, i_kv, i_state, i_o, i_copy, i_osq, i_ms, i_std, i_on = (
            sem(n) for n in ("i_diff", "i_expd", "i_expb", "i_ke", "i_qe", "i_tr", "i_ket", "i_kv", "i_state", "i_o",
                             "i_copy", "i_osq", "i_ms", "i_std", "i_on"))
        v_var, v_std, v_norm, v_gain, v_mm, v_out, w_masked = (
            sem(n) for n in ("v_var", "v_std", "v_norm", "v_gain", "v_mm", "v_out", "w_masked"))
        mix_raw, mix_hi, mix_lo, mix_lo_pool = (sem(n) for n in ("mix_raw", "mix_hi", "mix_lo", "mix_lo_pool"))
        a_sc, a_max, a_exp, a_norm, a_tr, a_pt, a_pv, a_hi_s = (
            sem(n) for n in ("a_sc", "a_max", "a_exp", "a_norm", "a_tr", "a_pt", "a_pv", "a_hi_s"))
        ck_sq, ck_ms, ck_std, ck_ready = sem("ck_sq"), sem("ck_ms"), sem("ck_std"), sem("ck_ready")
        b_tab, b_ready, b_ctx, b_edge = sem("b_tab"), sem("b_ready"), sem("b_ctx"), sem("b_edge")
        na_vb, na_ksq, na_kms, na_kstd, na_k, na_qsq, na_q, na_silu, na_ya, na_yb, na_conv, na_glu, na_vband = (
            sem(n) for n in ("na_vb", "na_ksq", "na_kms", "na_kstd", "na_k", "na_qsq", "na_q", "na_silu",
                             "na_ya", "na_yb", "na_conv", "na_glu", "na_vband"))
        u_sc, u_max, u_exp, u_norm, u_tr, u_pt, u_pv = (
            sem(n) for n in ("u_sc", "u_max", "u_exp", "u_norm", "u_tr", "u_pt", "u_pv"))
        y_silu, y_c, y_hi_s, y_lo_s = sem("y_silu"), sem("y_c"), sem("y_hi_s"), sem("y_lo_s")
        m_raw, m_hi_s, m_lo_s, na_conv_b = (sem(n) for n in ("m_raw", "m_hi_s", "m_lo_s", "na_conv_b"))
        out_done = sem("out_done")

        LN_EXP = "natural_log_exp_and_others"

        def inverse_root(chain, dst, src, eps):
            chain.link(nc.scalar.activation(dst, src, ACT.Ln, bias=eps_c[:, eps:eps + 1]))
            return nc.scalar.activation(dst, dst, ACT.Exp, scale=-0.5)

        def result(eng, st, g):
            eng.wait_ge(strip_done, st.n + 1)
            return proj[:, g.slot]

        def split_hi(act, st):
            if isinstance(st.n, int) and st.n >= STRIPS:
                return
            act.wait_ge(raw_in[st.slot], 16 * st.turn + 16)
            ge(act, strip_done, st.n - (RING - 1))
            nc.scalar.activation(w_hi[:, st.slot], raw[:, st.slot], ACT.Copy).then_inc(hi_ready, 1)

        def split_lo(dve, st):
            if isinstance(st.n, int) and st.n >= STRIPS:
                return
            dve.wait_ge(hi_ready, st.n + 1)
            nc.vector.tensor_tensor(w_lo[:, st.slot], raw[:, st.slot], w_hi[:, st.slot].bitcast(F32),
                                    ALU.subtract).then_inc(lo_ready, 1)

        def product(dst, wh, wl, xh, xl, start, stop, moving_weights=False):
            for n, (a, b) in enumerate(((wh, xh), (wh, xl), (wl, xh))):
                if moving_weights:
                    a, b = b, a
                mm = nc.tensor.matmul(dst, a, b, start=start and n == 0, stop=stop and n == 2)
            return mm

        def feature_strip(pe, st, g, xh, xl, first=0, blocks=SB, last=True, order=None, ready=None, n=T, blk0=0):
            pe.wait_ge(lo_ready, st.n + 1)
            if first == 0:
                ge(pe, proj_read[g.slot], g.turn)
            for j, k in enumerate(order or range(blocks)):
                if ready:
                    ready(k)
                at = (blk0 + k) * P
                mm = product(proj[:, g.slot, :n], w_hi[:, st.slot, at:at + P], w_lo[:, st.slot, at:at + P],
                             xh[:, first + k], xl[:, first + k], first == 0 and j == 0, last and j == blocks - 1)
            mm.then_inc(strip_done, 1)

        def strip_pair(pe, st, g, xh, xl, ready):
            both = ((st, g), (st.plus(1), g.plus(1)))
            pe.wait_ge(lo_ready, st.n + 2)
            for _, gg in both:
                ge(pe, proj_read[gg.slot], gg.turn)
            for k in range(KD):
                ready(k)
                for s, gg in both:
                    mm = product(proj[:, gg.slot], w_hi[:, s.slot, k * P:(k + 1) * P],
                                 w_lo[:, s.slot, k * P:(k + 1) * P], xh[:, k], xl[:, k], k == 0, k == KD - 1)
                    if k == KD - 1:
                        mm.then_inc(strip_done, 1)

        def token_strip(pe, st, q, groups, xh, xl, ready=None):
            pe.wait_ge(lo_ready, st.n + 1)
            for kk in range(2):
                k = 2 * q + kk
                if ready:
                    ready(k)
                for t, g in enumerate(groups):
                    if k == 0:
                        ge(pe, proj_read[g.slot], g.turn)
                    mm = product(proj[:, g.slot], w_hi[:, st.slot, kk * W5:(kk + 1) * W5],
                                 w_lo[:, st.slot, kk * W5:(kk + 1) * W5], xh[:, k, t * P:(t + 1) * P],
                                 xl[:, k, t * P:(t + 1) * P], k == 0, k == KD - 1, moving_weights=True)
            mm.then_inc(strip_done, 1)

        class Norm:
            def __init__(self, k, ck, n, chunks, src, dst, gain, shift, hi, lo, eps, mean, groups=None):
                self.k, self.ck, self.n, self.chunks, self.src, self.dst = k, ck, n, chunks, src, dst
                self.gain, self.shift, self.hi, self.lo, self.eps, self.mean = gain, shift, hi, lo, eps, mean
                self.c0 = 8 * k
                self.summed = k in (1, 3)
                self.a0 = {1: 0, 3: 7}.get(k)
                self.t0 = (0, 8, 9, 17, 18, 26, 34, 42)[k]
                self.h0 = {0: 0, 1: 8, 2: 16, 3: 24, 4: 32, 6: 40}.get(k)
                self.r0 = {0: 0, 2: 8, 4: 16, 5: 24}.get(k)
                self.z0 = (0, 8, 17, 25, 33, 41)[ck or 0]
                self.groups = groups

        def wout_at(n):
            return Nth(S_WOUT + 4 * n + 3), Nth(G_WOUT + WOUT_G[n])

        def groups_of(g0):
            return [Nth(g0 + c) for c in range(KD)]

        LN1 = Norm(0, 0, T, KD, h, h, lambda c: col("ln1_g", c), lambda c: col("ln1_b", c), a_hi, a_lo, 0, mean_d,
                   groups_of(G_DOWN1))
        MEMN = Norm(1, 1, M, KD, side, side, lambda c: col("mem_g", c), lambda c: col("mem_b", c), side_hi, side_lo,
                    1, mean_d)
        LN2 = Norm(2, 2, T, KD, h, h, lambda c: col("ln2_g", c), lambda c: col("ln2_b", c), a_hi, a_lo, 0, mean_d,
                   [wout_at(c)[1] for c in range(KD)])
        CTXN = Norm(3, None, M, KD, side, side, lambda c: mod_a[:, 1, c:c + 1], lambda c: modv[:, c, 1:2],
                    side_hi, side_lo, 2, mean_d)
        LN3 = Norm(4, 3, T, KD, h, h, lambda c: col("ln3_g", c), lambda c: col("ln3_b", c), a_hi, a_lo, 0, mean_d,
                   groups_of(G_XO))
        LN4 = Norm(5, 4, T, KD, h, h, lambda c: col("ln4_g", c), lambda c: col("ln4_b", c), None, None, 0, mean_d,
                   groups_of(G_DOWN2))
        MODN = Norm(6, None, T, KD, h, hm, lambda c: mod_a[:, 0, c:c + 1], lambda c: modv[:, c, 0:1], a_hi, a_lo, 2,
                    mean_d)
        CONFN = Norm(7, 5, T, KW, y[:, 2], y[:, 2], lambda c: col("lnc_g", c), lambda c: col("lnc_b", c), None, None,
                     2, mean_w)

        def pe_mean(pe, m):
            if not m.groups:
                pe.wait_ge(zsum_step, m.z0 + 1 + m.chunks)
                nc.tensor.matmul(aux[:, 0, :m.n], m.mean[:], zsum[:, :m.n], start=True, stop=True).then_inc(n_mean, 1)
                return
            pe.wait_ge(zsum_step, m.z0 + m.chunks)
            nc.tensor.matmul(aux[:, 0], m.mean[:], zsum, start=True, stop=False)
            g = m.groups[-1]
            pe.wait_ge(proj_read[g.slot], g.turn + 1)
            nc.tensor.matmul(aux[:, 0], m.mean[:], h[:, KD - 1], start=False, stop=True).then_inc(n_mean, 1)

        def pe_stats(pe, m):
            if m.summed:
                pe.wait_ge(n_acc, m.a0 + m.chunks - 1)
                nc.tensor.matmul(aux[:, 1, :m.n], m.mean[:], rstd[:, :m.n], start=True, stop=True).then_inc(n_stat, 1)
                return
            for c in range(m.chunks):
                pe.wait_ge(n_sq, m.c0 + c + 1)
                nc.tensor.matmul(aux[:, 1, :m.n], m.mean[:], sq[:, c % 2, :m.n], start=(c == 0),
                                 stop=(c == m.chunks - 1)).then_inc(n_stat, 1)

        def dve_centre(dve, m):
            dve.wait_ge(n_mean, m.ck + 1)
            for c in range(m.chunks):
                nc.vector.tensor_tensor(m.src[:, c], m.src[:, c], aux[:, 0, :m.n], ALU.subtract).then_inc(n_cent, 1)

        def act_squares(act, m, ready=None, shift=None, lo=0, hi=None):
            if lo == 0:
                nc.scalar.preload_act_table_set(LN_EXP)
            for c in range(lo, hi or m.chunks):
                if m.ck is None:
                    ready(c)
                else:
                    act.wait_ge(n_cent, 8 * m.ck + c + 1)
                if c >= 2 and m.summed:
                    act.wait_ge(n_acc, m.a0 + max(1, c - 2))
                elif c >= 2:
                    act.wait_ge(n_stat, m.t0 + c - 1)
                nc.scalar.activation(sq[:, c % 2, :m.n], m.src[:, c], ACT.Square,
                                     bias=shift(c) if shift else 0.0).then_inc(n_sq, 1)

        def act_std(act, m, chain):
            act.wait_ge(n_stat, m.t0 + (1 if m.summed else m.chunks))
            inverse_root(chain, rstd[:, :m.n], aux[:, 1, :m.n], m.eps).then_inc(n_std, 1)

        def dve_normalise(dve, m, lo=0, hi=None, before=None):
            if lo == 0:
                dve.wait_ge(n_std, m.k + 1)
            for c in range(lo, m.chunks + 1 if hi is None else hi):
                if c < m.chunks:
                    if before is not None:
                        dve.wait_ge(n_raw, before.r0 + c + 1)
                    nc.vector.scalar_tensor_tensor(m.dst[:, c], m.src[:, c], m.gain(c), rstd[:, :m.n], ALU.mult,
                                                   ALU.mult).then_inc(n_xn, 1)
                if c >= 1 and m.lo is not None:
                    dve.wait_ge(n_hi, m.h0 + c)
                    nc.vector.scalar_tensor_tensor(m.lo[:, c - 1], m.dst[:, c - 1], m.shift(c - 1),
                                                   m.hi[:, c - 1].bitcast(F32), ALU.add,
                                                   ALU.subtract).then_inc(n_lo, 1)

        def act_hi(act, m, lo=0, hi=None):
            for c in range(lo, m.chunks if hi is None else hi):
                act.wait_ge(n_xn, m.c0 + c + 1)
                nc.scalar.activation(m.hi[:, c], m.dst[:, c], ACT.Identity, bias=m.shift(c)).then_inc(n_hi, 1)

        def pool_shift(pool, m):
            for c in range(m.chunks):
                if m.hi is not None:
                    pool.wait_ge(n_lo, m.h0 + c + 1)
                else:
                    pool.wait_ge(n_sq, MODN.c0 + c + 1)
                nc.gpsimd.tensor_scalar(m.dst[:, c], m.dst[:, c], 1.0, m.shift(c), ALU.mult, ALU.add).then_inc(n_raw, 1)

        def pool_squares(pool, m):
            for c in range(1, m.chunks):
                pool.wait_ge(n_sq, m.c0 + c + 1)
                if c > 1:
                    pool.wait_ge(n_acc, m.a0 + c - 1)
                nc.gpsimd.tensor_tensor(rstd[:, :m.n], sq[:, 0, :m.n] if c == 1 else rstd[:, :m.n],
                                        sq[:, c % 2, :m.n], ALU.add).then_inc(n_acc, 1)

        def pool_sum(pool, m, ready):
            ge(pool, n_mean, m.ck)
            nc.gpsimd.memset(zsum[:, :m.n], 0.0).then_inc(zsum_step, 1)
            for c in range(m.chunks):
                ready(c)
                pool.wait_ge(zsum_step, m.z0 + 1 + c)
                nc.gpsimd.tensor_tensor(zsum[:, :m.n], zsum[:, :m.n], m.src[:, c], ALU.add).then_inc(zsum_step, 1)

        def pool_residual_sum(pool, m, beside=None):
            ge(pool, n_mean, m.ck)
            nc.gpsimd.memset(zsum, 0.0).then_inc(zsum_step, 1)
            for c in range(KD - 1):
                g = m.groups[c]
                pool.wait_ge(proj_read[g.slot], g.turn + 1)
                pool.wait_ge(zsum_step, m.z0 + 1 + c)
                nc.gpsimd.tensor_tensor(zsum, zsum, h[:, c], ALU.add).then_inc(zsum_step, 1)
                if c == 1 and beside:
                    beside()

        def lo_ready_of(pe, m):
            return lambda k: pe.wait_ge(n_lo, m.h0 + k + 1)

        def dve_residual(dve, s0, g0, factor, per_out=1, before=None):
            if before is not None:
                dve.wait_ge(n_raw, before.r0 + KD)
            with dve.Fori(0, KD // RING) as i:
                for q in range(RING):
                    for j in range(per_out):
                        st = Nth(s0 + q * per_out + j, RING * per_out, i)
                        split_lo(dve, st.plus(3))
                    g = Nth(g0 + q, RING, i)
                    res = result(dve, st, g)
                    hc = h[:, bass.ds(RING * i + q, 1)].rearrange("p a t -> p (a t)")
                    nc.vector.scalar_tensor_tensor(hc, res, factor, hc, ALU.mult,
                                                   ALU.add).then_inc(proj_read[g.slot], 1)

        def act_splits(act, s0, n):
            assert n % RING == 0
            with act.Fori(0, n // RING) as i:
                for q in range(RING):
                    split_hi(act, Nth(s0 + 3 + q, RING, i))

        def pe_ffn(pe, s0, g0, ready, pair=False):
            def two(i, first):
                if first and pair:
                    strip_pair(pe, Nth(s0), Nth(g0), a_hi, a_lo, ready)
                for j in range(2 if first and pair else 0, 4):
                    feature_strip(pe, Nth(s0 + j, 4, i), Nth(g0 + j, 4, i), a_hi, a_lo,
                                  ready=ready if first and j == 0 else None)
            two(0, True)
            with pe.Fori(1, KF // 2) as i:
                two(i, False)

        def pe_down(pe, s0, g0, hid0):
            with pe.Fori(0, KD // RING) as i:
                for q in range(RING):
                    for j in range(DOWN_STRIPS):
                        if q == 0:
                            pe.wait_ge(hid_l, hid0 + min(KF, SB * (j + 1)))
                        feature_strip(pe, Nth(s0 + q * DOWN_STRIPS + j, RING * DOWN_STRIPS, i), Nth(g0 + q, RING, i),
                                      hid_hi, hid_lo, first=SB * j, blocks=min(SB, KF - SB * j),
                                      last=(j == DOWN_STRIPS - 1))

        def act_ffn(act, s0, g0):
            def two(i, first):
                for j in range(4):
                    st, g = Nth(s0 + j, 4, i), Nth(g0 + j, 4, i)
                    split_hi(act, st.plus(3))
                    if j % 2 == 0:
                        res = result(act, st, g)
                        if not first:
                            act.wait_ge(proj_read[g.plus(1).slot], g.plus(1).turn)
                        nc.scalar.activation(sq[:, j // 2], res, ACT.Silu).then_inc(proj_read[g.slot], 1)
                    else:
                        act.wait_ge(proj_read[g.slot], g.turn + 1)
                        hc = hid_hi[:, bass.ds(2 * i + j // 2, 1)].rearrange("p a t -> p (a t)") if not first \
                            else hid_hi[:, j // 2]
                        nc.scalar.activation(hc, work[:, j // 2], ACT.Copy).then_inc(hid_h, 1)
            two(0, True)
            with act.Fori(1, KF // 2) as i:
                two(i, False)

        def dve_ffn(dve, s0, g0, hid0):
            def two(i, first):
                for j in range(4):
                    st, g = Nth(s0 + j, 4, i), Nth(g0 + j, 4, i)
                    split_lo(dve, st.plus(3))
                    if j % 2:
                        gate_g = Nth(g0 + j - 1, 4, i)
                        res = result(dve, st, g)
                        dve.wait_ge(proj_read[gate_g.slot], gate_g.turn + 1)
                        nc.vector.tensor_tensor(work[:, j // 2], sq[:, j // 2], res,
                                                ALU.mult).then_inc(proj_read[g.slot], 1)
                        dve.wait_ge(hid_h, hid0 + j // 2 + 1 + 2 * i)
                        a, b = (x[:, bass.ds(2 * i + j // 2, 1)].rearrange("p a t -> p (a t)") if not first
                                else x[:, j // 2] for x in (hid_lo, hid_hi))
                        nc.vector.tensor_tensor(a, work[:, j // 2], b.bitcast(F32), ALU.subtract).then_inc(hid_l, 1)
            two(0, True)
            with dve.Fori(1, KF // 2) as i:
                two(i, False)

        def ada_at(n):
            return Nth(S_WOUT + 4 * (n // 3) + n % 3), Nth(G_WOUT + ADA_G[n // 4])

        def pe_ada(pe, step):
            for n in range(3 * step, 3 * step + 3):
                st, g = ada_at(n)
                pe.wait_ge(lo_ready, st.n + 1)
                if n == 0:
                    pe.wait_ge(cond_split, 1)
                if n % 4 == 0:
                    ge(pe, proj_read[g.slot], g.turn)
                for kk in range(2):
                    k = 2 * (n % 4) + kk
                    for half in (w_hi, w_lo):
                        mm = nc.tensor.matmul(proj[0:4, g.slot], cond4[:, k], half[:, st.slot, kk * W5:(kk + 1) * W5],
                                              start=(k == 0 and half is w_hi), stop=(k == KD - 1 and half is w_lo))
                mm.then_inc(strip_done, 1)

        def pe_ada_turn(pe, a):
            _, g = ada_at(4 * a)
            pe.wait_ge(proj_read[g.slot], g.turn + 1)
            ge(pe, ada_out, a)
            for n in range(4):
                mm = nc.tensor.matmul(aux[:, 3, 2 * n:2 * n + 2], mod_row[0:4, n * P:(n + 1) * P], pair_sum[0:4],
                                      start=True, stop=True)
            mm.then_inc(ada_turned, 1)

        def dve_ada(dve, step):
            for n in range(3 * step, 3 * step + 3):
                st, g = ada_at(n)
                if n % 3:
                    split_lo(dve, st.plus(3))
                if n % 4 == 3:
                    res = result(dve, st, g)
                    ge(dve, ada_turned, n // 4)
                    nc.vector.tensor_copy(mod_row[0:4], res[0:4]).then_inc(proj_read[g.slot], 1)

        def dve_ada_take(dve, a):
            dve.wait_ge(ada_turned, a + 1)
            nc.vector.tensor_tensor(modv[:, 4 * a:4 * a + 4], aux[:, 3, 0:8].rearrange("p (n t) -> p n t", t=2),
                                    col("b_ada", 4 * a, 4).unsqueeze(2).to_broadcast([P, 4, 2]),
                                    ALU.add).then_inc(ada_out, 1)

        def act_only_splits(act, s0, lo, hi):
            for n in range(lo, hi):
                split_hi(act, Nth(s0 + n + 3))

        def dve_only_splits(dve, s0, lo, hi):
            for n in range(lo, hi):
                split_lo(dve, Nth(s0 + n + 3))

        MIX_ORDER = [0, 1, 4, 5, 2, 3, 6, 7]

        def mixed(k):
            return mb[:, k] if k < HH else su[:, k - HH]

        def halves(x, lev):
            n = 1 << lev
            flat = x.rearrange("p h t -> p (h t)")
            v = flat.rearrange("p (b two n) -> p b two n", two=2, n=n)
            return v[:, :, 0, :], v[:, :, 1, :]

        def level_ref(lev):
            n = 1 << lev
            lower, _ = halves(mb[:], lev)
            return lower[:, :, n - 1:n].to_broadcast([P, HH * T // (2 * n), n])

        def pe_level(pe, lev):
            if lev < LEVELS:
                pe.wait_ge(l_fac, lev + 1)
                pe.wait_ge(l_lowk, lev + 1)
            for cc in range(TB):
                for hd in range(HH):
                    if lev < LEVELS:
                        f = qk[:, lev % 2, hd, cc * P:(cc + 1) * P]
                        upper = f.rearrange("p (b two n) -> p b two n", two=2, n=1 << lev)[:, :, 1, :]
                        if cc % 2 == 0 and hd == 0 and lev:
                            pe.wait_ge(l_put, 2 * lev - 1 + cc // 2)
                        mm = nc.tensor.matmul(aux[:, cc // 2, (cc % 2) * 256 + hd * 64:(cc % 2) * 256 + hd * 64 + 64],
                                              f, upper, start=True, stop=True)
                        if cc % 2 and hd == HH - 1:
                            mm.then_inc(l_mm, 1)
                    else:
                        if cc < 2 and hd == 0:
                            pe.wait_ge(l_put, 2 * LEVELS - 1 + cc)
                        at = slice(cc * P, (cc + 1) * P)
                        mm = nc.tensor.matmul(aux[:, cc, hd * P:(hd + 1) * P], mk[:, hd, at], mq[:, hd, at],
                                              start=True, stop=True)
                        if hd == HH - 1:
                            mm.then_inc(l_mm, 1)

        def dve_put(dve, lev):
            if lev == 0:
                dve.wait_ge(m_zero, 1)
                dve.wait_ge(in_mask, 16 * 4)
            if lev < LEVELS:
                nb, n = P >> (lev + 1), 1 << lev
                for half in range(2):
                    dve.wait_ge(l_mm, 2 * lev + half + 1)
                    dst = score[:, 2 * half:2 * half + 2].rearrange("p c h (b two n) -> p (c h) b two n", two=2,
                                                                    n=n)[:, :, :, 1, :]
                    mask = levmask[:, lev].rearrange("p (b n) -> p b n", n=n).unsqueeze(1).to_broadcast(
                        [P, 2 * HH, nb, n])
                    data = aux[:, half].rearrange("p (c b n) -> p c b n", b=nb, n=n)
                    nc.vector.copy_predicated(dst, mask, data).then_inc(l_put, 1)
            else:
                for cc in range(TB):
                    dve.wait_ge(l_mm, 2 * LEVELS + cc + 1)
                    nc.vector.copy_predicated(score[:, cc], idmask[:].unsqueeze(1).to_broadcast([P, HH, P]),
                                              aux[:, cc].rearrange("p (h t) -> p h t", h=HH)).then_inc(l_put, 1)

        def dve_level(dve, lev):
            blo, bup = halves(mb[:], lev)
            dlo, dup = halves(md[:], lev)
            if lev >= 1:
                dve.wait_ge(l_lowk, lev)
                dve.wait_ge(l_fac, lev)
            if lev == 0:
                dve.wait_ge(m_b, HH)
            nc.vector.tensor_tensor(dlo, level_ref(lev), blo, ALU.subtract).then_inc(l_diff, 1)
            nc.vector.tensor_tensor(dup, bup, level_ref(lev), ALU.subtract).then_inc(l_diff, 1)

        def dve_level_mul(dve, lev):
            dve.wait_ge(l_exp, lev + 1)
            if lev >= 2:
                dve.wait_ge(l_mm, 2 * (lev - 1))
            _, dup = halves(md[:], lev)
            _, fup = halves(qk[:, lev % 2], lev)
            _, qup = halves(mq[:], lev)
            nc.vector.tensor_tensor(fup, dup, qup, ALU.mult).then_inc(l_fac, 1)

        def pool_level_mul(pool, lev):
            pool.wait_ge(l_exp, lev + 1)
            if lev == 0:
                pool.wait_ge(m_k, HH)
            if lev >= 2:
                pool.wait_ge(l_mm, 2 * (lev - 1))
            dlo, _ = halves(md[:], lev)
            flo, _ = halves(qk[:, lev % 2], lev)
            klo, _ = halves(mk[:], lev)
            nc.gpsimd.tensor_tensor(flo, dlo, klo, ALU.mult).then_inc(l_lowk, 1)

        def act_level(act, lev):
            act.wait_ge(l_diff, 2 * (lev + 1))
            nc.scalar.activation(md[:], md[:], ACT.Exp).then_inc(l_exp, 1)

        def pe_mix(pe):
            for i in range(24):
                st = Nth(S_MIX + i)
                if 8 <= i < 16:
                    g0 = G_MIX + (i // 4) * 4
                    token_strip(pe, st, i % 4, [Nth(g0 + t) for t in range(TB)], a_hi, a_lo)
                elif i == 0:
                    strip_pair(pe, st, Nth(G_MIX), a_hi, a_lo, lo_ready_of(pe, LN1))
                elif i > 1:
                    feature_strip(pe, st, Nth(G_MIX + i), a_hi, a_lo)
                if 7 <= i <= 14:
                    pe_level(pe, i - 7)
                if i == 15:
                    for cc in range(TB - 1):
                        if cc == 0:
                            pe.wait_ge(i_ke, 1)
                            pe.wait_ge(l_put, 2 * LEVELS + TB)
                        for hd in range(HH):
                            mm = nc.tensor.transpose(aux[:, cc, hd * P:(hd + 1) * P],
                                                     qk[:, 1, hd, cc * P:(cc + 1) * P], ident)
                        mm.then_inc(i_tr, 1)
                if i == 16:
                    ket = md[:, 0:3].rearrange("p c (h d) -> p c h d", h=HH)
                    for cc in range(TB - 1):
                        pe.wait_ge(i_ket, 3)
                        for hd in range(HH):
                            mm = nc.tensor.matmul(aux[:, cc, hd * P:(hd + 1) * P], ket[:, cc, hd],
                                                  mv[:, cc, hd * P:(hd + 1) * P], start=True, stop=True)
                        mm.then_inc(i_kv, 1)
                if i == 18:
                    pe.wait_ge(i_qe, 1)
                    pe.wait_ge(i_state, 9)
                    state = mk[:, 0:3].rearrange("p c (h d) -> p c h d", h=HH)
                    for hd in range(HH):
                        for cc in range(TB):
                            o = aux[:, hd, cc * P:(cc + 1) * P]
                            mm = nc.tensor.matmul(o, mv[:, cc, hd * P:(hd + 1) * P], score[:, cc, hd], start=True,
                                                  stop=(cc == 0))
                            if cc:
                                mm = nc.tensor.matmul(o, state[:, cc - 1, hd], qk[:, 0, hd, cc * P:(cc + 1) * P],
                                                      start=False, stop=True)
                        mm.then_inc(i_o, 1)
                if i == 19:
                    for hd in range(HH):
                        pe.wait_ge(i_osq, hd + 1)
                        nc.tensor.matmul(aux[:, hd], mean_p[:], mq[:, hd], start=True, stop=True).then_inc(i_ms, 1)
                if i == 21:
                    pe.wait_ge(v_gain, 2)
                    pe.wait_ge(w_masked, 1)
                    for g in range(HH):
                        pe.wait_ge(i_std, g + 1)
                        for t in range(TB):
                            mm = nc.tensor.matmul(aux[:, g, t * P:(t + 1) * P], sv[:, t, g * P:(g + 1) * P], wst[:, g],
                                                  start=True, stop=True)
                        mm.then_inc(v_mm, 1)

        def act_mix(act, chain):
            def mix_hi_of(n):
                k = MIX_ORDER[n]
                if k < HH:
                    act.wait_ge(mix_raw, k + 1)
                else:
                    act.wait_ge(v_out, 2 * (k - HH + 1))
                nc.scalar.activation(mix_h[:, k], mixed(k), ACT.Copy).then_inc(mix_hi, 1)

            for i in range(24):
                st, g = Nth(S_MIX + i), Nth(G_MIX + i)
                split_hi(act, st.plus(3))
                if i < 4:
                    res = result(act, st, g)
                    nc.scalar.activation(md[:, i], res, ACT.Sigmoid).then_inc(m_sig, 1)
                    nc.scalar.activation(mk[:, i], res, ACT.Sigmoid, scale=-1.0).then_inc(proj_read[g.slot], 1)
                if i == 3:
                    act.wait_ge(m_f, HH)
                    nc.scalar.activation(md[:], md[:], ACT.Ln).then_inc(m_lf, 1)
                if 4 <= i < 8:
                    res = result(act, st, g)
                    nc.scalar.activation(mq[:, i - 4], res, ACT.Copy).then_inc(proj_read[g.slot], 1)
                if 6 <= i < 13:
                    act_level(act, i - 6)
                if i == 11:
                    for t in range(TB):
                        gt = Nth(G_MIX + 8 + t)
                        nc.scalar.activation(mv[:, t], result(act, st, gt), ACT.Copy).then_inc(proj_read[gt.slot], 1)
                if i == 13:
                    act.wait_ge(i_diff, 1)
                    nc.scalar.activation(md[:], md[:], ACT.Exp).then_inc(i_expd, 1)
                    nc.scalar.activation(mb[:], mb[:], ACT.Exp).then_inc(i_expb, 1)
                if i == 15:
                    for t in range(TB):
                        gt = Nth(G_MIX + 12 + t)
                        nc.scalar.activation(sv[:, t], result(act, st, gt),
                                             ACT.Gelu_apprx_tanh).then_inc(proj_read[gt.slot], 1)
                if i == 16:
                    for cc in range(TB - 1):
                        act.wait_ge(i_tr, cc + 1)
                        if cc == 0:
                            act.wait_ge(i_ke, 1)
                        nc.scalar.activation(md[:, cc], aux[:, cc], ACT.Copy).then_inc(i_ket, 1)
                if 16 <= i < 20:
                    res = result(act, st, g)
                    nc.scalar.activation(su[:, i - 16], res, ACT.Gelu_apprx_tanh).then_inc(proj_read[g.slot], 1)
                if i == 17:
                    act.wait_ge(v_var, 16)
                    nc.scalar.activation(vstd[:, 0], bnag[:, :, 1], ACT.Sqrt, bias=eps_c[:, 1:2]).then_inc(v_std, 1)
                if i == 19:
                    for hd in range(HH):
                        act.wait_ge(i_o, hd + 1)
                        nc.scalar.activation(mb[:, hd], aux[:, hd], ACT.Copy).then_inc(i_copy, 1)
                        nc.scalar.activation(mq[:, hd], aux[:, hd], ACT.Square).then_inc(i_osq, 1)
                if i == 20:
                    nc.scalar.preload_act_table_set(LN_EXP)
                    for hd in range(HH):
                        act.wait_ge(i_ms, hd + 1)
                        inverse_root(chain, qk[:, 1, hd], aux[:, hd], 1).then_inc(i_std, 1)
                if i == 23:
                    for n in (1, 2, 3):
                        mix_hi_of(n)
                if i >= 20:
                    res = result(act, st, g)
                    nc.scalar.activation(mk[:, i - 20], res, ACT.Silu).then_inc(proj_read[g.slot], 1)
                if i == 22:
                    mix_hi_of(0)
            split_hi(act, Nth(S_WOUT + 3))
            for n in range(4, KD):
                mix_hi_of(n)

        def dve_mix(dve, chain):
            link = chain.link

            def mix_lo_of(k):
                dve.wait_ge(mix_hi, MIX_ORDER.index(k) + 1)
                nc.vector.tensor_tensor(mix_l[:, k], mixed(k), mix_h[:, k].bitcast(F32),
                                        ALU.subtract).then_inc(mix_lo, 1)

            def gating(gg):
                dve.wait_ge(v_mm, gg + 1)
                gu = Nth(G_MIX + 16 + gg)
                dve.wait_ge(proj_read[gu.slot], gu.turn + 1)
                dst = aux[:, gg].rearrange("p (c t) -> p c t", c=TB)
                nc.vector.tensor_tensor(dst, dst, rows[:, 2, gg * P:(gg + 1) * P].unsqueeze(1).to_broadcast(
                    [P, TB, P]), ALU.add).then_inc(v_out, 1)
                dve.wait_ge(v_out, 2 * gg + 1)
                nc.vector.tensor_tensor(su[:, gg], su[:, gg], aux[:, gg], ALU.mult).then_inc(v_out, 1)

            for i in range(24):
                st, g = Nth(S_MIX + i), Nth(G_MIX + i)
                split_lo(dve, st.plus(3))
                if i < 4:
                    dve.wait_ge(m_sig, i + 1)
                    nc.vector.tensor_scalar(md[:, i], md[:, i], lbv[:, 5, i:i + 1], lbv[:, 4, i:i + 1], ALU.mult,
                                            ALU.add).then_inc(m_f, 1)
                    dve.wait_ge(proj_read[g.slot], g.turn + 1)
                    nc.vector.tensor_scalar(mk[:, i], mk[:, i], lbv[:, 5, i:i + 1], None, ALU.mult).then_inc(m_k, 1)
                if i == 4:
                    dve.wait_ge(m_lf, 1)
                    dve.wait_ge(m_fresh, 2)
                    for hd in range(HH):
                        nc.vector.tensor_tensor_scan(mb[:, hd], work[:, 0], md[:, hd], 0.0, ALU.mult,
                                                     ALU.add).then_inc(m_b, 1)
                if 8 <= i <= 14:
                    dve_put(dve, i - 8)
                if 6 <= i < 13:
                    dve_level(dve, i - 6)
                    if i == 6:
                        gq = Nth(G_MIX + 7)
                        dve.wait_ge(proj_read[gq.slot], gq.turn + 1)
                    dve_level_mul(dve, i - 6)
                if i == 13:
                    dve.wait_ge(l_lowk, LEVELS)
                    dve.wait_ge(l_fac, LEVELS)
                    bh = mb[:].rearrange("p h (c t) -> p (h c) t", c=TB)
                    nc.vector.tensor_tensor(md[:].rearrange("p h (c t) -> p (h c) t", c=TB),
                                            bh[:, :, P - 1:P].to_broadcast([P, HH * TB, P]), bh,
                                            ALU.subtract).then_inc(i_diff, 1)
                    dve.wait_ge(i_expd, 1)
                    dve.wait_ge(l_mm, 2 * 6)
                    nc.vector.tensor_tensor(qk[:, 1], mk[:], md[:], ALU.mult).then_inc(i_ke, 1)
                if i == 14:
                    dve.wait_ge(i_expb, 1)
                    dve.wait_ge(l_mm, 2 * 7)
                    link(nc.vector.tensor_copy(decay[:], mb[:].rearrange("p h (c t) -> p h c t", c=TB)[:, :, :, P - 1]))
                    nc.vector.tensor_tensor(qk[:, 0], mq[:], mb[:], ALU.mult).then_inc(i_qe, 1)
                if i == 15:
                    dve_put(dve, LEVELS)
                if i == 16:
                    for t in range(TB):
                        dve.wait_ge(proj_read[Nth(G_MIX + 12 + t).slot], Nth(G_MIX + 12 + t).turn + 1)
                        for gg in range(HH):
                            last = nc.vector.bn_stats(bnst[:, 4 * t + gg], sv[:, t, gg * P:(gg + 1) * P])
                    link(last)
                    for n in range(16):
                        nc.vector.bn_aggr(bnag[:, n], bnst[:, n]).then_inc(v_var, 1)
                if i == 17:
                    state = mk[:, 0:3].rearrange("p c (h d) -> p c h d", h=HH)
                    for cc in range(TB - 1):
                        dve.wait_ge(i_kv, cc + 1)
                        if cc == 0:
                            nc.vector.tensor_copy(mk[:, 0], aux[:, 0]).then_inc(i_state, 1)
                        else:
                            dve.wait_ge(i_state, 4 * cc - 3)
                            for hd in range(HH):
                                nc.vector.scalar_tensor_tensor(state[:, cc, hd], state[:, cc - 1, hd],
                                                               decay[:, hd, cc:cc + 1],
                                                               aux[:, cc, hd * P:(hd + 1) * P], ALU.mult,
                                                               ALU.add).then_inc(i_state, 1)
                    dve.wait_ge(v_std, 1)
                    link(nc.vector.reciprocal(vstd[:, 1], vstd[:, 0]))
                if i in (18, 19):
                    for t in range(2 * (i - 18), 2 * (i - 18) + 2):
                        for gg in range(HH):
                            n = 4 * t + gg
                            nc.vector.tensor_scalar(sv[:, t, gg * P:(gg + 1) * P], sv[:, t, gg * P:(gg + 1) * P],
                                                    bnag[:, n, 0:1], vstd[:, 1, n:n + 1], ALU.subtract,
                                                    ALU.mult).then_inc(v_norm, 1)
                if i >= 20:
                    hd = i - 20
                    dve.wait_ge(i_std, hd + 1)
                    dve.wait_ge(i_copy, hd + 1)
                    nc.vector.scalar_tensor_tensor(mb[:, hd], mb[:, hd], col("hg_g"), qk[:, 1, hd], ALU.mult,
                                                   ALU.mult).then_inc(i_on, 1)
                if i == 22:
                    gating(0)
                    gating(1)
            gating(2)
            split_lo(dve, Nth(S_WOUT + 3))
            dve.wait_ge(v_mm, HH)
            mix_lo_of(4)
            mix_lo_of(5)
            gating(3)
            mix_lo_of(6)
            mix_lo_of(7)

        def pool_mix(pool):
            pool.wait_ge(hid_l, KF)
            pool.wait_ge(strip_done, S_MIX)
            nc.gpsimd.memset(score[:].rearrange("p c h t -> p (c h t)"), 0.0).then_inc(m_zero, 1)
            pool.wait_ge(n_mean, 1)
            nc.gpsimd.memset(work[:, 0], 1.0).then_inc(m_fresh, 1)
            pool.wait_ge(m_fresh, 1)
            nc.gpsimd.memset(work[:, 0, 0:T:P], 0.0).then_inc(m_fresh, 1)
            for dst, src in ((levmask[:].rearrange("p l t -> p (l t)"), mask_in[:, 0:LEVELS * 64]),
                             (idmask[:], mask_in[:, LEVELS * 64:]),
                             (wst[:].rearrange("p g t -> p (g t)"), wst_in),
                             (rows[:].rearrange("p a t -> p (a t)"), rows_in.partition_broadcast(P))):
                pool.dma_start(dst, src).then_inc(in_mask, 16)
            pool.wait_ge(in_mask, 16 * 4)
            nc.gpsimd.affine_select(out=wst[:], in_=wst[:], compare_op=ALU.is_ge, fill=0.0, base=0,
                                    pattern=[[0, HH], [1, P]], channel_multiplier=-1).then_inc(w_masked, 1)
            for lev in range(LEVELS):
                pool_level_mul(pool, lev)
            for n in range(2):
                pool.wait_ge(v_norm, 16)
                if n:
                    pool.wait_ge(v_gain, 1)
                nc.gpsimd.tensor_tensor(sv[:], sv[:], rows[:, n].unsqueeze(1).to_broadcast([P, TB, W5]),
                                        (ALU.mult, ALU.add)[n]).then_inc(v_gain, 1)
            for hd in range(HH + 1):
                if hd < HH:
                    gh = Nth(G_MIX + 20 + hd)
                    pool.wait_ge(i_on, hd + 1)
                    pool.wait_ge(proj_read[gh.slot], gh.turn + 1)
                    nc.gpsimd.tensor_tensor(mb[:, hd], mb[:, hd], mk[:, hd], ALU.mult).then_inc(mix_raw, 1)
                if hd:
                    pool.wait_ge(mix_hi, MIX_ORDER.index(hd - 1) + 1)
                    nc.gpsimd.tensor_tensor(mix_l[:, hd - 1], mb[:, hd - 1], mix_h[:, hd - 1].bitcast(F32),
                                            ALU.subtract).then_inc(mix_lo_pool, 1)

        MEM_PARTS, MEM_HI_PARTS = [(0, 2), (2, 4), (4, 6), (6, 9)], [(0, 2), (2, 4), (4, 6), (6, 8)]

        def pe_memkv(pe, lo, hi):
            for n in range(lo, hi):
                if n < KD:
                    feature_strip(pe, Nth(S_MEMK + n), Nth(G_MEMK + n), side_hi, side_lo, n=M,
                                  ready=lo_ready_of(pe, MEMN) if n == 0 else None)
                else:
                    half = (n - KD) // 4
                    token_strip(pe, Nth(S_MEMK + n), n % 4, [Nth(G_MEMV + MB * half + t) for t in range(MB)],
                                side_hi, side_lo)

        def act_memkv(act, lo, hi):
            for n in range(lo, hi):
                st = Nth(S_MEMK + n)
                if n:
                    split_hi(act, st.plus(3))
                if n < KD:
                    g = Nth(G_MEMK + n)
                    nc.scalar.activation(memk[:, n], result(act, st, g)[:, :M],
                                         ACT.Copy).then_inc(proj_read[g.slot], 1)
                elif n % 4 == 3:
                    half = (n - KD) // 4
                    for t in range(MB):
                        g = Nth(G_MEMV + MB * half + t)
                        nc.scalar.activation(memv[:, t, half * W5:(half + 1) * W5], result(act, st, g),
                                             ACT.Copy).then_inc(proj_read[g.slot], 1)

        def pe_attention(pe):
            def scores(u):
                hd, pr = u // 2, u % 2
                if u >= 2:
                    pe.wait_ge(a_exp, 2 * (u - 1))
                if u == 0:
                    for n in range(KD - RING, KD):
                        g = Nth(G_XQ + n)
                        pe.wait_ge(proj_read[g.slot], g.turn + 1)
                for t in range(2):
                    for kk in range(2):
                        at = (2 * pr + t) * P
                        mm = nc.tensor.matmul(aux[:, u % 2, t * M:(t + 1) * M], xq[:, 2 * hd + kk, at:at + P],
                                              memk[:, 2 * hd + kk], start=(kk == 0), stop=(kk == 1))
                mm.then_inc(a_sc, 1)

            def turn(u):
                pe.wait_ge(a_norm, 2 * u + 2)
                if u >= 2:
                    pe.wait_ge(a_pt, u - 1)
                for mt in range(MB):
                    for t in range(2):
                        mm = nc.tensor.transpose(aux[:, 2 + u % 2, (2 * mt + t) * P:(2 * mt + t + 1) * P],
                                                 xp[:, u % 2, t, mt * P:(mt + 1) * P], ident)
                mm.then_inc(a_tr, 1)

            def values(u):
                pe.wait_ge(a_pt, u + 1)
                g = Nth(G_PV + u)
                ge(pe, proj_read[g.slot], g.turn)
                for dk in range(2):
                    for mt in range(MB):
                        at = (2 * (u // 2) + dk) * P
                        mm = nc.tensor.matmul(proj[:, g.slot, dk * M:(dk + 1) * M], memv[:, mt, at:at + P],
                                              xpt[:, u % 2, mt], start=(mt == 0), stop=(mt == MB - 1))
                mm.then_inc(a_pv, 1)

            scores(0)
            scores(1)
            pe_ctxk(pe)
            for u in range(UNITS + 1):
                if u < UNITS:
                    turn(u)
                    if u + 2 < UNITS:
                        scores(u + 2)
                if u:
                    values(u - 1)

        def dve_attention(dve, chain):
            def top(u):
                dve.wait_ge(a_sc, u + 1)
                nc.vector.tensor_reduce(xs[:, 0, u], aux[:, u % 2].rearrange("p (t m) -> p t m", t=2), AX, ALU.max,
                                        negate=True).then_inc(a_max, 1)

            def norm(u):
                dve.wait_ge(a_exp, 2 * u + 2)
                chain.link(nc.vector.reciprocal(xs[:, 2, u], xs[:, 1, u]))
                for t in range(2):
                    nc.vector.tensor_scalar(xp[:, u % 2, t], xp[:, u % 2, t], xs[:, 2, u, t:t + 1], None,
                                            ALU.mult).then_inc(a_norm, 1)

            def take(u):
                dve.wait_ge(a_hi_s, u + 1)
                hd, pr = u // 2, u % 2
                dst = (x[:, 2 * hd:2 * hd + 2, pr * M:(pr + 1) * M] for x in (a_lo, a_hi))
                lo, hi = dst
                g = Nth(G_PV + u)
                nc.vector.tensor_tensor(lo, proj[:, g.slot].rearrange("p (d t) -> p d t", d=2), hi.bitcast(F32),
                                        ALU.subtract).then_inc(proj_read[g.slot], 1)

            top(0)
            top(1)
            norm(0)
            norm(1)
            dve_only_splits(dve, S_CTXK, 0, KW)
            for u in range(UNITS):
                if 2 <= u + 1 < UNITS:
                    top(u + 1)
                if u >= 2:
                    norm(u)
                if u >= 2:
                    take(u - 2)
            take(UNITS - 2)
            take(UNITS - 1)

        def act_attention(act):
            def exps(u):
                act.wait_ge(a_max, u + 1)
                if u >= 2:
                    act.wait_ge(a_tr, u - 1)
                for t in range(2):
                    nc.scalar.activation(xp[:, u % 2, t], aux[:, u % 2, t * M:(t + 1) * M], ACT.Exp,
                                         bias=xs[:, 0, u, t:t + 1],
                                         accum_out=xs[:, 1, u, t:t + 1]).then_inc(a_exp, 1)

            def turned(u):
                act.wait_ge(a_tr, u + 1)
                if u >= 2:
                    act.wait_ge(a_pv, u - 1)
                nc.scalar.activation(xpt[:, u % 2].rearrange("p m t -> p (m t)"), aux[:, 2 + u % 2],
                                     ACT.Copy).then_inc(a_pt, 1)

            def take(u):
                act.wait_ge(a_pv, u + 1)
                hd, pr = u // 2, u % 2
                nc.scalar.activation(a_hi[:, 2 * hd:2 * hd + 2, pr * M:(pr + 1) * M],
                                     proj[:, Nth(G_PV + u).slot].rearrange("p (d t) -> p d t", d=2),
                                     ACT.Copy).then_inc(a_hi_s, 1)

            exps(0)
            exps(1)
            act_ctxk(act)
            for u in range(UNITS):
                if 2 <= u + 1 < UNITS:
                    exps(u + 1)
                turned(u)
                if u >= 2:
                    take(u - 2)
            take(UNITS - 2)
            take(UNITS - 1)

        def pe_ctxk(pe):
            for n in range(KW):
                feature_strip(pe, Nth(S_CTXK + n), Nth(G_CTXK + n), side_hi, side_lo, n=M,
                              ready=lo_ready_of(pe, CTXN) if n == 0 else None)

        def act_ctxk(act):
            for n in range(KW):
                st, g = Nth(S_CTXK + n), Nth(G_CTXK + n)
                split_hi(act, st.plus(3))
                nc.scalar.activation(ksd[:, n], result(act, st, g)[:, :M], ACT.Square).then_inc(ck_sq, 1)
                nc.scalar.activation(ctxk[:, n], result(act, st, g)[:, :M], ACT.Copy).then_inc(proj_read[g.slot], 1)

        def pe_ctxk_norm(pe):
            pe.wait_ge(ck_sq, KW)
            for n in range(2):
                nc.tensor.matmul(aux[:, n], blk64, ksd[:, 2 * n:2 * n + 2].rearrange("p c t -> p (c t)"), start=True,
                                 stop=True).then_inc(ck_ms, 1)

        def act_ctxk_norm(act, chain):
            nc.scalar.preload_act_table_set(LN_EXP)
            for n in range(2):
                act.wait_ge(ck_ms, n + 1)
                inverse_root(chain, krs[:, 2 * n:2 * n + 2].rearrange("p c t -> p (c t)"), aux[:, n],
                             2).then_inc(ck_std, 1)

        def dve_ctxk_norm(dve):
            dve.wait_ge(ck_std, 2)
            dve.wait_ge(proj_read[Nth(G_CTXK + 3).slot], Nth(G_CTXK + 3).turn + 1)
            flat = [x[:].rearrange("p c t -> p (c t)") for x in (ctxk, krs)]
            nc.vector.scalar_tensor_tensor(flat[0], flat[0], col("kn_g"), flat[1], ALU.mult,
                                           ALU.mult).then_inc(ck_ready, 1)

        def pe_ctxv(pe, lo, hi):
            for n in range(lo, hi):
                token_strip(pe, Nth(S_CTXV + n), n, [Nth(G_CTXV + t) for t in range(MB)], side_hi, side_lo)

        def act_ctxv_take(act):
            for t in range(MB):
                g = Nth(G_CTXV + t)
                nc.scalar.activation(ctxv[:, t], result(act, Nth(S_CTXV + 3), g),
                                     ACT.Copy).then_inc(proj_read[g.slot], 1)

        NA_G = [0, 1, 2, 3, 4, 6, 6, 7, 8, 9, 10, 11]
        Q_MS = 5
        UN = 2 * NCB

        def na_st(j, i):
            return Nth(S_NA + j, NA_STRIPS, i)

        def na_g(j, i):
            return Nth(G_NA + j, NA_GROUPS, i)

        def grid(x, rows, at, n, r0=0):
            return x.rearrange("p (r c) -> p r c", c=GRID)[:, r0:r0 + rows, at:at + n]

        def pe_na(pe, i, first):
            def scores(u):
                cb, lo = u // 2, HD * (u % 2)
                part = slice(lo, lo + HD)
                if u == 0:
                    pe.wait_ge(na_k, 1 + i)
                    pe.wait_ge(na_q, 1 + i)
                    pe.wait_ge(na_vband, 2 + 2 * i)
                    pe.wait_ge(b_ctx, 2 + 2 * i)
                if u >= 2:
                    pe.wait_ge(u_exp, u - 1 + UN * i)
                q = nq[part, cb * P:(cb + 1) * P]
                nc.tensor.matmul(aux[:, u % 2, :M], q, grid(nk[part], ROWS, BAND_AT[cb], BAND), start=True, stop=True)
                nc.tensor.matmul(aux[:, u % 2, M:], q, ck_c[part], start=True, stop=True).then_inc(u_sc, 1)

            def turn(u):
                pe.wait_ge(u_norm, u + 1 + UN * i)
                if u or not first:
                    pe.wait_ge(u_pt, u + UN * i)
                for b in range(4):
                    mm = nc.tensor.transpose(aux[:, 2, b * P:(b + 1) * P], npr[:, u % 2, b * P:(b + 1) * P], ident)
                mm.then_inc(u_tr, 1)

            def values(u):
                cb, lo = u // 2, HD * (u % 2)
                pe.wait_ge(u_pt, u + 1 + UN * i)
                if u == 0 and not first:
                    pe.wait_ge(na_ya, i)
                for b in range(4):
                    v = vband[:, 2 * cb + b, lo:lo + HD] if b < 2 else cv_c[:, b - 2, lo:lo + HD]
                    mm = nc.tensor.matmul(aux[lo:lo + HD, 3, cb * P:(cb + 1) * P], v, npt[:, u % 2, b * P:(b + 1) * P],
                                          start=(b == 0), stop=(b == 3))
                mm.then_inc(u_pv, 1)

            for j in range(NA_STRIPS):
                st, g = na_st(j, i), na_g(NA_G[j], i)
                if j in (5, 6):
                    feature_strip(pe, st, g, a_hi, a_lo, first=4 * (j - 5), blocks=4, last=(j == 6))
                elif first and j == 0:
                    strip_pair(pe, st, g, a_hi, a_lo, lo_ready_of(pe, MODN))
                elif not (first and j == 1):
                    feature_strip(pe, st, g, a_hi, a_lo)
                if j == 3:
                    pe.wait_ge(na_ksq, 1 + i)
                    nc.tensor.matmul(aux[:, 2], blk64, nsq[:, 0], start=True, stop=True).then_inc(na_kms, 1)
                if j == 4:
                    gq = na_g(Q_MS, i)
                    pe.wait_ge(na_qsq, 1 + i)
                    pe.wait_ge(proj_read[gq.slot], gq.turn)
                    nc.tensor.matmul(proj[:, gq.slot], blk64, nsq[:, 1], start=True, stop=True).then_inc(na_kms, 1)
                if j == 5:
                    pe.wait_ge(proj_read[na_g(NA_G[4], i).slot], na_g(NA_G[4], i).turn + 1)
                    for n in range(2 * NCB):
                        mm = nc.tensor.transpose(aux[:, n // 4, (n % 4) * P:(n % 4 + 1) * P],
                                                 nvt[:, n], ident)
                        if n % 4 == 3:
                            mm.then_inc(na_vb, 1)
                a = 2 * (j - 7)
                if 7 <= j <= 10:
                    turn(a)
                if 8 <= j <= 11:
                    values(a - 2)
                    values(a - 1)
                if 6 <= j <= 9:
                    scores(a + 2)
                if 7 <= j <= 10:
                    turn(a + 1)
                if 6 <= j <= 9:
                    scores(a + 3)

        def chunk(x, i):
            return x[:, i] if isinstance(i, int) else x[:, bass.ds(i, 1)].rearrange("p a t -> p (a t)")

        def act_na(act, i, first, chain):
            def exps(u):
                act.wait_ge(u_max, u + 1 + UN * i)
                if u >= 2 or not first:
                    act.wait_ge(u_tr, u - 1 + UN * i)
                nc.scalar.activation(npr[:, u % 2], aux[:, u % 2], ACT.Exp, bias=ns[:, 0, u:u + 1],
                                     accum_out=ns[:, 1, u:u + 1]).then_inc(u_exp, 1)

            def turned(u):
                act.wait_ge(u_tr, u + 1 + UN * i)
                if u >= 2 or not first:
                    act.wait_ge(u_pv, u - 1 + UN * i)
                nc.scalar.activation(npt[:, u % 2], aux[:, 2], ACT.Copy).then_inc(u_pt, 1)

            def take(j, dst, func=ACT.Copy):
                g = na_g(NA_G[j], i)
                nc.scalar.activation(dst, result(act, na_st(j, i), g), func).then_inc(proj_read[g.slot], 1)

            for j in range(NA_STRIPS):
                st, g = na_st(j, i), na_g(NA_G[j], i)
                split_hi(act, st.plus(3))
                a = 2 * (j - 7)
                if 7 <= j <= 10:
                    turned(a)
                if j == 0:
                    if not first:
                        act.wait_ge(na_conv_b, i)
                    take(0, nat[:])
                if j == 1:
                    take(1, nsg[:], ACT.Sigmoid)
                    nc.scalar.preload_act_table_set(LN_EXP)
                if j == 2:
                    res = result(act, st, g)
                    if not first:
                        act.wait_ge(u_sc, UN * i)
                        act.wait_ge(na_kms, 2 * i)
                    nc.scalar.activation(nsq[:, 0], res, ACT.Square).then_inc(na_ksq, 1)
                    take(2, nk[:])
                if j == 3:
                    res = result(act, st, g).rearrange("p (r b q) -> p r b q", b=NCB, q=QC)
                    by_block = [x.rearrange("p (b r q) -> p r b q", b=NCB, q=QC) for x in (nsq[:, 1], nq[:])]
                    nc.scalar.activation(by_block[0], res, ACT.Square).then_inc(na_qsq, 1)
                    nc.scalar.activation(by_block[1], res, ACT.Copy).then_inc(proj_read[g.slot], 1)
                if j == 4:
                    act.wait_ge(na_kms, 1 + 2 * i)
                    inverse_root(chain, nsq[:, 0], aux[:, 2], 2).then_inc(na_kstd, 1)
                    res = result(act, st, g)
                    if not first:
                        act.wait_ge(na_vb, 2 * i)
                    for cb in range(NCB):
                        dst = nvt[:, 2 * cb:2 * cb + 2].rearrange("p b (r c) -> p (b r) c", c=BAND)
                        ins = nc.scalar.activation(dst, grid(res, ROWS, BAND_AT[cb], BAND), ACT.Copy)
                    ins.then_inc(proj_read[g.slot], 1)
                if j == 5:
                    gq = na_g(Q_MS, i)
                    act.wait_ge(na_kms, 2 + 2 * i)
                    inverse_root(chain, nsq[:, 1], proj[:, gq.slot], 2).then_inc(proj_read[gq.slot], 1)
                    for n in range(2):
                        act.wait_ge(na_vb, n + 1 + 2 * i)
                        nc.scalar.activation(vband[:, 4 * n:4 * n + 4].rearrange("p b d -> p (b d)"),
                                             aux[:, n], ACT.Copy).then_inc(na_vband, 1)
                if j == 6:
                    take(6, chunk(zc, i))
                if j == 7:
                    if not first:
                        act.wait_ge(na_ya, i)
                        act.wait_ge(na_yb, i)
                    take(7, nza[:])
                if j == 8:
                    take(8, nbg[:])
                if j == 9:
                    take(9, ncg[:])
                if j == 11:
                    take(11, nzb[:])
                if 7 <= j <= 10:
                    turned(a + 1)
                if 6 <= j <= 9:
                    exps(a + 2)
                    exps(a + 3)
                if j == 11:
                    for z in (7, 11):
                        gz = na_g(NA_G[z], i)
                        act.wait_ge(proj_read[gz.slot], gz.turn + 1)
                    nc.scalar.activation(nza[:], nza[:], ACT.Silu).then_inc(na_silu, 1)
                    nc.scalar.activation(nzb[:], nzb[:], ACT.Silu).then_inc(na_silu, 1)

        CONV_TAPS = {2: 5, 3: 5, 4: 4, 5: 2, 6: 3, 7: 4, 8: 4, 9: 4}

        def conv_start(c):
            at = COLS["conf_w"][0]
            if isinstance(c, int):
                return cols[:, at + TAPS * c:at + TAPS * (c + 1)], col("conf_b", c)
            return cols[:, bass.ds(at + TAPS * c, TAPS)], cols[:, bass.ds(COLS["conf_b"][0] + c, 1)]

        def dve_conv(dve, c, step, chain):
            dst = chunk(y[:, 2], c)
            if step == min(CONV_TAPS):
                w, b = conv_start(c)
                chain.link(nc.vector.tensor_copy(wtap[:, :TAPS], w))
                chain.link(nc.vector.tensor_copy(wtap[:, TAPS:TAPS + 1], b))
                dve.wait_ge(na_glu, c + 1)
            t0 = sum(n for s, n in CONV_TAPS.items() if s < step)
            for tap in range(t0, t0 + CONV_TAPS[step]):
                src = glu[:, tap:tap + T]
                if tap == 0:
                    ins = nc.vector.tensor_scalar(dst, src, wtap[:, 0:1], wtap[:, TAPS:TAPS + 1], ALU.mult, ALU.add)
                else:
                    ins = nc.vector.scalar_tensor_tensor(dst, src, wtap[:, tap:tap + 1], dst, ALU.mult, ALU.add)
                if tap == TAPS - 1:
                    ins.then_inc(na_conv, 1)
                else:
                    chain.link(ins)

        def dve_na(dve, i, first, chain):
            link = chain.link

            def top(u):
                dve.wait_ge(u_sc, u + 1 + UN * i)
                if u == 0:
                    dve.wait_ge(b_ready, 6 + 6 * i)
                kind = BIAS_KIND[u // 2]
                link(nc.vector.tensor_tensor(aux[:, u % 2, :M], aux[:, u % 2, :M], bias[:, u % 2, kind], ALU.add))
                nc.vector.tensor_reduce(ns[:, 0, u:u + 1], aux[:, u % 2], AX, ALU.max, negate=True).then_inc(u_max, 1)

            def norm(u):
                dve.wait_ge(u_exp, u + 1 + UN * i)
                link(nc.vector.reciprocal(ns[:, 2, u:u + 1], ns[:, 1, u:u + 1]))
                nc.vector.tensor_scalar(npr[:, u % 2], npr[:, u % 2], ns[:, 2, u:u + 1], None,
                                        ALU.mult).then_inc(u_norm, 1)

            for j in range(NA_STRIPS):
                st, g = na_st(j, i), na_g(NA_G[j], i)
                if 7 <= j <= 10:
                    norm(2 * (j - 7))
                    norm(2 * (j - 7) + 1)
                split_lo(dve, st.plus(3))
                if j == 2:
                    ga, gg = na_g(NA_G[0], i), na_g(NA_G[1], i)
                    dve.wait_ge(proj_read[ga.slot], ga.turn + 1)
                    dve.wait_ge(proj_read[gg.slot], gg.turn + 1)
                    if first:
                        dve.wait_ge(b_edge, 2)
                    else:
                        dve.wait_ge(na_conv, i)
                    nc.vector.tensor_tensor(glu[:, TAPS // 2:TAPS // 2 + T], nat[:], nsg[:], ALU.mult)\
                        .then_inc(na_glu, 1)
                if j == 4:
                    dve.wait_ge(na_kstd, 1 + i)
                    gk = na_g(NA_G[2], i)
                    dve.wait_ge(proj_read[gk.slot], gk.turn + 1)
                    nc.vector.scalar_tensor_tensor(nk[:], nk[:], col("kn_g"), nsq[:, 0], ALU.mult,
                                                   ALU.mult).then_inc(na_k, 1)
                if j == 5:
                    gs, gq = na_g(Q_MS, i), na_g(NA_G[3], i)
                    dve.wait_ge(proj_read[gs.slot], gs.turn + 1)
                    dve.wait_ge(proj_read[gq.slot], gq.turn + 1)
                    nc.vector.scalar_tensor_tensor(nq[:], nq[:], qg8[:], nsq[:, 1], ALU.mult,
                                                   ALU.mult).then_inc(na_q, 1)
                if j in CONV_TAPS:
                    dve_conv(dve, i, j, chain)
                if 6 <= j <= 9:
                    top(2 * (j - 6))
                    top(2 * (j - 6) + 1)
                if j == 10:
                    res = result(dve, st, g)
                    gc = na_g(NA_G[9], i)
                    dve.wait_ge(proj_read[gc.slot], gc.turn + 1)
                    nc.vector.tensor_tensor(cv[:, 1:T + 1], ncg[:], res, ALU.mult).then_inc(proj_read[g.slot], 1)
                    dve.wait_ge(proj_read[g.slot], g.turn + 1)
                    at = COLS["short_w"][0]
                    w = col("short_w", 3 * i, 3) if first else cols[:, bass.ds(at + 3 * i, 3)]
                    link(nc.vector.tensor_copy(wtap[:, TAPS + 1:TAPS + 4], w))
                    acc = nat[:]
                    link(nc.vector.tensor_scalar(acc, cv[:, 0:T], wtap[:, TAPS + 1:TAPS + 2], None, ALU.mult))
                    for k in (1, 2):
                        link(nc.vector.scalar_tensor_tensor(acc, cv[:, k:k + T], wtap[:, TAPS + 1 + k:TAPS + 2 + k],
                                                            acc, ALU.mult, ALU.add))
                    nc.vector.tensor_tensor(nbg[:], nbg[:], acc, ALU.mult).then_inc(na_conv_b, 1)
                if j == 11:
                    dve.wait_ge(na_silu, 2 + 2 * i)
                    dve.wait_ge(na_conv_b, 1 + i)
                    nc.vector.tensor_tensor(chunk(y[:, 1], i), nbg[:], nzb[:], ALU.mult).then_inc(na_yb, 1)
                if j == 11:
                    dve.wait_ge(u_pv, UN + UN * i)
                    dst = chunk(y[:, 0], i).rearrange("p (r b q) -> p r b q", b=NCB, q=QC)
                    src = aux[:, 3].rearrange("p (b r q) -> p r b q", b=NCB, q=QC)
                    nc.vector.tensor_tensor(dst, src, nza[:].rearrange("p (r b q) -> p r b q", b=NCB, q=QC),
                                            ALU.mult).then_inc(na_ya, 1)

        def pool_na(pool, i, first):
            if not first:
                pool.wait_ge(u_max, UN * i)
            src = rpb_in[:, 2 * i:2 * i + 2] if first else rpb_in[:, bass.ds(2 * i, 2)]
            pool.dma_start(btab[:], src).then_inc(b_tab, 16)
            if not first:
                pool.wait_ge(u_pv, UN * i)
            nc.gpsimd.tensor_copy(ck_c[:], chunk(ctxk, i)).then_inc(b_ctx, 1)
            v = ctxv[:, :, P * i:P * (i + 1)] if first else ctxv[:, :, bass.ds(P * i, P)]
            nc.gpsimd.tensor_copy(cv_c[:], v).then_inc(b_ctx, 1)
            pool.wait_ge(b_tab, 16 + 16 * i)
            for hd in range(2):
                for kind in range(3):
                    tab = btab[:, hd].rearrange("p (r m) -> p r m", m=RPB_W)[:, :, BIAS_AT + BIAS_OFF[kind]:
                                                                             BIAS_AT + BIAS_OFF[kind] + BAND]
                    nc.gpsimd.tensor_tensor(bias[:, hd, kind].rearrange("p (r m) -> p r m", m=BAND), tab,
                                            band[:, kind].rearrange("p (r m) -> p r m", m=BAND),
                                            ALU.add).then_inc(b_ready, 1)

        def pe_merge(pe, i, first, fill=None):
            for q in range(RING):
                n = RING * i + q
                for j in range(MERGE_STRIPS):
                    st = Nth(S_MERGE + MERGE_STRIPS * q + j, RING * MERGE_STRIPS, i)
                    g = Nth(G_MERGE + MERGE_GROUPS * q + j, RING * MERGE_GROUPS, i)
                    if j < 3:
                        feature_strip(pe, st, g, a_hi, a_lo)
                        if fill and q == 0:
                            fill[j]()
                        continue
                    pe.wait_ge(lo_ready, st.n + 1)
                    for br in ((0, 1), (2,))[j - 3]:
                        gb = g if j == 3 and br == 0 else g.plus(1)
                        ge(pe, proj_read[gb.slot], gb.turn)
                        if first and q == 0:
                            pe.wait_ge(y_lo_s, KW * (br + 1))
                        for k in range(KW):
                            at = ((br % 2) * KW + k) * P
                            mm = product(proj[:, gb.slot], w_hi[:, st.slot, at:at + P], w_lo[:, st.slot, at:at + P],
                                         y_hi[:, KW * br + k], y_lo[:, KW * br + k], k == 0, k == KW - 1)
                    mm.then_inc(strip_done, 1)

        def act_merge(act, i, first, fill=None):
            for q in range(RING):
                n = RING * i + q
                for j in range(MERGE_STRIPS):
                    st = Nth(S_MERGE + MERGE_STRIPS * q + j, RING * MERGE_STRIPS, i)
                    g = Nth(G_MERGE + MERGE_GROUPS * q + j, RING * MERGE_GROUPS, i)
                    split_hi(act, st.plus(3))
                    if j < 3:
                        if fill and q == 0:
                            fill[j]()
                        if q or not first:
                            act.wait_ge(m_raw, n)
                        nc.scalar.activation(gate[:, j], result(act, st, g), ACT.Sigmoid)\
                            .then_inc(proj_read[g.slot], 1)
                act.wait_ge(m_raw, n + 1)
                nc.scalar.activation(chunk(m_hi, n), mrg[:, 0], ACT.Copy).then_inc(m_hi_s, 1)

        def dve_merge(dve, i, first, chain, fill=None):
            link = chain.link
            for q in range(RING):
                n = RING * i + q
                for j in range(MERGE_STRIPS):
                    st = Nth(S_MERGE + MERGE_STRIPS * q + j, RING * MERGE_STRIPS, i)
                    split_lo(dve, st.plus(3))
                    if fill and q == 0 and j < 3:
                        fill[j]()
                    if j < 3:
                        continue
                    for br in ((0, 1), (2,))[j - 3]:
                        gg = Nth(G_MERGE + MERGE_GROUPS * q + br, RING * MERGE_GROUPS, i)
                        gb = gg.plus(3)
                        dve.wait_ge(proj_read[gg.slot], gg.turn + 1)
                        res = result(dve, st, gb)
                        nc.vector.tensor_tensor(gate[:, br], gate[:, br], res, ALU.mult)\
                            .then_inc(proj_read[gb.slot], 1)
                        dve.wait_ge(proj_read[gb.slot], gb.turn + 1)
                        if br == 1:
                            link(nc.vector.tensor_tensor(mrg[:, 1], gate[:, 0], gate[:, 1], ALU.add))
                        if br == 2:
                            nc.vector.tensor_tensor(mrg[:, 0], mrg[:, 1], gate[:, 2], ALU.add).then_inc(m_raw, 1)
                dve.wait_ge(m_hi_s, n + 1)
                nc.vector.tensor_tensor(chunk(m_lo, n), mrg[:, 0], chunk(m_hi, n).bitcast(F32),
                                        ALU.subtract).then_inc(m_lo_s, 1)

        block = ctx.enter_context(nc.Block())

        @block.sync
        def _(sp):
            def load(s, t, t_int):
                if t_int:
                    sp.wait_ge(lo_ready, RING * t + s - RING + 1)
                src = stream[RING * t + s] if isinstance(t, int) else \
                    stream[bass.ds(RING * t + s, 1)].rearrange("a p n -> (a p) n")
                sp.dma_start(raw[:, s], src).then_inc(raw_in[s], 16)
            load(0, 0, 0)
            for n in range(4):
                sp.dma_start(h[:, 2 * n:2 * n + 2], x_in[:, 2 * n:2 * n + 2]).then_inc(in_x[n], 16)
            for s in range(1, RING):
                load(s, 0, 0)
            with sp.Fori(1, STRIPS // RING) as t:
                for s in range(RING):
                    load(s, t, 1)

        @block.gpsimd
        def _(pool):
            for dst, value in ((ones_full, 1.0), (mean_d, 1.0 / D), (mean_w, 1.0 / W5), (mean_p, 1.0 / P)):
                nc.gpsimd.memset(dst[:], value).then_inc(const_set, 1)
            for n, value in enumerate((LN_EPS / ALPHA ** 2, LN_EPS, EPS, 0.0)):
                nc.gpsimd.memset(eps_c[:, n:n + 1], value).then_inc(const_set, 1)
            pool.wait_ge(hid_l, KF)
            pool_residual_sum(pool, LN1)
            pool.wait_ge(in_cols, 16)
            pool_shift(pool, LN1)
            pool_mix(pool)
            pool.wait_ge(mix_lo, HH)
            pool.wait_ge(mix_lo_pool, HH)
            pool.dma_start(side[:], mem_in).then_inc(in_mem, 16)
            pool_sum(pool, MEMN, lambda c: pool.wait_ge(in_mem, 16) if c == 0 else None)
            pool_residual_sum(pool, LN2, beside=lambda: pool_squares(pool, MEMN))
            pool_shift(pool, LN2)
            pool.wait_ge(n_lo, MEMN.h0 + KD)
            pool.dma_start(side[:], ctx_in).then_inc(in_ctx, 16)
            pool_squares(pool, CTXN)
            pool_residual_sum(pool, LN3)
            pool_shift(pool, LN3)
            pool.wait_ge(hid_l, 2 * KF)
            pool_residual_sum(pool, LN4)
            pool_shift(pool, LN4)
            pool.wait_ge(n_lo, MODN.h0 + KD)
            nc.gpsimd.memset(cv[:], 0.0).then_inc(b_edge, 1)
            nc.gpsimd.memset(glu[:], 0.0).then_inc(b_edge, 1)
            pool.dma_start(band[:].rearrange("p k t -> p (k t)"), band_in).then_inc(in_band, 16)
            pool.wait_ge(in_band, 16)
            pool.wait_ge(ck_ready, 1)
            for t in range(MB):
                g = Nth(G_CTXV + t)
                pool.wait_ge(proj_read[g.slot], g.turn + 1)
            pool_na(pool, 0, True)
            with pool.Fori(1, KW) as i:
                pool_na(pool, i, False)
            pool_sum(pool, CONFN, lambda c: pool.wait_ge(na_conv, c + 1))

        @block.scalar
        def _(act):
            chain = Chain(act, act_step)
            act.dma_start(cols[:], cols_in).then_inc(in_cols, 16)
            act.dma_start(consts[:].rearrange("p a t -> p (a t)"), const_in).then_inc(in_const, 16)
            nc.scalar.preload_act_table_set(LN_EXP)
            act.wait_ge(const_set, 8)
            split_hi(act, Nth(0))
            for c in range(KD):
                act.wait_ge(in_x[c // 2], 16)
                nc.scalar.activation(a_hi[:, c], h[:, c], ACT.Copy).then_inc(x_hi, 1)
            split_hi(act, Nth(1))
            split_hi(act, Nth(2))
            act.wait_ge(lb_max, 2)
            nc.scalar.activation(lbv[:, 1:3], lbv[:, 1:3], ACT.Exp).then_inc(lb_exp, 1)
            act.wait_ge(in_cols, 16)
            chain.link(nc.scalar.activation(cond_s[:].rearrange("p k t -> p (k t)"), col("cond", 0, 2 * KD), ACT.Silu))
            nc.scalar.activation(cond4[:, :, 0:2], cond_s[:], ACT.Copy).then_inc(cond_silu, 1)
            act_ffn(act, S_FFN1, G_FFN1)
            act_splits(act, S_DOWN1, DOWN_STRIPS * KD)
            act_squares(act, LN1)
            act_std(act, LN1, chain)
            act_hi(act, LN1)
            act_mix(act, chain)
            for n in range(KD):
                act_only_splits(act, S_WOUT, 4 * n + 1, 4 * n + 5)
                if n == 2:
                    act_squares(act, MEMN, hi=4)
                if n == 3:
                    act_squares(act, MEMN, lo=4)
                if n == 4:
                    act_std(act, MEMN, chain)
                if 4 <= n < 8:
                    act_hi(act, MEMN, *MEM_HI_PARTS[n - 4])
            act_squares(act, LN2)
            act_memkv(act, 0, 3)
            act_std(act, LN2, chain)
            act_memkv(act, 3, 6)
            for n in range(KD):
                act_hi(act, LN2, n, n + 1)
                act_memkv(act, 6 + n, 7 + n)
            act_memkv(act, 14, 16)
            for n in range(KD):
                st, g = Nth(S_XQ + n), Nth(G_XQ + n)
                split_hi(act, st.plus(3))
                nc.scalar.activation(xq[:, n], result(act, st, g), ACT.Copy,
                                     scale=float(2 * P) ** -0.5).then_inc(proj_read[g.slot], 1)
                if n == 1:
                    act_squares(act, CTXN, ready=lambda c: act.wait_ge(in_ctx, 16), hi=4)
                if n == 2:
                    act_squares(act, CTXN, ready=lambda c: act.wait_ge(in_ctx, 16), lo=4)
                if n == 4:
                    act_std(act, CTXN, chain)
                if 4 <= n < 8:
                    act_hi(act, CTXN, *MEM_HI_PARTS[n - 4])
            act_attention(act)
            act_ctxk_norm(act, chain)
            act_only_splits(act, S_XO, 0, KD)
            act_squares(act, LN3)
            act_only_splits(act, S_CTXV, 0, 2)
            act_std(act, LN3, chain)
            act_only_splits(act, S_CTXV, 2, 4)
            act_ctxv_take(act)
            act_hi(act, LN3)
            act_ffn(act, S_FFN2, G_FFN2)
            act_splits(act, S_DOWN2, DOWN_STRIPS * KD)
            act_squares(act, LN4)
            act_std(act, LN4, chain)
            act_squares(act, MODN, ready=lambda c: act.wait_ge(n_xn, LN4.c0 + c + 1), shift=LN4.shift)
            act_std(act, MODN, chain)
            act_hi(act, MODN)
            act_na(act, 0, True, chain)
            with act.Fori(1, KW) as i:
                chain.enter(2, i - 1)
                act_na(act, i, False, chain)
                chain.leave(KW - 1)

            def split_y(b):
                for k in range(KW):
                    if b == 2:
                        act.wait_ge(y_c, k + 1)
                    else:
                        act.wait_ge((na_ya, na_yb)[b], KW)
                    nc.scalar.activation(y_hi[:, KW * b + k], y[:, b, k], ACT.Copy).then_inc(y_hi_s, 1)

            def conf_silu():
                act_std(act, CONFN, chain)
                for c in range(KW):
                    act.wait_ge(n_xn, CONFN.c0 + c + 1)
                    nc.scalar.activation(y[:, 2, c], y[:, 2, c], ACT.Silu,
                                         bias=CONFN.shift(c)).then_inc(y_silu, 1)

            nc.scalar.activation(zc[:], zc[:], ACT.Silu).then_inc(y_silu, 1)
            act_squares(act, CONFN)
            act.wait_ge(u_pv, UN * KW)
            act.wait_ge(na_conv, KW)
            act_merge(act, 0, True, [lambda: (split_y(0), conf_silu()), lambda: (split_y(1), split_y(2)),
                                     lambda: None])
            with act.Fori(1, KD // RING) as i:
                act_merge(act, i, False)
            for n in range(KD):
                split_hi(act, Nth(S_WO + n + 3))
                g = Nth(G_WO + n)
                act.wait_ge(proj_read[g.slot], g.turn + 1)
                act.dma_start(out[n], h[:, n]).then_inc(out_done, 16)
            act.wait_ge(out_done, 16 * KD)

        @block.vector
        def _(dve):
            chain = Chain(dve, dve_step)
            link = chain.link
            dve.wait_ge(in_cols, 16)
            a, b = col("lb", 0, HH), col("lb", HH, HH)
            link(nc.vector.tensor_tensor(lbv[:, 0], a, b, ALU.max))
            nc.vector.tensor_tensor(lbv[:, 1], a, lbv[:, 0], ALU.subtract).then_inc(lb_max, 1)
            nc.vector.tensor_tensor(lbv[:, 2], b, lbv[:, 0], ALU.subtract).then_inc(lb_max, 1)
            link(nc.vector.tensor_scalar(qg8[:], col("qn_g"), float(HD) ** -0.5, None, ALU.mult))
            split_lo(dve, Nth(0))
            for c in range(KD):
                dve.wait_ge(x_hi, c + 1)
                nc.vector.tensor_tensor(a_lo[:, c], h[:, c], a_hi[:, c].bitcast(F32), ALU.subtract).then_inc(x_lo, 1)
            split_lo(dve, Nth(1))
            split_lo(dve, Nth(2))
            dve.wait_ge(lb_exp, 1)
            link(nc.vector.tensor_tensor(lbv[:, 3], lbv[:, 1], lbv[:, 2], ALU.add))
            link(nc.vector.reciprocal(lbv[:, 6], lbv[:, 3]))
            link(nc.vector.tensor_tensor(lbv[:, 4], lbv[:, 1], lbv[:, 6], ALU.mult))
            link(nc.vector.tensor_scalar(lbv[:, 5], lbv[:, 4], -1.0, 1.0, ALU.mult, ALU.add))
            dve.wait_ge(cond_silu, 1)
            nc.vector.tensor_tensor(cond4[:, :, 2:4], cond_s[:], cond4[:, :, 0:2].bitcast(F32), ALU.subtract)\
                .then_inc(cond_split, 1)
            dve.wait_ge(in_const, 16)
            link(nc.vector.tensor_tensor(pair_sum[:], ident[:, 0:2], ident[:, 2:4], ALU.add))
            dve_ffn(dve, S_FFN1, G_FFN1, 0)
            dve_residual(dve, S_DOWN1, G_DOWN1, 0.5 / ALPHA, DOWN_STRIPS)
            dve_centre(dve, LN1)
            dve_normalise(dve, LN1)
            dve_mix(dve, chain)
            dve.wait_ge(n_raw, LN1.r0 + KD)
            for n in range(KD):
                dve_ada(dve, n)
                st, g = wout_at(n)
                split_lo(dve, st.plus(3))
                nc.vector.scalar_tensor_tensor(h[:, n], result(dve, st, g), 1.0 / ALPHA, h[:, n], ALU.mult,
                                               ALU.add).then_inc(proj_read[g.slot], 1)
                split_lo(dve, st.plus(4))
                if n % 4:
                    dve_ada_take(dve, n - 1 - n // 4)
                if n == 1:
                    dve_centre(dve, MEMN)
                if 4 <= n < 8:
                    dve_normalise(dve, MEMN, *MEM_PARTS[n - 4])
            dve_centre(dve, LN2)
            dve_only_splits(dve, S_MEMK, 1, 3)
            dve_only_splits(dve, S_MEMK, 3, 6)
            for n in range(KD):
                dve_normalise(dve, LN2, n, n + 1 + n // (KD - 1))
                dve_only_splits(dve, S_MEMK, 6 + n, 7 + n)
            for which in range(2):
                nc.vector.scalar_tensor_tensor(mod_a[:, which], modv[:, KD:2 * KD, which], 1.0, col("norm_g", 0, KD),
                                               ALU.add, ALU.mult).then_inc(mod_ready, 1)
            dve_only_splits(dve, S_MEMK, 14, 16)
            for n in range(KD):
                split_lo(dve, Nth(S_XQ + n + 3))
                if n == 4:
                    dve.wait_ge(mod_ready, 2)
                if 4 <= n < 8:
                    dve_normalise(dve, CTXN, *MEM_PARTS[n - 4])
            dve_attention(dve, chain)
            dve_ctxk_norm(dve)
            dve_residual(dve, S_XO, G_XO, 1.0 / ALPHA, before=LN2)
            dve_centre(dve, LN3)
            dve_only_splits(dve, S_CTXV, 0, 2)
            dve_only_splits(dve, S_CTXV, 2, 4)
            dve_normalise(dve, LN3)
            dve_ffn(dve, S_FFN2, G_FFN2, KF)
            dve_residual(dve, S_DOWN2, G_DOWN2, 0.5 / ALPHA, DOWN_STRIPS, before=LN3)
            dve_centre(dve, LN4)
            dve_normalise(dve, LN4)
            dve_normalise(dve, MODN, before=LN4)
            dve_na(dve, 0, True, chain)
            with dve.Fori(1, KW) as i:
                chain.enter(NA_LINKS, i - 1)
                dve_na(dve, i, False, chain)
                chain.leave(KW - 1)

            def split_y(b):
                for k in range(KW):
                    dve.wait_ge(y_hi_s, KW * b + k + 1)
                    nc.vector.tensor_tensor(y_lo[:, KW * b + k], y[:, b, k], y_hi[:, KW * b + k].bitcast(F32),
                                            ALU.subtract).then_inc(y_lo_s, 1)

            def conf_end():
                dve_normalise(dve, CONFN)
                for c in range(KW):
                    dve.wait_ge(y_silu, c + 2)
                    nc.vector.tensor_tensor(y[:, 2, c], y[:, 2, c], zc[:, c], ALU.mult).then_inc(y_c, 1)

            dve_centre(dve, CONFN)
            dve_merge(dve, 0, True, chain, [lambda: (split_y(0), conf_end()), lambda: (split_y(1), split_y(2)),
                                            lambda: None])
            with dve.Fori(1, KD // RING) as i:
                chain.enter(RING, i - 1)
                dve_merge(dve, i, False, chain)
                chain.leave(KD // RING - 1)
            for n in range(KD):
                st, g = Nth(S_WO + n), Nth(G_WO + n)
                split_lo(dve, st.plus(3))
                nc.vector.scalar_tensor_tensor(h[:, n], result(dve, st, g), modv[:, 2 * KD + n, 0:1], h[:, n],
                                               ALU.mult, ALU.add).then_inc(proj_read[g.slot], 1)

        @block.tensor
        def _(pe):
            pe.wait_ge(const_set, 8)
            pe_ffn(pe, S_FFN1, G_FFN1, lambda k: pe.wait_ge(x_lo, k + 1))
            pe_down(pe, S_DOWN1, G_DOWN1, 0)
            pe_mean(pe, LN1)
            pe_stats(pe, LN1)
            pe.wait_ge(in_const, 16)
            pe_mix(pe)
            for n in range(KD):
                ready = (lambda k: pe.wait_ge(mix_lo, k - HH + 1) if k >= HH else pe.wait_ge(mix_lo_pool, k + 1)) \
                    if n == 0 else None
                pe_ada(pe, n)
                if n == 4:
                    pe_stats(pe, MEMN)
                st, g = wout_at(n)
                feature_strip(pe, st, g, mix_h, mix_l, order=MIX_ORDER, ready=ready)
                if n % 4:
                    pe_ada_turn(pe, n - 1 - n // 4)
                if n == 1:
                    pe_mean(pe, MEMN)
            pe_mean(pe, LN2)
            pe_memkv(pe, 0, 3)
            pe_stats(pe, LN2)
            pe_memkv(pe, 3, 6)
            pe_memkv(pe, 6, 16)
            for n in range(KD):
                feature_strip(pe, Nth(S_XQ + n), Nth(G_XQ + n), a_hi, a_lo,
                              ready=lo_ready_of(pe, LN2) if n == 0 else None)
                if n == 3:
                    pe_stats(pe, CTXN)
            pe_attention(pe)
            pe_ctxk_norm(pe)
            for u in range(UNITS - RING, UNITS):
                g = Nth(G_PV + u)
                pe.wait_ge(proj_read[g.slot], g.turn + 1)
            with pe.Fori(0, KD // RING) as i:
                for q in range(RING):
                    feature_strip(pe, Nth(S_XO + q, RING, i), Nth(G_XO + q, RING, i), a_hi, a_lo)
            pe_mean(pe, LN3)
            pe_ctxv(pe, 0, 2)
            pe_stats(pe, LN3)
            pe_ctxv(pe, 2, 4)
            pe_ffn(pe, S_FFN2, G_FFN2, lo_ready_of(pe, LN3), pair=True)
            pe_down(pe, S_DOWN2, G_DOWN2, KF)
            pe_mean(pe, LN4)
            pe_stats(pe, LN4)
            pe_stats(pe, MODN)
            pe_na(pe, 0, True)
            with pe.Fori(1, KW) as i:
                pe_na(pe, i, False)
            pe_mean(pe, CONFN)
            pe_merge(pe, 0, True, [lambda: pe_stats(pe, CONFN), lambda: None, lambda: None])
            with pe.Fori(1, KD // RING) as i:
                pe_merge(pe, i, False)
            for n in range(KD):
                feature_strip(pe, Nth(S_WO + n), Nth(G_WO + n), m_hi, m_lo,
                              ready=(lambda k: pe.wait_ge(m_lo_s, k + 1)) if n == 0 else None)


def feature_major(w):
    k, n = w.shape
    return w.reshape(k // P, P, n // P, P).transpose(2, 1, 0, 3).reshape(n // P, P, k)


def token_major(w):
    return w.reshape(4, 2, P, W5).transpose(0, 2, 1, 3).reshape(4, P, 2 * W5)


def down_strips(w):
    blocks = feature_major(w)
    return np.pad(blocks, ((0, 0), (0, 0), (0, DOWN_STRIPS * SB * P - F_FF))).reshape(
        KD, P, DOWN_STRIPS, SB * P).transpose(0, 2, 1, 3).reshape(KD * DOWN_STRIPS, P, SB * P)


def vector_cols(v):
    return v.reshape(-1, P).T


def weight_stream(i):
    def ffn(tag):
        gate, up = feature_major(i[tag + "_w_gate"][0]), feature_major(i[tag + "_w_up"][0])
        return [np.stack([gate, up], 1).reshape(2 * KF, P, SB * P), down_strips(i[tag + "_w_down"][0])]

    w_ada = i["w_ada_2"][0]
    ada = np.concatenate([token_major(w_ada[:, n * W5:(n + 1) * W5]) for n in range(6)], 0)
    w_in = i["w_in"][0]
    q, fz, iv, g, u, v = (w_in[:, n * W5:(n + 1) * W5] for n in range(6))
    parts = ffn("ffn1")
    parts += [feature_major(fz), feature_major(q), token_major(iv), token_major(v), feature_major(u),
              feature_major(g)]
    w_out = feature_major(i["w_out"][0])
    parts += [np.concatenate([ada.reshape(KD, 3, P, SB * P), w_out[:, None]], 1).reshape(4 * KD, P, SB * P)]
    w_v = i["xa_w_v"][0]
    w2 = i["w_in_2"][0]
    part = [w2[:, n * W5:(n + 1) * W5] for n in range(11)]
    parts += [feature_major(i["xa_w_k"][0]), token_major(w_v[:, :W5]), token_major(w_v[:, W5:]),
              feature_major(i["xa_w_q"][0]), feature_major(part[1]), feature_major(i["xa_w_o"][0]),
              token_major(part[2])]
    parts += ffn("ffn2")
    na = [feature_major(part[n]) for n in (8, 9, 1, 0, 2)]
    z = feature_major(part[10])
    zero = np.zeros_like(z[:, :, :4 * P])
    na += [np.concatenate([z[:, :, :4 * P], zero], 2), np.concatenate([z[:, :, 4 * P:], zero], 2)]
    na += [feature_major(part[n]) for n in (3, 4, 5, 6, 7)]
    parts += [np.stack(na, 1).reshape(KW * NA_STRIPS, P, SB * P)]
    gates = [feature_major(w2[:, 11 * W5 + n * D:11 * W5 + (n + 1) * D]) for n in range(3)]
    oa, ob, oc = (feature_major(i["w_out_" + n + "_2"][0]) for n in "abc")
    parts += [np.stack(gates + [np.concatenate([oa, ob], 2), np.concatenate([oc, np.zeros_like(oc)], 2)],
                       1).reshape(KD * MERGE_STRIPS, P, SB * P)]
    parts += [feature_major(i["w_o_2"][0])]
    whole = np.concatenate(parts, 0)
    assert whole.shape == (STRIPS, P, SB * P), whole.shape
    return whole


def column_table(i):
    named = {n: vector_cols(i[n]) for n in ("ln1_g", "ln1_b", "ln2_g", "ln2_b", "ln3_g", "ln3_b", "ln4_g", "ln4_b")}
    named["mem_g"], named["mem_b"] = vector_cols(i["mem_ln_g"]), vector_cols(i["mem_ln_b"])
    named["norm_g"] = vector_cols(i["norm_g_2"])
    named["lb"] = i["hg_lb_logits"].reshape(2 * HH, P).T
    named["hg_g"] = vector_cols(i["hg_norm_g"])
    named["b_ada"] = vector_cols(i["b_ada_2"])
    named["cond"] = np.stack([vector_cols(i["c_2"]), vector_cols(i["c_ctx_2"])], 2).reshape(P, 2 * KD)
    named["qn_g"] = np.tile(i["q_norm_g_2"].reshape(HD, 1), (2, 1))
    named["kn_g"] = np.tile(i["k_norm_g_2"].reshape(HD, 1), (2, 1))
    named["short_w"] = i["conv_short_w_2"][0].reshape(3, KW, P).transpose(2, 1, 0).reshape(P, 3 * KW)
    named["conf_w"] = i["conv_conf_w_2"][0].reshape(TAPS, KW, P).transpose(2, 1, 0).reshape(P, TAPS * KW)
    named["conf_b"] = vector_cols(i["conv_conf_b_2"])
    named["lnc_g"], named["lnc_b"] = vector_cols(i["ln_conf_g_2"]), vector_cols(i["ln_conf_b_2"])
    assert all(named[n].shape[1] == COLS[n][1] for n in COLS)
    return np.concatenate([named[n] for n in COLS], 1)


def shape_constants():
    p = np.arange(P)
    consts = np.concatenate([np.eye(P), (p[:, None] // HD == p // HD) / HD], 1).astype(np.float32)
    masks = []
    for lev in range(LEVELS):
        n = 1 << lev
        t = np.concatenate([np.arange(n) + 2 * n * b + n for b in range(P // (2 * n))])
        masks.append((p[:, None] // (2 * n) == t // (2 * n)) & (p[:, None] % (2 * n) < n))
    masks = np.concatenate(masks + [np.eye(P, dtype=bool)], 1).astype(np.int32)
    band = np.zeros((P, 3, ROWS, BAND), np.float32)
    for kind, cb in enumerate((0, 1, 3)):
        qcol = cb * QC + p % QC
        start = np.clip(qcol - 8, 0, GRID - 16)
        rel = BAND_AT[cb] + np.arange(BAND)[None] - start[:, None]
        band[:, kind] = np.where((rel >= 0) & (rel < 16), 0.0, -1e30)[:, None]
    return consts, masks, band.reshape(P, -1)


def bias_windows(rpb):
    pad = np.pad(rpb, ((0, 0), (0, 0), (BAND, BAND)))
    r, q = np.arange(P) // QC, np.arange(P) % QC
    rows = (ROWS - 1 - r)[:, None] + np.arange(ROWS)
    colsx = np.arange(RPB_W)[None] - BIAS_AT + (15 + BAND) - q[:, None]
    return pad[:, rows[:, :, None], colsx[:, None, :]].transpose(1, 0, 2, 3).reshape(P, NH, ROWS * RPB_W)


def token_chunks(a):
    return a.T.reshape(KD, P, -1).transpose(1, 0, 2)


def kernel(**inputs):
    import concourse.bacc as bacc
    from concourse.bass_utils import run_bass_kernel_spmd

    i = {n: np.asarray(a) for n, a in inputs.items()}
    consts, masks, band = shape_constants()
    rows = np.concatenate([i["sg_ln_g"].reshape(-1), i["sg_ln_b"].reshape(-1), i["sg_b_s"].reshape(-1)])
    arrays = {
        "stream": weight_stream(i), "x_in": token_chunks(i["x"][0]), "mem_in": token_chunks(i["mem"][0]),
        "ctx_in": token_chunks(i["ctx_2"][0]), "cols_in": column_table(i), "const_in": consts, "mask_in": masks,
        "rows_in": rows, "wst_in": i["sg_w_s"][0].transpose(2, 0, 1).reshape(P, HH * P), "band_in": band,
        "rpb_in": bias_windows(i["rpb_2"][0]),
    }
    nc = bacc.Bacc("TRN2", target_bir_lowering=False, num_devices=1)
    aps = []
    for name in arrays:
        a = arrays[name] = np.ascontiguousarray(arrays[name])
        aps.append(nc.dram_tensor(name, a.shape, mybir.dt.from_np(a.dtype), kind="ExternalInput").ap())
    out = nc.dram_tensor("out", (KD, P, T), F32, kind="ExternalOutput").ap()
    hybrid_blocks(nc, *aps, out)
    r = run_bass_kernel_spmd(nc, [arrays], core_ids=[0])
    return r.results[0]["out"].reshape(D, T).T.reshape(1, T, D)
```
